# Optimizing a Trainium2 kernel written in Bass

```python
import math
import jax, jax.numpy as jnp
from jax import lax
import numpy as np

D_MODEL = 1024
BATCH = 1
SEQ = 256
DEPTH = 4

N_MIXERS = 3
N_SUBLAYERS = 3
N_MOD = 3
Q_BLOCK = 128
LN_EPS = 1e-5
RMS_EPS = 1e-6
DEEPNORM_ALPHA = (2.0 * DEPTH) ** 0.25
DEEPNORM_BETA = (8.0 * DEPTH) ** -0.25
FFN_HIDDEN = ((8 * D_MODEL // 3 + 255) // 256) * 256
FFN_RES_WEIGHT = 0.5

MLA_HEADS = D_MODEL // 128
MLA_Q_RANK = 3 * D_MODEL // 8
MLA_KV_RANK = D_MODEL // 4
MLA_NOPE_DIM = 128
MLA_ROPE_DIM = 64
MLA_V_DIM = 128
ROPE_THETA = 10000.0

DIFF_HEAD_DIM = 64
DIFF_HEADS = D_MODEL // (2 * DIFF_HEAD_DIM)
LAMBDA_STD = 0.1

SSM_INNER = 2 * D_MODEL
SSM_HEAD_DIM = 64
SSM_HEADS = SSM_INNER // SSM_HEAD_DIM
SSM_STATE = 128
SSM_GROUPS = 4
SSM_CONV = 4
SSM_CHUNK = 128
SSM_CONV_DIM = SSM_INNER + 2 * SSM_GROUPS * SSM_STATE

N_MLA_LAYERS = (DEPTH + 2) // 3
N_DIFF_LAYERS = (DEPTH + 1) // 3
N_SSM_LAYERS = DEPTH // 3


def _layernorm(x, g, b):
    xf = x.astype(jnp.float32)
    mu = jnp.mean(xf, axis=-1, keepdims=True)
    var = jnp.mean(jnp.square(xf - mu), axis=-1, keepdims=True)
    return ((xf - mu) * lax.rsqrt(var + LN_EPS) * g + b).astype(x.dtype)

def _rmsnorm(x, g):
    xf = x.astype(jnp.float32)
    return (xf * lax.rsqrt(jnp.mean(xf * xf, axis=-1, keepdims=True) + RMS_EPS) * g).astype(x.dtype)

def _swiglu(h, w_in, w_out):
    gate, up = jnp.split(h @ w_in, 2, axis=-1)
    return (jax.nn.silu(gate) * up) @ w_out

def _sublayer(x, fn, mod_j, g, b, weight):
    shift, scale, gate = mod_j[:, 0, None, :], mod_j[:, 1, None, :], mod_j[:, 2, None, :]
    y = fn(x * (1 + scale) + shift)
    return _layernorm(DEEPNORM_ALPHA * x + weight * gate * y, g, b)

def _causal_blocks(q, k, v, attend):
    seq = q.shape[1]
    outs = []
    for start in range(0, seq, Q_BLOCK):
        end = start + Q_BLOCK
        mask = jnp.arange(end)[None, :] <= jnp.arange(start, end)[:, None]
        outs.append(attend(q[:, start:end], k[:, :end], v[:, :end], mask))
    return jnp.concatenate(outs, axis=1)

def _rope(x, cos, sin):
    xf = x.astype(jnp.float32)
    x1, x2 = jnp.split(xf, 2, axis=-1)
    return jnp.concatenate([x1 * cos - x2 * sin, x1 * sin + x2 * cos], axis=-1).astype(x.dtype)

def _mla(h, positions, w_in, q_norm_g, kv_norm_g, w_q_up, w_kv_up, w_out):
    b, s, _ = h.shape
    cq, ckv, k_rope = jnp.split(h @ w_in, [MLA_Q_RANK, MLA_Q_RANK + MLA_KV_RANK], axis=-1)
    q = (_rmsnorm(cq, q_norm_g) @ w_q_up).reshape(b, s, MLA_HEADS, MLA_NOPE_DIM + MLA_ROPE_DIM)
    kv = (_rmsnorm(ckv, kv_norm_g) @ w_kv_up).reshape(b, s, MLA_HEADS, MLA_NOPE_DIM + MLA_V_DIM)
    q_nope, q_rope = q[..., :MLA_NOPE_DIM], q[..., MLA_NOPE_DIM:]
    k_nope, v = kv[..., :MLA_NOPE_DIM], kv[..., MLA_NOPE_DIM:]
    inv_freq = ROPE_THETA ** (-jnp.arange(0, MLA_ROPE_DIM, 2, dtype=jnp.float32) / MLA_ROPE_DIM)
    ang = positions.astype(jnp.float32)[..., None] * inv_freq
    cos, sin = jnp.cos(ang)[:, :, None, :], jnp.sin(ang)[:, :, None, :]
    q_rope = _rope(q_rope, cos, sin)
    k_rope = _rope(k_rope[:, :, None, :], cos, sin)
    q = jnp.concatenate([q_nope, q_rope], axis=-1)
    k = jnp.concatenate([k_nope, jnp.broadcast_to(k_rope, (b, s, MLA_HEADS, MLA_ROPE_DIM))], axis=-1)
    scale = (MLA_NOPE_DIM + MLA_ROPE_DIM) ** -0.5

    def attend(qb, kb, vb, mask):
        sc = jnp.einsum('bqhd,bkhd->bhqk', qb, kb).astype(jnp.float32) * scale
        p = jax.nn.softmax(jnp.where(mask, sc, -jnp.inf), axis=-1).astype(vb.dtype)
        return jnp.einsum('bhqk,bkhv->bqhv', p, vb)

    o = _causal_blocks(q, k, v, attend)
    return o.reshape(b, s, MLA_HEADS * MLA_V_DIM) @ w_out

def _diff_attn(h, layer, w_in, lambda_q, lambda_k, subln_g, w_out):
    b, s, _ = h.shape
    lam_init = 0.8 - 0.6 * math.exp(-0.3 * layer)
    q, k, v = jnp.split(h @ w_in, 3, axis=-1)
    q = q.reshape(b, s, DIFF_HEADS, 2, DIFF_HEAD_DIM)
    k = k.reshape(b, s, DIFF_HEADS, 2, DIFF_HEAD_DIM)
    v = v.reshape(b, s, DIFF_HEADS, 2 * DIFF_HEAD_DIM)
    lq, lk = lambda_q.astype(jnp.float32), lambda_k.astype(jnp.float32)
    lam = jnp.exp(jnp.sum(lq[0] * lk[0])) - jnp.exp(jnp.sum(lq[1] * lk[1])) + lam_init
    scale = DIFF_HEAD_DIM ** -0.5

    def attend(qb, kb, vb, mask):
        sc = jnp.einsum('bqhid,bkhid->bhiqk', qb, kb).astype(jnp.float32) * scale
        p = jax.nn.softmax(jnp.where(mask, sc, -jnp.inf), axis=-1)
        a = (p[:, :, 0] - lam * p[:, :, 1]).astype(vb.dtype)
        return jnp.einsum('bhqk,bkhe->bqhe', a, vb)

    o = _causal_blocks(q, k, v, attend)
    o = _rmsnorm(o, subln_g) * (1.0 - lam_init)
    return o.reshape(b, s, D_MODEL) @ w_out

def _ssd_scan(x, dt, a, bmat, cmat):
    b, s, nh, p = x.shape
    g, n = bmat.shape[2], bmat.shape[3]
    hg = nh // g
    nc, L = s // SSM_CHUNK, SSM_CHUNK

    def chunks(t):
        return jnp.moveaxis(t.reshape(b, nc, L, *t.shape[2:]), 1, 0)

    xs = chunks(x.reshape(b, s, g, hg, p))
    dts = chunks(dt.reshape(b, s, g, hg))
    bs, cs = chunks(bmat), chunks(cmat)
    causal = jnp.tril(jnp.ones((L, L), dtype=bool))[None, :, :, None, None]
    a_g = a.reshape(g, hg)

    def step(state, inp):
        xc, dtc, bc, cc = inp
        acum = jnp.cumsum(dtc * a_g, axis=1)
        seg = acum[:, :, None] - acum[:, None, :]
        decay = jnp.exp(jnp.where(causal, seg, -jnp.inf))
        cb = jnp.einsum('blgn,bsgn->blsg', cc, bc)
        y = jnp.einsum('blsg,blsgh,bsghp->blghp', cb, decay, xc * dtc[..., None])
        y = y + jnp.einsum('blgn,bghpn->blghp', cc, state) * jnp.exp(acum)[..., None]
        last = acum[:, -1]
        w = jnp.exp(last[:, None] - acum) * dtc
        state = state * jnp.exp(last)[..., None, None] + jnp.einsum('bsgn,bsgh,bsghp->bghpn', bc, w, xc)
        return state, y

    state0 = jnp.zeros((b, g, hg, p, n), jnp.float32)
    _, ys = lax.scan(step, state0, (xs, dts, bs, cs))
    return jnp.moveaxis(ys, 0, 1).reshape(b, s, nh, p)

def _mamba2(h, w_in, conv_w, conv_b, dt_bias, a_log, d_skip, norm_g, w_out):
    b, s, _ = h.shape
    z, xbc, dt = jnp.split(h @ w_in, [SSM_INNER, SSM_INNER + SSM_CONV_DIM], axis=-1)
    xbc = lax.conv_general_dilated(
        xbc, conv_w[:, None, :], window_strides=(1,), padding=((SSM_CONV - 1, 0),),
        dimension_numbers=('NWC', 'WIO', 'NWC'), feature_group_count=SSM_CONV_DIM) + conv_b
    xbc = jax.nn.silu(xbc)
    xs, bmat, cmat = jnp.split(xbc, [SSM_INNER, SSM_INNER + SSM_GROUPS * SSM_STATE], axis=-1)
    dt = jax.nn.softplus(dt.astype(jnp.float32) + dt_bias.astype(jnp.float32))
    a = -jnp.exp(a_log.astype(jnp.float32))
    xh = xs.reshape(b, s, SSM_HEADS, SSM_HEAD_DIM).astype(jnp.float32)
    y = _ssd_scan(xh, dt, a,
                  bmat.reshape(b, s, SSM_GROUPS, SSM_STATE).astype(jnp.float32),
                  cmat.reshape(b, s, SSM_GROUPS, SSM_STATE).astype(jnp.float32))
    y = y + d_skip.astype(jnp.float32)[:, None] * xh
    y = y.reshape(b, s, SSM_INNER).astype(h.dtype) * jax.nn.silu(z)
    gs = SSM_INNER // SSM_GROUPS
    y = _rmsnorm(y.reshape(b, s, SSM_GROUPS, gs), norm_g.reshape(SSM_GROUPS, gs)).reshape(b, s, SSM_INNER)
    return y @ w_out

def first_inputs(seed: int = 0) -> dict:
    key = jax.random.key(seed)
    ks = iter(jax.random.split(key, 32))

    def nrm(shape, scale):
        return jax.random.normal(next(ks), shape, jnp.float32) * scale

    D, F = D_MODEL, FFN_HIDDEN
    x = nrm((BATCH, SEQ, D), 1.0)
    c = nrm((BATCH, D), 1.0)
    offsets = jax.random.randint(next(ks), (BATCH, 1), 0, 4096, dtype=jnp.int32)
    positions = offsets + jnp.arange(SEQ, dtype=jnp.int32)[None, :]
    w_mod = nrm((DEPTH, D, N_SUBLAYERS * N_MOD * D), 0.5 * D ** -0.5)
    b_mod = nrm((DEPTH, N_SUBLAYERS * N_MOD * D), 0.02)
    ln_g = 1.0 + nrm((DEPTH, N_SUBLAYERS, D), 0.02)
    ln_b = nrm((DEPTH, N_SUBLAYERS, D), 0.02)
    ffn_w_in = nrm((DEPTH, 2, D, 2 * F), D ** -0.5)
    ffn_w_out = nrm((DEPTH, 2, F, D), F ** -0.5 * DEEPNORM_BETA)

    na = N_MLA_LAYERS
    mla_w_in = nrm((na, D, MLA_Q_RANK + MLA_KV_RANK + MLA_ROPE_DIM), D ** -0.5)
    mla_q_norm_g = 1.0 + nrm((na, MLA_Q_RANK), 0.02)
    mla_kv_norm_g = 1.0 + nrm((na, MLA_KV_RANK), 0.02)
    mla_w_q_up = nrm((na, MLA_Q_RANK, MLA_HEADS * (MLA_NOPE_DIM + MLA_ROPE_DIM)), MLA_Q_RANK ** -0.5)
    mla_w_kv_up = nrm((na, MLA_KV_RANK, MLA_HEADS * (MLA_NOPE_DIM + MLA_V_DIM)), MLA_KV_RANK ** -0.5)
    mla_w_out = nrm((na, MLA_HEADS * MLA_V_DIM, D), (MLA_HEADS * MLA_V_DIM) ** -0.5 * DEEPNORM_BETA)

    nb = N_DIFF_LAYERS
    diff_w_in = nrm((nb, D, 3 * D), D ** -0.5)
    diff_lambda_q = nrm((nb, 2, DIFF_HEAD_DIM), LAMBDA_STD)
    diff_lambda_k = nrm((nb, 2, DIFF_HEAD_DIM), LAMBDA_STD)
    diff_subln_g = 1.0 + nrm((nb, 2 * DIFF_HEAD_DIM), 0.02)
    diff_w_out = nrm((nb, D, D), D ** -0.5 * DEEPNORM_BETA)

    nc = N_SSM_LAYERS
    ssm_w_in = nrm((nc, D, 2 * SSM_INNER + 2 * SSM_GROUPS * SSM_STATE + SSM_HEADS), D ** -0.5)
    ssm_conv_w = nrm((nc, SSM_CONV, SSM_CONV_DIM), SSM_CONV ** -0.5)
    ssm_conv_b = nrm((nc, SSM_CONV_DIM), 0.02)
    u = jax.random.uniform(next(ks), (nc, SSM_HEADS), jnp.float32)
    dt0 = jnp.exp(u * (math.log(0.1) - math.log(1e-3)) + math.log(1e-3))
    ssm_dt_bias = dt0 + jnp.log(-jnp.expm1(-dt0))
    ssm_a_log = jnp.log(jax.random.uniform(next(ks), (nc, SSM_HEADS), jnp.float32, 1.0, 16.0))
    ssm_d_skip = 1.0 + nrm((nc, SSM_HEADS), 0.02)
    ssm_norm_g = 1.0 + nrm((nc, SSM_INNER), 0.02)
    ssm_w_out = nrm((nc, SSM_INNER, D), SSM_INNER ** -0.5 * DEEPNORM_BETA)

    return {
        "x": x, "c": c, "positions": positions,
        "w_mod": w_mod, "b_mod": b_mod, "ln_g": ln_g, "ln_b": ln_b,
        "ffn_w_in": ffn_w_in, "ffn_w_out": ffn_w_out,
        "mla_w_in": mla_w_in, "mla_q_norm_g": mla_q_norm_g, "mla_kv_norm_g": mla_kv_norm_g,
        "mla_w_q_up": mla_w_q_up, "mla_w_kv_up": mla_w_kv_up, "mla_w_out": mla_w_out,
        "diff_w_in": diff_w_in, "diff_lambda_q": diff_lambda_q, "diff_lambda_k": diff_lambda_k,
        "diff_subln_g": diff_subln_g, "diff_w_out": diff_w_out,
        "ssm_w_in": ssm_w_in, "ssm_conv_w": ssm_conv_w, "ssm_conv_b": ssm_conv_b,
        "ssm_dt_bias": ssm_dt_bias, "ssm_a_log": ssm_a_log, "ssm_d_skip": ssm_d_skip,
        "ssm_norm_g": ssm_norm_g, "ssm_w_out": ssm_w_out,
    }

def first_block(x, c, positions, w_mod, b_mod, ln_g, ln_b, ffn_w_in, ffn_w_out,
              mla_w_in, mla_q_norm_g, mla_kv_norm_g, mla_w_q_up, mla_w_kv_up, mla_w_out,
              diff_w_in, diff_lambda_q, diff_lambda_k, diff_subln_g, diff_w_out,
              ssm_w_in, ssm_conv_w, ssm_conv_b, ssm_dt_bias, ssm_a_log, ssm_d_skip,
              ssm_norm_g, ssm_w_out):
    cond = jax.nn.silu(c)
    for i in range(DEPTH):
        mod = (cond @ w_mod[i] + b_mod[i]).reshape(-1, N_SUBLAYERS, N_MOD, D_MODEL)
        kind, idx = i % N_MIXERS, i // N_MIXERS

        x = _sublayer(x, lambda h: _swiglu(h, ffn_w_in[i, 0], ffn_w_out[i, 0]),
                      mod[:, 0], ln_g[i, 0], ln_b[i, 0], FFN_RES_WEIGHT)

        if kind == 0:
            mixer = lambda h: _mla(h, positions, mla_w_in[idx], mla_q_norm_g[idx], mla_kv_norm_g[idx],
                                   mla_w_q_up[idx], mla_w_kv_up[idx], mla_w_out[idx])
        elif kind == 1:
            mixer = lambda h: _diff_attn(h, i, diff_w_in[idx], diff_lambda_q[idx], diff_lambda_k[idx],
                                         diff_subln_g[idx], diff_w_out[idx])
        else:
            mixer = lambda h: _mamba2(h, ssm_w_in[idx], ssm_conv_w[idx], ssm_conv_b[idx], ssm_dt_bias[idx],
                                      ssm_a_log[idx], ssm_d_skip[idx], ssm_norm_g[idx], ssm_w_out[idx])
        x = _sublayer(x, mixer, mod[:, 1], ln_g[i, 1], ln_b[i, 1], 1.0)

        x = _sublayer(x, lambda h: _swiglu(h, ffn_w_in[i, 1], ffn_w_out[i, 1]),
                      mod[:, 2], ln_g[i, 2], ln_b[i, 2], FFN_RES_WEIGHT)
    return x


DEPTH_2 = 1

N_MEM = 256
GN_EPS = 1e-5
ATT_HEADS = 8
ATT_HEAD_DIM = 64
ATT_WIDTH = ATT_HEADS * ATT_HEAD_DIM
ROT_DIM = ATT_HEAD_DIM // 4
ROPE_THETA_2 = 500000.0
DILATED_PATTERNS = ((128, 1), (512, 4), (2048, 16))
RET_HEADS = 4
RET_HEAD_DIM = 128
RET_WIDTH = RET_HEADS * RET_HEAD_DIM
RET_CHUNK = 128
RET_ROPE_THETA = 10000.0
MIX_WIDTH = ATT_WIDTH + RET_WIDTH
IN_PROJ_WIDTH = 3 * ATT_WIDTH + 4 * RET_WIDTH
XATT_HEADS = 4
XATT_HEAD_DIM = D_MODEL // XATT_HEADS
FFN_HIDDEN_2 = -(-(8 * D_MODEL) // (3 * 256)) * 256


def rms_norm(x, g):
    xf = x.astype(jnp.float32)
    y = xf * lax.rsqrt(jnp.mean(xf * xf, axis=-1, keepdims=True) + RMS_EPS)
    return (y * g.astype(jnp.float32)).astype(x.dtype)

def rope(x, pos, rot_dim, theta):
    inv = theta ** (-(jnp.arange(0, rot_dim, 2, dtype=jnp.float32) / rot_dim))
    ang = pos.astype(jnp.float32)[:, None] * inv[None, :]
    cos, sin = jnp.cos(ang), jnp.sin(ang)
    xr = x[..., :rot_dim].astype(jnp.float32)
    x1, x2 = xr[..., : rot_dim // 2], xr[..., rot_dim // 2:]
    rot = jnp.concatenate([x1 * cos - x2 * sin, x2 * cos + x1 * sin], axis=-1)
    return jnp.concatenate([rot.astype(x.dtype), x[..., rot_dim:]], axis=-1)

def window_attn_by_stride(q, k, v, window, dilation):
    B, H, S, dh = q.shape
    n_keys = window // dilation
    L = S // dilation
    nb = -(-L // n_keys)
    Lp = nb * n_keys

    def to_classes(t):
        t = t.reshape(B, H, L, dilation, dh).transpose(0, 1, 3, 2, 4)
        return jnp.pad(t, [(0, 0)] * 3 + [(0, Lp - L), (0, 0)])

    def with_prev(t):
        cur = t.reshape(B, H, dilation, nb, n_keys, dh)
        prev = jnp.pad(cur, [(0, 0)] * 3 + [(1, 0), (0, 0), (0, 0)])[:, :, :, :nb]
        return jnp.concatenate([prev, cur], axis=-2)

    qb = to_classes(q).reshape(B, H, dilation, nb, n_keys, dh)
    kb = with_prev(to_classes(k))
    vb = with_prev(to_classes(v)).astype(jnp.float32)
    s = jnp.einsum('bhrnid,bhrnjd->bhrnij', qb, kb).astype(jnp.float32) * (dh ** -0.5)
    i = jnp.arange(n_keys)[:, None]
    j = jnp.arange(2 * n_keys)[None, :]
    band = (j >= i) & (j <= i + n_keys)
    not_before_start = (jnp.arange(nb)[:, None, None] > 0) | (j[None] >= n_keys)
    mask = band[None] & not_before_start
    s = jnp.where(mask, s, -jnp.inf)
    m = jnp.max(s, axis=-1)
    p = jnp.exp(s - m[..., None])
    l = jnp.sum(p, axis=-1)
    o = jnp.einsum('bhrnij,bhrnjd->bhrnid', p, vb) / l[..., None]

    def back(t, has_d):
        if has_d:
            t = t.reshape(B, H, dilation, Lp, dh)[:, :, :, :L]
            return t.transpose(0, 1, 3, 2, 4).reshape(B, H, S, dh)
        t = t.reshape(B, H, dilation, Lp)[:, :, :, :L]
        return t.transpose(0, 1, 3, 2).reshape(B, H, S)

    return back(o, True), back(m, False), back(l, False)

def dilated_attention(q, k, v):
    outs = [window_attn_by_stride(q, k, v, w, r) for (w, r) in DILATED_PATTERNS]
    m_all = jnp.max(jnp.stack([m for _, m, _ in outs], axis=0), axis=0)
    wts = [l * jnp.exp(m - m_all) for _, m, l in outs]
    num = sum(wt[..., None] * o for wt, (o, _, _) in zip(wts, outs))
    den = sum(wts)
    return num / den[..., None]

def retention(q, k, v):
    B, H, S, dk = q.shape
    dv = v.shape[-1]
    C = RET_CHUNK
    nc = S // C
    log_g = jnp.log(1.0 - 2.0 ** (-5.0 - jnp.arange(H, dtype=jnp.float32)))
    n = jnp.arange(C, dtype=jnp.float32)
    rel = n[:, None] - n[None, :]
    decay_mask = jnp.where(rel >= 0, jnp.exp(log_g[:, None, None] * jnp.maximum(rel, 0.0)), 0.0)
    xi = jnp.exp(log_g[:, None] * (n + 1.0))
    zeta = jnp.exp(log_g[:, None] * (C - 1.0 - n))
    chunk_decay = jnp.exp(log_g * C)

    def chunks(t):
        return t.reshape(B, H, nc, C, t.shape[-1]).transpose(2, 0, 1, 3, 4)

    def step(R, qkv):
        qc, kc, vc = qkv
        inner = jnp.einsum('bhnd,bhmd->bhnm', qc, kc) * decay_mask
        o = jnp.einsum('bhnm,bhme->bhne', inner, vc)
        o = o + jnp.einsum('bhnd,bhde->bhne', qc, R) * xi[:, :, None]
        R = R * chunk_decay[:, None, None] + jnp.einsum('bhmd,bhme->bhde', kc * zeta[:, :, None], vc)
        return R, o

    R0 = jnp.zeros((B, H, dk, dv), jnp.float32)
    _, o = lax.scan(step, R0, (chunks(q), chunks(k), chunks(v)))
    return o.transpose(1, 2, 0, 3, 4).reshape(B, H, S, dv)

def hybrid_mixer(h, w_in, attn_gn_g, ret_gn_g, w_out):
    B, S, _ = h.shape
    proj = h @ w_in
    splits = list(np.cumsum([ATT_WIDTH] * 3 + [RET_WIDTH] * 3))
    aq, ak, av, rq, rk, rv, rg = jnp.split(proj, splits, axis=-1)
    pos = jnp.arange(S)

    def heads(t, nh, d):
        return t.reshape(B, S, nh, d).transpose(0, 2, 1, 3)

    aq = rope(heads(aq, ATT_HEADS, ATT_HEAD_DIM), pos, ROT_DIM, ROPE_THETA_2)
    ak = rope(heads(ak, ATT_HEADS, ATT_HEAD_DIM), pos, ROT_DIM, ROPE_THETA_2)
    a = dilated_attention(aq, ak, heads(av, ATT_HEADS, ATT_HEAD_DIM))
    a = a * lax.rsqrt(jnp.mean(a * a, axis=-1, keepdims=True) + RMS_EPS)
    a = a.transpose(0, 2, 1, 3).reshape(B, S, ATT_WIDTH) * attn_gn_g.astype(jnp.float32)

    rq = rope(heads(rq, RET_HEADS, RET_HEAD_DIM).astype(jnp.float32), pos, RET_HEAD_DIM, RET_ROPE_THETA)
    rk = rope(heads(rk, RET_HEADS, RET_HEAD_DIM).astype(jnp.float32), pos, RET_HEAD_DIM, RET_ROPE_THETA)
    rk = rk * (RET_HEAD_DIM ** -0.5)
    r = retention(rq, rk, heads(rv, RET_HEADS, RET_HEAD_DIM).astype(jnp.float32))
    mu = jnp.mean(r, axis=-1, keepdims=True)
    var = jnp.mean(jnp.square(r - mu), axis=-1, keepdims=True)
    r = (r - mu) * lax.rsqrt(var + GN_EPS)
    r = r.transpose(0, 2, 1, 3).reshape(B, S, RET_WIDTH) * ret_gn_g.astype(jnp.float32)
    r = jax.nn.silu(rg.astype(jnp.float32)) * r

    y = jnp.concatenate([a, r], axis=-1).astype(h.dtype)
    return y @ w_out

def memory_cross_attn(h, mem, mem_norm_g, w_q, w_kv, w_o):
    B, S, _ = h.shape
    mh = rms_norm(mem, mem_norm_g)
    q = (h @ w_q).reshape(B, S, XATT_HEADS, XATT_HEAD_DIM)
    k, v = jnp.split(mh @ w_kv, 2, axis=-1)
    k = k.reshape(B, N_MEM, XATT_HEADS, XATT_HEAD_DIM)
    v = v.reshape(B, N_MEM, XATT_HEADS, XATT_HEAD_DIM)
    s = jnp.einsum('bshd,bmhd->bhsm', q, k).astype(jnp.float32) * (XATT_HEAD_DIM ** -0.5)
    p = jax.nn.softmax(s, axis=-1)
    o = jnp.einsum('bhsm,bmhd->bshd', p.astype(v.dtype), v).reshape(B, S, D_MODEL)
    return o @ w_o

def swiglu(h, w_gate_up, w_down):
    g, u = jnp.split(h @ w_gate_up, 2, axis=-1)
    return (jax.nn.silu(g) * u) @ w_down

def second_inputs(seed: int = 0) -> dict:
    key = jax.random.key(seed)
    ks = jax.random.split(key, 20)

    def w(k, shape, fan_in):
        return jax.random.normal(k, shape, jnp.float32) * (fan_in ** -0.5)

    def gain(k, n):
        return 1.0 + 0.05 * jax.random.normal(k, (DEPTH_2, n), jnp.float32)

    return {
        "x": jax.random.normal(ks[0], (BATCH, SEQ, D_MODEL), jnp.float32),
        "mem": jax.random.normal(ks[1], (BATCH, N_MEM, D_MODEL), jnp.float32),
        "pre_mix_g": gain(ks[2], D_MODEL),
        "post_mix_g": gain(ks[3], D_MODEL),
        "w_in": w(ks[4], (DEPTH_2, D_MODEL, IN_PROJ_WIDTH), D_MODEL),
        "attn_gn_g": gain(ks[5], ATT_WIDTH),
        "ret_gn_g": gain(ks[6], RET_WIDTH),
        "w_out": w(ks[7], (DEPTH_2, MIX_WIDTH, D_MODEL), MIX_WIDTH),
        "pre_mem_g": gain(ks[8], D_MODEL),
        "post_mem_g": gain(ks[9], D_MODEL),
        "mem_norm_g": gain(ks[10], D_MODEL),
        "w_q_mem": w(ks[11], (DEPTH_2, D_MODEL, D_MODEL), D_MODEL),
        "w_kv_mem": w(ks[12], (DEPTH_2, D_MODEL, 2 * D_MODEL), D_MODEL),
        "w_o_mem": w(ks[13], (DEPTH_2, D_MODEL, D_MODEL), D_MODEL),
        "pre_ffn_g": gain(ks[14], D_MODEL),
        "post_ffn_g": gain(ks[15], D_MODEL),
        "w_gate_up": w(ks[16], (DEPTH_2, D_MODEL, 2 * FFN_HIDDEN_2), D_MODEL),
        "w_down": w(ks[17], (DEPTH_2, FFN_HIDDEN_2, D_MODEL), FFN_HIDDEN_2),
    }

def second_block(x, mem, pre_mix_g, post_mix_g, w_in, attn_gn_g, ret_gn_g, w_out,
              pre_mem_g, post_mem_g, mem_norm_g, w_q_mem, w_kv_mem, w_o_mem,
              pre_ffn_g, post_ffn_g, w_gate_up, w_down):
    for l in range(DEPTH_2):
        y = hybrid_mixer(rms_norm(x, pre_mix_g[l]), w_in[l], attn_gn_g[l], ret_gn_g[l], w_out[l])
        x = x + rms_norm(y, post_mix_g[l])
        y = memory_cross_attn(rms_norm(x, pre_mem_g[l]), mem, mem_norm_g[l],
                              w_q_mem[l], w_kv_mem[l], w_o_mem[l])
        x = x + rms_norm(y, post_mem_g[l])
        y = swiglu(rms_norm(x, pre_ffn_g[l]), w_gate_up[l], w_down[l])
        x = x + rms_norm(y, post_ffn_g[l])
    return x


def setup_inputs(seed=0):
    out = dict(first_inputs(seed))
    for name, value in second_inputs(seed + 1).items():
        if name != "x":
            out[name + "_2"] = value
    return out


def reference(
    x, c, positions, w_mod, b_mod, ln_g, ln_b, ffn_w_in, ffn_w_out, mla_w_in, mla_q_norm_g,
    mla_kv_norm_g, mla_w_q_up, mla_w_kv_up, mla_w_out, diff_w_in, diff_lambda_q, diff_lambda_k,
    diff_subln_g, diff_w_out, ssm_w_in, ssm_conv_w, ssm_conv_b, ssm_dt_bias, ssm_a_log,
    ssm_d_skip, ssm_norm_g, ssm_w_out, mem_2, pre_mix_g_2, post_mix_g_2, w_in_2, attn_gn_g_2,
    ret_gn_g_2, w_out_2, pre_mem_g_2, post_mem_g_2, mem_norm_g_2, w_q_mem_2, w_kv_mem_2,
    w_o_mem_2, pre_ffn_g_2, post_ffn_g_2, w_gate_up_2, w_down_2,
):
    x = first_block(
        x, c, positions, w_mod, b_mod, ln_g, ln_b, ffn_w_in, ffn_w_out, mla_w_in, mla_q_norm_g,
        mla_kv_norm_g, mla_w_q_up, mla_w_kv_up, mla_w_out, diff_w_in, diff_lambda_q,
        diff_lambda_k, diff_subln_g, diff_w_out, ssm_w_in, ssm_conv_w, ssm_conv_b, ssm_dt_bias,
        ssm_a_log, ssm_d_skip, ssm_norm_g, ssm_w_out,
    )
    return second_block(
        x, mem_2, pre_mix_g_2, post_mix_g_2, w_in_2, attn_gn_g_2, ret_gn_g_2, w_out_2,
        pre_mem_g_2, post_mem_g_2, mem_norm_g_2, w_q_mem_2, w_kv_mem_2, w_o_mem_2, pre_ffn_g_2,
        post_ffn_g_2, w_gate_up_2, w_down_2,
    )


_drawn_inputs = setup_inputs


def setup_inputs(seed=0):
    import zlib

    import numpy as np

    out = dict(_drawn_inputs(seed))
    spreads = {}
    factors = {'mla_q_norm_g': 8.0,
     'mla_kv_norm_g': 8.0,
     'diff_lambda_q': 8.0,
     'diff_lambda_k': 8.0,
     'diff_subln_g': 8.0,
     'ssm_conv_b': 8.0,
     'ssm_d_skip': 8.0,
     'ssm_norm_g': 8.0,
     'ret_gn_g_2': 2.854}
    for name, (base, spread) in spreads.items():
        noise = np.random.default_rng([zlib.crc32(name.encode()), seed]).standard_normal(out[name].shape)
        drawn = base * np.exp(spread * noise) if base else spread * noise
        out[name] = __import__('jax').numpy.asarray(drawn.astype(out[name].dtype))
    for name, factor in factors.items():
        out[name] = (out[name] * factor).astype(out[name].dtype)
    return out
```

```python
import math
from contextlib import ExitStack

import numpy as np

import concourse.bass as bass
from concourse import mybir

F32 = mybir.dt.float32
F32R = mybir.dt.float32r
I32 = mybir.dt.int32
ACT = mybir.ActivationFunctionType
ALU = mybir.AluOpType
AX = mybir.AxisListType.X
ds = bass.ds

P = 128
D = 1024
DC = D // P
S = 256
ST = S // P
DEPTH = 4
SUB = 3
F = 2816
FC = F // P
FP = F // 256
LN_EPS, RMS_EPS = 1e-5, 1e-6
ALPHA = (2.0 * DEPTH) ** 0.25
NEG = -1e30
HALF = 1024
SLOT = 2 * HALF
RAW = 4
CW = P + S
MODU = 3 * D // 2
TWO_PI = 2 * math.pi

MLA_H, MLA_ROPE, QR, KVR = 8, 64, 384, 256
SSM_H, SSM_G, SSM_INNER = 32, 4, 2048
XH = 4
RET_H = 4


def constants():
    i = np.arange(P)
    c = {}
    c["ident"] = np.eye(P)
    c["ones"] = np.ones((P, P))
    c["half"] = (i[:, None] // 64 == i[None, :] // 64).astype(float)
    tri = (i[:, None] <= i[None, :]).astype(float)
    c["tri"] = np.concatenate([tri, np.ones((P, P)), tri], 1)
    low = np.where(i[None, :] <= i[:, None], 0.0, NEG)
    c["causal"] = np.concatenate([low, np.zeros((P, P)), low], 1)

    def rotation(width, half):
        m = np.zeros((P, P))
        for f in range(P):
            g, r = f // width * width, f % width
            if r < half:
                m[g + r + half, f] = -1.0
            elif r < 2 * half:
                m[g + r - half, f] = 1.0
        return m

    c["rot_mla"] = rotation(64, 32)
    inv = np.float32(10000.0) ** (-np.arange(0, MLA_ROPE, 2, dtype=np.float32) / np.float32(MLA_ROPE))
    c["misc"] = np.zeros((P, 8))
    c["misc"][:, 0] = inv[i % 32]
    c["misc"][:, 1] = LN_EPS
    c["misc"][:, 2] = RMS_EPS
    c["misc"][:, 3] = math.pi / 2
    c["misc"][:, 4] = 1.0
    first = list(c)

    c["rot_att"] = rotation(64, 8)
    c["rot_ret"] = rotation(128, 64)
    pos = np.arange(S, dtype=np.float32)

    def tables(width, rot, theta):
        half = rot // 2
        inv = np.float32(theta) ** (-(np.arange(0, rot, 2, dtype=np.float32) / np.float32(rot)))
        cos, sin = np.ones((P, S)), np.zeros((P, S))
        for f in range(P):
            r = f % width
            if r < rot:
                ang = pos * inv[r % half]
                cos[f], sin[f] = np.cos(ang.astype(np.float64)), np.sin(ang.astype(np.float64))
        return cos, sin

    c["cos_att"], c["sin_att"] = tables(64, 16, 500000.0)
    c["cos_ret"], c["sin_ret"] = tables(128, 128, 10000.0)

    def causal_table(fn):
        q, k = i[:, None], i[None, :]
        return np.concatenate([fn(q, k), fn(q + P, k), fn(q + P, k + P)], 1)

    def seen(q, k):
        d = q - k
        return (d >= 0) * ((d <= 128).astype(float) + (d % 4 == 0) + (d % 16 == 0))

    times = causal_table(seen)
    c["dil_add"] = np.where(times > 0, 0.0, NEG)
    c["dil_times"] = times
    for h in range(RET_H):
        g = np.log1p(-(2.0 ** (-5.0 - h)))

        def decay(k, q, g=g):
            return np.where(q >= k, np.exp(g * np.maximum(q - k, 0)), 0.0) * 128.0 ** -0.5
        k, q = i[:, None], np.arange(S)[None, :]
        c[f"decay{h}"] = np.concatenate([decay(k, q), decay(k + P, q[:, P:])], 1)
    second = [k for k in c if k not in first]

    def pack(names):
        at, o = {}, 0
        for k in names:
            at[k] = (o, c[k].shape[1])
            o += c[k].shape[1]
        return np.concatenate([c[k] for k in names], 1).astype(np.float32), at

    return pack(first), pack(second)


ROWS = (("mla_q_norm_g", 6), ("mla_kv_norm_g", 4), ("diff_subln_g", 1), ("ssm_conv_b", 24), ("ssm_norm_g", 16),
        ("attn_gn_g_2", 4), ("ret_gn_g_2", 4), ("pre_mix_g_2", 8), ("post_mix_g_2", 8), ("pre_mem_g_2", 8),
        ("post_mem_g_2", 8), ("mem_norm_g_2", 8), ("pre_ffn_g_2", 8), ("post_ffn_g_2", 8), ("c", 8))
NROWS = sum(r for _, r in ROWS)
LNG, LNB, MISC = 288, 384, 480
CONVW = MISC + NROWS
VCOLS = CONVW + 96


def column(name, at=0):
    o = MISC
    for k, r in ROWS:
        if k == name:
            return o + at
        o += r


ATT = ("scores", "maxed", "exped", "probs", "turned", "turned_out", "mixed", "mixed_out")
SIGNALS = {
    "init": dict(vec_turned=2, vec_ready=3, cond_ready=1, z_in=1, mod_sum=1, angle=1, rope_sin=2, lam_sum=1, lam_exp=1, hf=4, h_hi=4, h_lo=4, ax_ready=1),
    "ffn": dict(a_hi=FP, a_lo=FP),
    "ln": dict(z_ready=8, ln_sum=1, centred=2, squared=4, ln_var=1, std=1, mod_sum=1, hf=4, h_hi=4, h_lo=4, ax_ready=1),
    "mla": dict(lat_sq=3, lat_sum=1, kr_rot=1, lat_std=1, lat_n=2, lat_hi=2, lat_lo=2, kr_ready=1, qr_rot=2, qr_ready=2, mixed_hi=MLA_H,
                **{k: MLA_H for k in ATT}),
    "diff": dict(fin_sq=4, fin_sum=4, fin_std=4, fin_n=4, fin_hi=4, fin_lo=4, **{k: 8 for k in ATT}),
    "ssm": dict(conv_out=12, x_turned=8, x_out=8, dt_in=1, dt_ln=1, adt=1, acum=1, acum_t=1, cb=4, cb_out=4, spread=SSM_H,
                dec=SSM_H, dec_exp=SSM_H, mixing=SSM_H, ssd=SSM_H, y_out=SSM_H // 2,
                fin_sq=4, fin_sum=4, fin_std=4, fin_n=4, fin_hi=4, fin_lo=4),
    "ln_last": dict(z_ready=8, ln_sum=1, centred=2, squared=4, ln_var=1, std=1, mod_sum=1, ax_ready=1),
    "pre": dict(squared=4, x_sum=1, std=1, hf=4, h_hi=4, h_lo=4),
    "post": dict(y_sq=2, y_sum=1, std=1, ax_ready=1),
    "hyb": dict(rot=8, rot_out=8, kq=4, kq_out=4, ret=4, ret_out=4, fin_mean=2, fin_cent=2,
                fin_sq=4, fin_sum=4, fin_std=4, fin_n=4, fin_hi=4, fin_lo=4, **{k: 8 for k in ATT}),
    "mem": dict(mem_std=1, mem_n=1, mem_turned=1, mem_f=1, mem_hi=1, mem_lo=1),
    "xatt": dict(mixed_hi=XH, **{k: XH for k in ATT}),
    "store": dict(out_turned=1, out_ready=1),
}


class Step:
    def __init__(self, kind, args, n):
        self.kind, self.args = kind, args
        self.n = n
        self.lin = {}


class Linear:
    def __init__(self, n, b, l, p, upb):
        self.n, self.b, self.l, self.p, self.upb = n, b, l, p, upb


class Plan:
    def __init__(self, steps):
        self.steps, self.total = [], {}
        self.mods = SUB * DEPTH
        self.blocks = []
        self.used = []
        self.load_at = []
        self.slot = [0] * RAW
        self.lin = 0
        self.free_need, self.free_val = [], []
        self.free = [0, 0]
        for name, *args in steps:
            st = Step(name, args, {k: self.total.get(k, 0) for k in SEMS})
            {"ffn": self.plan_ffn, "mla": self.plan_mla, "diff": self.plan_diff, "ssm": self.plan_ssm, "hyb": self.plan_hyb,
             "xatt": self.plan_xatt}.get(name, self.plan_none)(st, *args)
            for k, v in SIGNALS[name].items():
                self.total[k] = self.total.get(k, 0) + v
            self.steps.append(st)

    def pair(self, explicit=True):
        p = len(self.free_need)
        self.free_need.append(self.free[p % 2])
        self.free[p % 2] += explicit
        self.free_val.append(self.free[p % 2])
        return p

    def block(self, loads, units):
        b = len(self.blocks)
        self.blocks.append(loads)
        self.slot[b % RAW] += 16 * len(loads)
        self.load_at.append(self.slot[b % RAW])
        self.used.append((self.lin + units[0], self.lin + units[1]))
        self.lin += units[-1]
        return b

    def linear(self, st, name, loads, units=(1, 2), pairs=1):
        g = Linear(len(loads), len(self.blocks), self.lin, len(self.free_need), units[-1])
        for x in loads:
            self.block(x, units)
            for _ in range(pairs):
                self.pair()
        st.lin[name] = g
        return g

    def project(self, st, w, k):
        n = k // 2
        g = Linear(n, len(self.blocks), self.lin, len(self.free_need), 2)
        for j in range(n):
            self.block([("out", w, j)], (1, 2) if j < n - 1 else (1, 3))
        self.pair(False), self.pair(False)
        st.lin["out"] = g

    def plan_none(self, st, *args):
        pass

    def cols(self, st, name, w, lo, hi):
        self.linear(st, name, [[("cols", w, c)] for c in range(lo, hi, 256)])

    def plan_diff(self, st, s, w):
        self.cols(st, "qk", w["in"], 0, 2 * D)
        self.cols(st, "v", w["in"], 2 * D, 3 * D)
        self.project(st, w["out"], DC)

    def plan_ssm(self, st, s, w):
        self.cols(st, "z", w["in"], 0, SSM_INNER)
        self.cols(st, "xbc", w["in"], SSM_INNER, 2 * SSM_INNER + D)
        self.linear(st, "dt", [[("dt", w["in"], 2 * SSM_INNER + D)]], (1, 1))
        self.project(st, w["out"], SSM_INNER // P)

    def plan_hyb(self, st, w):
        for i, k in enumerate(("aqk", "av", "rqk", "rv", "rg")):
            lo, hi = (0, 1024, 1536, 2560, 3072)[i], (1024, 1536, 2560, 3072, 3584)[i]
            self.cols(st, k, w["in"], lo, hi)
        self.project(st, w["out"], DC)

    def plan_xatt(self, st, w):
        self.cols(st, "q", w["q"], 0, D)
        self.cols(st, "k", w["kv"], 0, D)
        self.cols(st, "v", w["kv"], D, 2 * D)
        self.project(st, w["out"], DC)

    def plan_ffn(self, st, s, w_in, w_out):
        self.linear(st, "in", [[("cols", w_in, (j % 2) * F + (j // 2) * 256)] for j in range(2 * FP)])
        self.project(st, w_out, FC)

    def plan_mla(self, st, s, w):
        self.linear(st, "latent", [[("cols", w["in"], 0)], [("cols", w["in"], 256)],
                                   [("part", w["in"], 512, 0, 192), ("part", w["in"], 640, 192, 64)]])
        self.linear(st, "q", [[("q_up", w["q"], h, k) for k in range(3)] + [("q_up_rope", w["q"], h, k) for k in range(3)]
                              for h in range(0, MLA_H, 2)], (1, 1))
        self.linear(st, "kv", [[("rows2", w["kv"], h)] for h in range(0, MLA_H, 4)], (2, 2), pairs=2)
        self.project(st, w["out"], DC)


SEMS = sorted({k for v in SIGNALS.values() for k in v})


def walk(eng, g, turn, first=2, last=0):
    rounds = (g.n - first - last) // 4
    if rounds < 2:
        first, rounds = g.n, 0
    elif not last:
        first = g.n - 4 * rounds
    for i in range(first):
        turn(i, None)
    if rounds:
        with eng.Fori(0, rounds) as it:
            for i in range(first, first + 4):
                turn(i, it)
        for i in range(first + 4 * rounds, g.n):
            turn(i, None)


def program(nc, plan, A, out, first, second):
    steps = plan.steps
    NB = len(plan.blocks)
    ctx = ExitStack()
    with ctx:
        def sem(name):
            return ctx.enter_context(nc.semaphore(name))

        arena = ctx.enter_context(nc.sbuf_tensor("arena", [P, 53200], F32))
        base = 16512
        top = [base]

        def at(name, shape, offset, dt=F32):
            assert base <= offset and offset + 4 * int(np.prod(shape[1:])) <= base + 4 * 53200 - 64
            return nc.alloc_sbuf_tensor_at(name, shape, dt, offset=offset)

        def room(nbytes):
            o = top[0]
            top[0] += (nbytes + 31) // 32 * 32
            return o

        raw = [at(f"raw{i}", [P, SLOT], room(4 * SLOT)) for i in range(RAW)]
        whi = [at(f"whi{i}", [P, SLOT], room(4 * SLOT), F32R) for i in range(2)]
        wlo = [at(f"wlo{i}", [P, SLOT], room(4 * SLOT), F32R) for i in range(2)]
        o_ah, o_al, o_hh, o_hl = room(4 * FC * S), room(4 * FC * S), room(4 * DC * S), room(4 * DC * S)
        A_hi, A_lo = at("A_hi", [P, FC, S], o_ah, F32R), at("A_lo", [P, FC, S], o_al, F32R)
        H_hi, H_lo = at("H_hi", [P, DC, S], o_hh, F32R), at("H_lo", [P, DC, S], o_hl, F32R)
        ax = at("ax", [P, DC, S], room(4 * DC * S))
        o_z = room(4 * DC * S)
        z = at("z", [P, DC, S], o_z)
        o_hf = room(4 * DC * S)
        hf = at("hf", [P, DC, S], o_hf)
        o_s1 = room(4 * 16 * S)
        o_mod = room(4 * 2 * MODU)
        mod_w = at("mod_w", [P, 2, MODU], o_mod)
        mod_acc = at("mod_acc", [P, 2, MODU], room(4 * 2 * MODU))
        K1 = at("K1", [P, first[2]], room(4 * first[2]))
        V = at("V", [P, VCOLS], room(4 * VCOLS))
        cond = at("cond", [P, DC], room(32))
        modc = at("modc", [P, 24], room(96))
        G1, B1, G2, B2, gw = (at(k, [P, DC], room(32)) for k in ("G1", "B1", "G2", "B2", "gw"))
        t8 = at("t8", [P, 2, DC], room(64))
        std = at("std", [P, 2, S], room(8 * S))
        cosm, sinm = at("cosm", [P, S], room(4 * S)), at("sinm", [P, S], room(4 * S))
        tiny = at("tiny", [P, 64], room(256))
        pool_tick = at("pool_tick", [P, 16], room(64))

        sq = at("sq", [P, DC, S], o_s1 + 4 * DC * S)
        sg = at("sg", [P, 2, 2, S], o_s1)
        am = at("am", [P, 2, 2, S], o_s1 + 16 * S)
        rows = at("rows", [P, 8, P], o_al)
        x_in = at("x_in", [P, ST, D], o_ah)
        x_out = at("x_out", [P, ST, D], o_s1)
        posi = at("posi", [P, S], o_al + 8192, I32)
        ang = at("ang", [P, 3, S], o_al + 12288)
        lat = at("lat", [P, 6, S], o_s1)
        latn = at("latn", [P, 5, S], o_hf)
        QN = at("QN", [P, DC, S], o_ah + 20 * S)
        QRp = at("QRp", [P, 4, S], o_ah + 52 * S)
        KRp = at("KRp", [P, S], o_ah + 68 * S)
        KN = at("KN", [P, DC, S], o_al + 20 * S)
        VT = at("VT", [P, ST, D], o_al + 52 * S)
        rtmp = at("rtmp", [P, 2, 2, S], o_s1 + 4 * 8 * S)
        prob = at("prob", [P, 2, HALF], o_hf)
        probT = at("probT", [P, 2, 512], o_s1 + 4 * 12 * S)
        stat = at("stat", [P, 2, 16], room(128))
        sqj = at("sqj", [P, D], o_s1 + 4 * DC * S)
        O1 = at("O1", [P, DC, S], o_s1)
        zr = at("zr", [P, DC, S], o_z, F32R)
        M_hi, M_lo = A_hi[:, 14:22, :], zr
        RG = at("RG", [P, 4, S], o_ah)
        Z = at("Z", [P, 16, S], o_s1)
        XC, XT = at("XC", [P, 16, S], o_ah), at("XT", [P, ST, SSM_INNER], o_al)
        Bm, Cm = at("Bm", [P, 4, S], o_ah + 64 * S), at("Cm", [P, 4, S], o_al + 64 * S)
        CB = at("CB", [P, SSM_G, CW], o_hh)
        dec, mixw = at("dec", [P, 2, CW], o_hl), at("mixw", [P, 2, CW], o_hl + 8 * CW)
        conv = at("conv", [P, 2, 2, S], o_hf)
        yt = at("yt", [P, 2, S], o_hf)
        dts = at("dts", [P, 8, 2, SSM_H], o_hf + 16 * S)
        acT = at("acT", [SSM_H, S], o_hf + 16 * S + 4 * 512)
        sqg = at("sqg", [P, 2, 4, S], o_hf)
        dtb, alog = at("dtb", [P, SSM_H], room(128)), at("alog", [P, SSM_H], room(128))
        skiprow, dskip = at("skiprow", [P, SSM_H], room(128)), at("dskip", [P, 16], room(64))
        lamrow = at("lamrow", [P, 4, 64], o_al + 16384)
        K2 = at("K2", [P, second[2]], o_mod)
        mem = at("mem", [P, ST, D], o_mod + 4 * second[2])
        assert 4 * second[2] + 4 * ST * D <= 8 * 2 * MODU
        assert top[0] <= base + 4 * 53200 - 64, top[0]

        ps = ctx.enter_context(nc.psum_tensor("ps", [P, 8, 512], F32))

        def kc(name, lo=0, hi=None):
            o, w = first[1][name]
            return K1[:, o + lo:o + (w if hi is None else hi)]

        def kc2(name, lo=0, hi=None):
            o, w = second[1][name]
            return K2[:, o + lo:o + (w if hi is None else hi)]

        ident, ones = kc("ident"), kc("ones")

        def bank(p):
            return 2 * (p % 2)

        def ybank(g, c):
            b = bank(g.p + c // 4) + c % 4 // 2
            return ps[:, b, c % 2 * S:(c % 2 + 1) * S]

        def vcol(o, n=1):
            return V[:, o:o + n]

        w_loaded = [sem(f"w_loaded{i}") for i in range(RAW)]
        w_hi, w_lo = sem("w_hi"), sem("w_lo")
        products = sem("products")
        banks_free = [sem("banks_free0"), sem("banks_free1")]
        init_loaded, mod_loaded = sem("init_loaded"), [sem("mod_loaded0"), sem("mod_loaded1")]
        second_loaded = sem("second_loaded")
        mod_used = sem("mod_used")
        dve_step, act_step, pool_step = sem("dve_step"), sem("act_step"), sem("pool_step")
        stored = sem("stored")
        s = {k: sem(k) for k in SEMS}

        def rows_of(name):
            x = A[name]
            while len(x.shape) > 1:
                x = x.rearrange("a b -> (a b)") if len(x.shape) == 2 else x.rearrange("a b c -> a (b c)")
            return x.rearrange("(r p) -> r p", p=P)

        def init_loads():
            yield K1[:, :], first[0]
            o = 0
            for name, r in ROWS[::-1]:
                o += r
                yield rows[NROWS - o:NROWS - o + r, 6, :], rows_of(name)
            yield x_in[:, :, :], A["x"][0].rearrange("(t p) d -> p t d", p=P)
            yield rows[0:96, 4, :], rows_of("ln_g")
            yield rows[0:96, 5, :], rows_of("ln_b")
            for i in range(DEPTH):
                yield rows[0:72, i, :], A["b_mod"][i].rearrange("(r p) -> r p", p=P)
            yield rows[0:96, 7, :], rows_of("ssm_conv_w")
            for i, k in enumerate(("diff_lambda_q", "diff_lambda_k")):
                yield lamrow[:, 2 * i:2 * i + 2, :], A[k][0].partition_broadcast(P)
            yield dtb[:, :], A["ssm_dt_bias"][0].partition_broadcast(P)
            yield alog[:, :], A["ssm_a_log"][0].partition_broadcast(P)
            yield skiprow[:, :], A["ssm_d_skip"][0].partition_broadcast(P)
            yield posi[:, :], A["positions"][0].partition_broadcast(P)
        n_init = 16 * len(list(init_loads()))

        block = ctx.enter_context(nc.Block())

        @block.sync
        def _(sp):
            def view(kind, slot, *a):
                r = raw[slot]
                if kind == "cols":
                    w, c = a
                    return r[:, :].rearrange("p (k n) -> p k n", k=DC), w.rearrange("(k p) n -> p k n", p=P)[:, :, c]
                if kind == "dt":
                    w, c = a
                    return (r[:, 0:DC * SSM_H].rearrange("p (k n) -> p k n", k=DC),
                            w.rearrange("(k p) n -> p k n", p=P)[:, :, c:c + SSM_H])
                if kind == "part":
                    w, c, to, n = a
                    return (r[:, :].rearrange("p (k n) -> p k n", k=DC)[:, :, to:to + n],
                            w.rearrange("(k p) n -> p k n", p=P)[:, :, c:c + n])
                if kind == "out":
                    w, k = a
                    return r[:, :].rearrange("p (k n) -> p k n", k=2), w.rearrange("(k p) n -> p k n", p=P)[:, k, :]
                if kind == "rows2":
                    w, h = a
                    return (r[:, :].rearrange("p (k n) -> p k n", k=2),
                            w.rearrange("(k p) n -> p k n", p=P)[:, :, h * 256:h * 256 + 1024])
                w, h, k = a
                v = w.rearrange("(k p) (h n) -> p k h n", p=P, n=192)
                o = k * 384
                if kind == "q_up":
                    return r[:, o:o + 256].rearrange("p (h n) -> p h n", h=2), v[:, k, h:h + 2, 0:128]
                return r[:, o + 256:o + 384].rearrange("p (h n) -> p h n", h=2), v[:, k, h:h + 2, 128:192]

            def load(b, it=None):
                if b >= RAW:
                    sp.wait_ge(w_lo, 2 * (b - RAW + 1) if it is None else 2 * (b - RAW + 1) + 8 * it)
                for kind, *a in plan.blocks[b]:
                    if kind == "cols":
                        w, c = a
                        a = [w, ds(c if it is None else it * 512 + c, 256)]
                    elif kind == "out":
                        w, j = a
                        a = [w, ds(2 * j if it is None else it * 8 + 2 * j, 2)]
                    sp.dma_start(*view(kind, b % RAW, *a)).then_inc(w_loaded[b % RAW], 16)

            def load_mod(sub, k, half, it=None):
                u = 16 * sub + 2 * k + half
                if u >= 2:
                    sp.wait_ge(mod_used, u - 1 if it is None else u - 1 + 2 * it)
                w = A["w_mod"][sub // SUB][:, sub % SUB * 3 * D + half * MODU:][:, 0:MODU]
                row = k * P if it is None else it * P + k * P
                sp.dma_start(mod_w[:, half, :], w[ds(row, P), :]).then_inc(mod_loaded[half], 16)

            for st in steps:
                if st.kind == "init":
                    for dst, src in init_loads():
                        sp.dma_start(dst, src).then_inc(init_loaded, 16)
                    for k in range(DC):
                        for half in range(2):
                            load_mod(0, k, half)
                if st.kind == "ffn":
                    nxt = st.args[0] + 1
                    mods = nxt < min(SUB * DEPTH, plan.mods)
                    def turn_in(i, it):
                        load(g.b + i, it)
                        if mods and i >= 2 and i % 2:
                            load_mod(nxt, (i - 2) // 4, (i - 2) // 2 % 2, it)

                    g = st.lin["in"]
                    first = 6 if g.b < RAW else 2
                    walk(sp, g, turn_in, first)

                    def turn_out(i, it):
                        load(g.b + i, it)
                        if mods and i in (1, 3):
                            load_mod(nxt, 6, i // 2, it)

                    for half in range(2 * mods):
                        load_mod(nxt, 5, half)
                    g = st.lin["out"]
                    walk(sp, g, turn_out, 1, 2)
                    if st.args[0] == SUB * DEPTH - 1:
                        sp.wait_ge(s["mod_sum"], st.n["mod_sum"])
                        sp.dma_start(K2[:, :], second[0]).then_inc(second_loaded, 16)
                        sp.dma_start(mem[:, :, :], A["mem_2"][0].rearrange("(t p) d -> p t d", p=P)).then_inc(second_loaded, 16)
                if st.kind in ("mla", "diff", "ssm", "hyb", "xatt"):
                    nxt = st.args[0] + 1 if st.kind not in ("hyb", "xatt") else 10 ** 6
                    todo = [(nxt, k, half) for k in range(DC) for half in range(2)] if nxt < plan.mods else []
                    for g in st.lin.values():
                        for b in range(g.b, g.b + g.n):
                            load(b)
                            for _ in range(2):
                                if todo:
                                    load_mod(*todo.pop(0))
                    for x in todo:
                        load_mod(*x)
                if st.kind == "store":
                    sp.wait_ge(s["out_ready"], st.n["out_ready"] + 1)
                    sp.dma_start(out[0].rearrange("(t p) d -> p t d", p=P), x_out[:, :, :]).then_inc(stored, 16)
                    sp.wait_ge(stored, 16)

        @block.gpsimd
        def _(pool):
            n = min(plan.mods, SUB * DEPTH)
            if n > 1:
                pool.wait_ge(s["cond_ready"], 1)
                with pool.Fori(1, n) as sub:
                    pool.wait_ge(s["mod_sum"], sub)
                    for k in range(DC):
                        for half in range(2):
                            pool.wait_ge(mod_loaded[half], sub * 128 + 16 * (k + 1))
                            nc.gpsimd.tensor_tensor(pool_tick[:, 2 * k + half:2 * k + half + 1], cond[:, 0:1], cond[:, 0:1], ALU.add)
                            w = mod_w[:, half, :]
                            if k == 0:
                                nc.gpsimd.tensor_scalar(mod_acc[:, half, :], w, cond[:, 0:1], 1.0, ALU.mult, ALU.mult)\
                                    .then_inc(mod_used, 1)
                                continue
                            nc.gpsimd.tensor_scalar(w, w, cond[:, k:k + 1], 1.0, ALU.mult, ALU.mult).then_inc(pool_step, 1)
                            pool.wait_ge(pool_step, sub * 14 - 14 + 2 * (k - 1) + half + 1)
                            pool.wait_ge(mod_used, sub * 16 + 2 * k + half - 1)
                            nc.gpsimd.tensor_tensor(mod_acc[:, half, :], mod_acc[:, half, :], w, ALU.add)\
                                .then_inc(mod_used, 1)

        @block.scalar
        def _(act):
            step = [0]

            def link(ins):
                step[0] += 1
                ins.then_inc(act_step, 1)
                act.wait_ge(act_step, step[0])

            def copy(dst, src):
                return nc.scalar.activation(dst, src, ACT.Copy)

            def convert(b, it=None, upb=0):
                if b >= NB:
                    return
                act.wait_ge(w_loaded[b % RAW], plan.load_at[b] if it is None else plan.load_at[b] + 16 * it)
                for h in range(2):
                    if b >= 2:
                        u = plan.used[b - 2][h]
                        act.wait_ge(products, u if it is None else 4 * upb * it + u)
                    copy(whi[b % 2][:, h * HALF:(h + 1) * HALF], raw[b % RAW][:, h * HALF:(h + 1) * HALF]).then_inc(w_hi, 1)

            def split_h(n):
                for q in range(4):
                    act.wait_ge(s["hf"], n["hf"] + q + 1)
                    copy(H_hi[:, 2 * q:2 * q + 2, :], hf[:, 2 * q:2 * q + 2, :]).then_inc(s["h_hi"], 1)

            def evacuate(g, j, dst, b=None):
                p = g.p + j
                act.wait_ge(products, g.l + (j + 1) * g.upb)
                copy(dst, ps[:, bank(p):bank(p) + 2, 0:S]).then_inc(banks_free[p % 2], 1)

            def attend(n, heads, scale, kind):
                maps = 2 if kind == "diff" else 1
                full = kind == "xatt"
                width = 512 if full else CW
                tiles = ((0, S), (S, 2 * S)) if full else ((0, P), (P, CW))

                def exps(h):
                    act.wait_ge(s["maxed"], n["maxed"] + h + 1)
                    for m in range(maps):
                        for t, (a, b) in enumerate(tiles):
                            src = ps[:, 4 + h % 2, a:b] if full else prob[:, h % 2, m * width + a:m * width + b]
                            i = nc.scalar.activation(prob[:, h % 2, m * width + a:m * width + b], src, ACT.Exp,
                                                     bias=stat[:, h % 2, 4 + 2 * m + t:5 + 2 * m + t], scale=scale,
                                                     accum_out=None if kind == "dilated" else stat[:, h % 2, 8 + 2 * m + t:9 + 2 * m + t])
                    i.then_inc(s["exped"], 1)

                def turned(h):
                    act.wait_ge(s["turned"], n["turned"] + h + 1)
                    if h >= 2:
                        act.wait_ge(s["mixed"], n["mixed"] + h - 1)
                    copy(probT[:, h % 2, 0:width], ps[:, 6, 0:width]).then_inc(s["turned_out"], 1)

                def rounded(h):
                    act.wait_ge(s["mixed"], n["mixed"] + h + 1)
                    if kind == "xatt":
                        copy(H_hi[:, 2 * h:2 * h + 2, :], ps[:, 7, :].rearrange("p (c n) -> p c n", c=2)).then_inc(s["mixed_hi"], 1)
                    else:
                        copy(H_hi[:, h, :], ps[:, 7, 0:S]).then_inc(s["mixed_hi"], 1)

                for i in range(heads + 3):
                    if i < heads:
                        exps(i)
                    if 1 <= i <= heads:
                        turned(i - 1)
                    if i >= 3 and kind in ("mla", "xatt"):
                        rounded(i - 3)

            def act_init(st, n):
                act.wait_ge(s["vec_turned"], 1)
                copy(V[:, 0:288], ps[:, 0, 0:288]).then_inc(s["vec_ready"], 1)
                copy(V[:, 288:CONVW], ps[:, 1, 0:CONVW - 288]).then_inc(s["vec_ready"], 1)
                copy(V[:, CONVW:CONVW + 96], ps[:, 2, 0:96]).then_inc(s["vec_ready"], 1)
                act.wait_ge(s["vec_ready"], 3)
                nc.scalar.activation(cond[:, :], vcol(column("c"), DC), ACT.Silu).then_inc(s["cond_ready"], 1)
                act.wait_ge(s["lam_sum"], 1)
                nc.scalar.activation(tiny[:, 6:8], tiny[:, 4:6], ACT.Exp).then_inc(s["lam_exp"], 1)
                act.wait_ge(s["vec_turned"], 2)
                copy(z[:, :, :], ps[:, 4:8, :].rearrange("p b (c n) -> p (b c) n", c=2)).then_inc(s["z_in"], 1)
                act.wait_ge(s["angle"], 1)
                nc.scalar.activation(sinm[:, :], ang[:, 0, :], ACT.Sin).then_inc(s["rope_sin"], 1)
                link(nc.scalar.activation(ang[:, 1, :], ang[:, 0, :], ACT.Abs))
                nc.scalar.activation(cosm[:, :], ang[:, 1, :], ACT.Sin, bias=kc("misc", 3, 4), scale=-1.0).then_inc(s["rope_sin"], 1)
                convert(0)
                convert(1)
                split_h(n)

            def act_ln(st, n):
                for q in range(4):
                    if q % 2 == 0:
                        act.wait_ge(s["centred"], n["centred"] + q // 2 + 1)
                    nc.scalar.activation(sq[:, 2 * q:2 * q + 2, :], z[:, 2 * q:2 * q + 2, :], ACT.Square).then_inc(s["squared"], 1)
                act.wait_ge(s["ln_var"], n["ln_var"] + 1)
                nc.scalar.activation(std[:, 0, :], ps[:, 5, 0:S], ACT.Sqrt, bias=kc("misc", 1, 2), scale=1.0 / D).then_inc(s["std"], 1)
                if st.kind == "ln":
                    split_h(n)

            def act_ffn(st, n):
                g = st.lin["in"]

                def gate(i, it=None):
                    p = g.p + i
                    u = g.l + 2 * (i + 1)
                    act.wait_ge(products, u if it is None else 8 * it + u)
                    nc.scalar.activation(sg[:, i // 2 % 2], ps[:, bank(p):bank(p) + 2, 0:S], ACT.Silu)\
                        .then_inc(banks_free[p % 2], 1)

                def product_hi(j, it=None):
                    p = g.p + 2 * j + 1
                    v = plan.free_val[p]
                    act.wait_ge(banks_free[p % 2], v if it is None else 2 * it + v)
                    to = A_hi[:, 2 * j:2 * j + 2, :] if it is None else A_hi[:, ds(it * 4 + 2 * j, 2), :]
                    copy(to, am[:, j % 2]).then_inc(s["a_hi"], 1)

                def turn(i, it=None):
                    convert(g.b + i + 2, it, 2)
                    if i % 2 == 0:
                        gate(i, it)
                    if i % 2 == 0 and i >= 2:
                        product_hi(i // 2 - 1, it)

                walk(act, g, turn)
                product_hi(FP - 1)
                projected(st)

            def projected(st):
                g = st.lin["out"]
                walk(act, g, lambda i, it: convert(g.b + i + 2, it, 2), 1, 2)

            def act_mla(st, n):
                g = st.lin["latent"]
                for j in range(3):
                    convert(g.b + j + 2)
                    evacuate(g, j, lat[:, 2 * j:2 * j + 2, :])
                    act.wait_ge(banks_free[(g.p + j) % 2], plan.free_val[g.p + j])
                    m = 2 if j < 2 else 1
                    nc.scalar.activation(sq[:, 2 * j:2 * j + m, :], lat[:, 2 * j:2 * j + m, :], ACT.Square).then_inc(s["lat_sq"], 1)
                act.wait_ge(s["lat_sum"], n["lat_sum"] + 1)
                nc.scalar.activation(std[:, 0, :], ps[:, 4, 0:S], ACT.Sqrt, bias=kc("misc", 2, 3), scale=1.0 / QR)
                nc.scalar.activation(std[:, 1, :], ps[:, 4, S:2 * S], ACT.Sqrt, bias=kc("misc", 2, 3), scale=1.0 / KVR)\
                    .then_inc(s["lat_std"], 1)
                for i, (a, b) in enumerate(((0, 3), (3, 5))):
                    act.wait_ge(s["lat_n"], n["lat_n"] + i + 1)
                    copy(A_hi[:, a:b, :], latn[:, a:b, :]).then_inc(s["lat_hi"], 1)
                g = st.lin["q"]
                for j in range(g.n):
                    p = g.p + j
                    convert(g.b + j + 2)
                    act.wait_ge(products, g.l + j + 1)
                    copy(QN[:, 2 * j:2 * j + 2, :], ps[:, bank(p), :].rearrange("p (c n) -> p c n", c=2))
                    copy(QRp[:, j, :], ps[:, bank(p) + 1, 0:S]).then_inc(banks_free[p % 2], 1)
                g = st.lin["kv"]
                for j in range(g.n):
                    p = g.p + 2 * j
                    convert(g.b + j + 2)
                    act.wait_ge(products, g.l + 2 * j + 1)
                    copy(KN[:, 4 * j:4 * j + 4, :], ps[:, bank(p):bank(p) + 2, :].rearrange("p b (c n) -> p (b c) n", c=2))\
                        .then_inc(banks_free[p % 2], 1)
                    act.wait_ge(products, g.l + 2 * j + 2)
                    copy(VT[:, :, 512 * j:512 * j + 512], ps[:, bank(p + 1):bank(p + 1) + 2, :]).then_inc(banks_free[(p + 1) % 2], 1)
                attend(n, MLA_H, 192.0 ** -0.5, "mla")
                projected(st)

            def linear_evac(g, dst, func=ACT.Copy):
                for j in range(g.n):
                    p = g.p + j
                    convert(g.b + j + 2)
                    act.wait_ge(products, g.l + (j + 1) * g.upb)
                    nc.scalar.activation(dst(j), ps[:, bank(p):bank(p) + 2, 0:S], func).then_inc(banks_free[p % 2], 1)

            def fin_stats(n, i, scale, eps):
                act.wait_ge(s["fin_sum"], n["fin_sum"] + i + 1)
                nc.scalar.activation(z[:, 2 * i:2 * i + 2, :], ps[:, 4 + i, :].rearrange("p (c n) -> p c n", c=2), ACT.Sqrt,
                                     bias=kc("misc", eps, eps + 1), scale=scale).then_inc(s["fin_std"], 1)

            def fin_round(n):
                for i in range(4):
                    act.wait_ge(s["fin_n"], n["fin_n"] + i + 1)
                    copy(H_hi[:, 2 * i:2 * i + 2, :], O1[:, 2 * i:2 * i + 2, :]).then_inc(s["fin_hi"], 1)

            def act_diff(st, n):
                linear_evac(st.lin["qk"], lambda j: (QN if j < 4 else KN)[:, 2 * (j % 4):2 * (j % 4) + 2, :])
                linear_evac(st.lin["v"], lambda j: VT[:, :, 256 * j:256 * j + 256])
                attend(n, 8, 64.0 ** -0.5, "diff")
                for i in range(4):
                    act.wait_ge(s["mixed_out"], n["mixed_out"] + 8)
                    nc.scalar.activation(sq[:, 2 * i:2 * i + 2, :], O1[:, 2 * i:2 * i + 2, :], ACT.Square).then_inc(s["fin_sq"], 1)
                for i in range(4):
                    fin_stats(n, i, 1.0 / P, 2)
                fin_round(n)
                projected(st)

            def act_ssm(st, n):
                linear_evac(st.lin["z"], lambda j: Z[:, 2 * j:2 * j + 2, :], ACT.Silu)
                g = st.lin["xbc"]
                for j in range(g.n):
                    p = g.p + j
                    convert(g.b + j + 2)
                    act.wait_ge(banks_free[p % 2], plan.free_val[p])
                    dst = XC[:, 2 * j:2 * j + 2, :] if j < 8 else (Bm if j < 10 else Cm)[:, 2 * (j % 2):2 * (j % 2) + 2, :]
                    nc.scalar.activation(dst, conv[:, j % 2], ACT.Silu).then_inc(s["conv_out"], 1)
                g = st.lin["dt"]
                convert(g.b + 2)
                link(nc.scalar.activation(alog[:, :], alog[:, :], ACT.Exp))
                act.wait_ge(s["dt_in"], n["dt_in"] + 1)
                link(nc.scalar.activation(dts[:, 1], dts[:, 0], ACT.Abs))
                link(nc.scalar.activation(dts[:, 2], dts[:, 1], ACT.Exp, scale=-1.0))
                nc.scalar.activation(dts[:, 3], dts[:, 2], ACT.Ln, bias=kc("misc", 4, 5)).then_inc(s["dt_ln"], 1)
                for q in range(8):
                    act.wait_ge(s["x_turned"], n["x_turned"] + q + 1)
                    copy(XT[:, q // 4, q % 4 * 512:q % 4 * 512 + 512], ps[:, 4 + q % 2, :]).then_inc(s["x_out"], 1)
                act.wait_ge(s["acum"], n["acum"] + 1)
                copy(acT[:, :], ps[0:SSM_H, 4, 0:S]).then_inc(s["acum_t"], 1)
                for h in range(SSM_H):
                    act.wait_ge(s["dec"], n["dec"] + h + 1)
                    nc.scalar.activation(dec[:, h % 2, :], dec[:, h % 2, :], ACT.Exp).then_inc(s["dec_exp"], 1)
                act.wait_ge(s["y_out"], n["y_out"] + 16)

                def squares(i):
                    nc.scalar.activation(sqg[:, i % 2], Z[:, 4 * i:4 * i + 4, :], ACT.Square).then_inc(s["fin_sq"], 1)

                squares(0)
                for i in range(4):
                    if i < 3:
                        squares(i + 1)
                    act.wait_ge(s["fin_sum"], n["fin_sum"] + i + 1)
                    nc.scalar.activation(std[:, i % 2, :], ps[:, 4 + i % 2, 0:S], ACT.Sqrt, bias=kc("misc", 2, 3), scale=1.0 / 512)\
                        .then_inc(s["fin_std"], 1)
                    act.wait_ge(s["fin_n"], n["fin_n"] + i + 1)
                    copy(A_hi[:, 4 * i:4 * i + 4, :], Z[:, 4 * i:4 * i + 4, :]).then_inc(s["fin_hi"], 1)
                projected(st)

            def act_hyb(st, n):
                L = st.lin
                linear_evac(L["aqk"], lambda j: (QN if j < 2 else KN)[:, 2 * (j % 2):2 * (j % 2) + 2, :])
                linear_evac(L["av"], lambda j: VT[:, :, 256 * j:256 * j + 256])
                linear_evac(L["rqk"], lambda j: (QN if j < 2 else KN)[:, 4 + 2 * (j % 2):6 + 2 * (j % 2), :])
                linear_evac(L["rv"], lambda j: VT[:, :, 512 + 256 * j:768 + 256 * j])
                linear_evac(L["rg"], lambda j: RG[:, 2 * j:2 * j + 2, :], ACT.Silu)
                attend(n, 8, 64.0 ** -0.5, "dilated")
                for i in range(4):
                    if i < 2:
                        act.wait_ge(s["mixed_out"], n["mixed_out"] + 8)
                    else:
                        act.wait_ge(s["fin_cent"], n["fin_cent"] + i - 1)
                    nc.scalar.activation(sq[:, 2 * i:2 * i + 2, :], O1[:, 2 * i:2 * i + 2, :], ACT.Square).then_inc(s["fin_sq"], 1)
                for i in range(4):
                    fin_stats(n, i, 1.0 / 64 if i < 2 else 1.0 / P, 2 if i < 2 else 1)
                fin_round(n)
                projected(st)

            def act_mem(st, n):
                act.wait_ge(second_loaded, 32)
                act.wait_ge(s["h_hi"], n["h_hi"])
                for t in range(ST):
                    link(nc.scalar.activation(sqj[:, :], mem[:, t, :], ACT.Square, accum_out=tiny[:, 8 + t:9 + t]))
                nc.scalar.activation(tiny[:, 10:12], tiny[:, 8:10], ACT.Sqrt, bias=kc("misc", 2, 3), scale=1.0 / D).then_inc(s["mem_std"], 1)
                act.wait_ge(s["mem_f"], n["mem_f"] + 1)
                copy(M_hi, hf[:, :, :]).then_inc(s["mem_hi"], 1)

            def act_xatt(st, n):
                L = st.lin
                linear_evac(L["q"], lambda j: QN[:, 2 * j:2 * j + 2, :])
                linear_evac(L["k"], lambda j: KN[:, 2 * j:2 * j + 2, :])
                linear_evac(L["v"], lambda j: VT[:, :, 256 * j:256 * j + 256])
                attend(n, XH, 256.0 ** -0.5, "xatt")
                projected(st)

            def act_pre(st, n):
                act.wait_ge(s["ax_ready"], n["ax_ready"])
                for q in range(4):
                    nc.scalar.activation(sq[:, 2 * q:2 * q + 2, :], ax[:, 2 * q:2 * q + 2, :], ACT.Square).then_inc(s["squared"], 1)
                act.wait_ge(s["x_sum"], n["x_sum"] + 1)
                nc.scalar.activation(std[:, 0, :], ps[:, 5, 0:S], ACT.Sqrt, bias=kc("misc", 2, 3), scale=1.0 / D).then_inc(s["std"], 1)
                split_h(n)

            def act_post(st, n):
                g = steps[steps.index(st) - 1].lin["out"]
                for h in range(2):
                    act.wait_ge(products, g.l + 2 * (g.n - 1) + 2 + h)
                    b = bank(g.p + h)
                    nc.scalar.activation(sq[:, 4 * h:4 * h + 4, :], ps[:, b:b + 2, :].rearrange("p b (c n) -> p (b c) n", c=2), ACT.Square)\
                        .then_inc(s["y_sq"], 1)
                act.wait_ge(s["y_sum"], n["y_sum"] + 1)
                nc.scalar.activation(std[:, 0, :], ps[:, 5, 0:S], ACT.Sqrt, bias=kc("misc", 2, 3), scale=1.0 / D).then_inc(s["std"], 1)

            def act_store(st, n):
                act.wait_ge(s["out_turned"], n["out_turned"] + 1)
                copy(x_out[:, :, :], ps[:, 4:8, :].rearrange("p (t b) n -> p t (b n)", t=ST)).then_inc(s["out_ready"], 1)

            for st in steps:
                {"init": act_init, "ln": act_ln, "ln_last": act_ln, "ffn": act_ffn, "mla": act_mla, "diff": act_diff, "ssm": act_ssm,
                 "pre": act_pre, "post": act_post, "hyb": act_hyb, "mem": act_mem, "xatt": act_xatt,
                 "store": act_store}[st.kind](st, st.n)

        @block.vector
        def _(dve):
            step = [0]

            def link(ins):
                step[0] += 1
                ins.then_inc(dve_step, 1)
                dve.wait_ge(dve_step, step[0])

            tt, ts, stt = nc.vector.tensor_tensor, nc.vector.tensor_scalar, nc.vector.scalar_tensor_tensor

            def convert(b, it=None):
                if b >= NB:
                    return
                for h in range(2):
                    v = 2 * b + h + 1
                    dve.wait_ge(w_hi, v if it is None else 8 * it + v)
                    r = slice(h * HALF, (h + 1) * HALF)
                    tt(wlo[b % 2][:, r], raw[b % RAW][:, r], whi[b % 2][:, r].bitcast(F32), ALU.subtract).then_inc(w_lo, 1)

            def coefficients(sub, n):
                dve.wait_ge(s["mod_sum"], n["mod_sum"] + 1)
                if sub < SUB * DEPTH:
                    i, j = divmod(sub, SUB)
                    link(tt(modc[:, :], ps[:, 6, 0:24], vcol(72 * i + 24 * j, 24), ALU.add))
                    link(ts(t8[:, 0, :], modc[:, 8:16], 1.0, None, ALU.add))
                    if sub:
                        g, b = vcol(LNG + 8 * (sub - 1), 8), vcol(LNB + 8 * (sub - 1), 8)
                        tt(G1[:, :], t8[:, 0, :], g, ALU.mult)
                        link(tt(t8[:, 1, :], t8[:, 0, :], b, ALU.mult))
                        tt(B1[:, :], t8[:, 1, :], modc[:, 0:8], ALU.add)
                        ts(G2[:, :], g, ALPHA, None, ALU.mult)
                        ts(B2[:, :], b, ALPHA, None, ALU.mult)
                    else:
                        nc.vector.tensor_copy(G1[:, :], t8[:, 0, :])
                        nc.vector.tensor_copy(B1[:, :], modc[:, 0:8])
                        nc.vector.memset(G2[:, :], ALPHA)
                        nc.vector.memset(B2[:, :], 0.0)
                    link(ts(gw[:, :], modc[:, 16:24], 1.0 if j == 1 else 0.5, None, ALU.mult))
                else:
                    nc.vector.tensor_copy(G2[:, :], vcol(LNG + 8 * (sub - 1), 8))
                    link(nc.vector.tensor_copy(B2[:, :], vcol(LNB + 8 * (sub - 1), 8)))

            def spread(n, last=False):
                for c in range(0 if last else DC):
                    i = ts(hf[:, c, :], z[:, c, :], G1[:, c:c + 1], B1[:, c:c + 1], ALU.mult, ALU.add)
                    if c % 2:
                        i.then_inc(s["hf"], 1)
                for q in range(0 if last else 4):
                    dve.wait_ge(s["h_hi"], n["h_hi"] + q + 1)
                    r = slice(2 * q, 2 * q + 2)
                    tt(H_lo[:, r, :], hf[:, r, :], H_hi[:, r, :].bitcast(F32), ALU.subtract).then_inc(s["h_lo"], 1)
                for c in range(DC):
                    i = ts(ax[:, c, :], z[:, c, :], G2[:, c:c + 1], B2[:, c:c + 1], ALU.mult, ALU.add)
                i.then_inc(s["ax_ready"], 1)

            def dve_init(st, n):
                dve.wait_ge(init_loaded, n_init)
                link(nc.vector.tensor_copy(ang[:, 2, :], posi[:, :]))
                link(ts(ang[:, 0, :], ang[:, 2, :], kc("misc", 0, 1), None, ALU.mult))
                magic = 1.5 * 2.0 ** 23
                link(ts(ang[:, 1, :], ang[:, 0, :], 1.0 / TWO_PI, magic, ALU.mult, ALU.add))
                link(ts(ang[:, 1, :], ang[:, 1, :], magic, None, ALU.subtract))
                c1, c2 = 6.28125, 0.0019350051879882812
                for c in (c1, c2, TWO_PI - c1 - c2):
                    link(stt(ang[:, 0, :], ang[:, 1, :], -c, ang[:, 0, :], ALU.mult, ALU.add))
                ts(ang[:, 0, :], ang[:, 0, :], 3.1415925, -3.1415925, ALU.min, ALU.max).then_inc(s["angle"], 1)
                for i in range(2):
                    r = slice(64 * i, 64 * i + 64)
                    nc.vector.tensor_copy(dskip[r, :], skiprow[r, :].rearrange("p (c i) -> p c i", i=2)[:, :, i])
                lam_init = 0.8 - 0.6 * math.exp(-0.3 * 1)
                link(tt(lamrow[:, 0:2, :], lamrow[:, 0:2, :], lamrow[:, 2:4, :], ALU.mult))
                nc.vector.tensor_reduce(tiny[:, 4:6], lamrow[:, 0:2, :], AX, ALU.add).then_inc(s["lam_sum"], 1)
                dve.wait_ge(s["lam_exp"], 1)
                link(tt(tiny[:, 2:3], tiny[:, 7:8], tiny[:, 6:7], ALU.subtract))
                ts(tiny[:, 0:1], tiny[:, 2:3], lam_init, None, ALU.subtract)
                dve.wait_ge(s["vec_ready"], 3)
                ts(tiny[:, 1:2], vcol(column("diff_subln_g")), 1.0 - lam_init, None, ALU.mult)
                dve.wait_ge(s["cond_ready"], 1)
                for k in range(DC):
                    for half in range(2):
                        dve.wait_ge(mod_loaded[half], 16 * (k + 1))
                        w = mod_w[:, half, :]
                        if k == 0:
                            ts(mod_acc[:, half, :], w, cond[:, 0:1], None, ALU.mult).then_inc(mod_used, 1)
                            continue
                        dve.wait_ge(mod_used, 2 * k + half - 1)
                        stt(mod_acc[:, half, :], w, cond[:, k:k + 1], mod_acc[:, half, :], ALU.mult, ALU.add).then_inc(mod_used, 1)
                convert(0)
                convert(1)
                coefficients(0, n)
                dve.wait_ge(s["z_in"], 1)
                spread(n)

            def dve_ln(st, n):
                sub = st.args[0]
                g = steps[steps.index(st) - 1].lin["out"]
                for c in range(DC):
                    if c % 4 == 0:
                        if c == 0:
                            dve.wait_ge(s["ax_ready"], n["ax_ready"])
                        dve.wait_ge(products, g.l + 2 * (g.n - 1) + 2 + c // 4)
                    stt(z[:, c, :], ybank(g, c), gw[:, c:c + 1], ax[:, c, :], ALU.mult, ALU.add).then_inc(s["z_ready"], 1)
                dve.wait_ge(s["ln_sum"], n["ln_sum"] + 1)
                dve.wait_ge(s["z_ready"], n["z_ready"] + DC)
                mean = ps[:, 4, 0:S].unsqueeze(1).to_broadcast([P, 4, S])
                for h in range(2):
                    r = slice(4 * h, 4 * h + 4)
                    stt(z[:, r, :], mean, -1.0 / D, z[:, r, :], ALU.mult, ALU.add).then_inc(s["centred"], 1)
                coefficients(sub + 1, n)
                dve.wait_ge(s["std"], n["std"] + 1)
                link(nc.vector.reciprocal(std[:, 1, :], std[:, 0, :]))
                rstd = std[:, 1, :].unsqueeze(1).to_broadcast([P, 4, S])
                dve.wait_ge(s["centred"], n["centred"] + 2)
                for h in range(2):
                    r = slice(4 * h, 4 * h + 4)
                    link(tt(z[:, r, :], z[:, r, :], rstd, ALU.mult))
                spread(n, st.kind == "ln_last")

            def dve_ffn(st, n):
                g = st.lin["in"]

                def product(j, it=None):
                    p = g.p + 2 * j + 1
                    v = plan.free_val[p - 1]
                    dve.wait_ge(banks_free[(p - 1) % 2], v if it is None else 2 * it + v)
                    u = g.l + 4 * (j + 1)
                    dve.wait_ge(products, u if it is None else 8 * it + u)
                    tt(am[:, j % 2], sg[:, j % 2], ps[:, bank(p):bank(p) + 2, 0:S], ALU.mult).then_inc(banks_free[p % 2], 1)

                def product_lo(j, it=None):
                    v = n["a_hi"] + j + 1
                    dve.wait_ge(s["a_hi"], v if it is None else 2 * it + v)
                    r = slice(2 * j, 2 * j + 2) if it is None else ds(it * 4 + 2 * j, 2)
                    tt(A_lo[:, r, :], am[:, j % 2], A_hi[:, r, :].bitcast(F32), ALU.subtract).then_inc(s["a_lo"], 1)

                def turn(i, it=None):
                    convert(g.b + i + 2, it)
                    if i % 2 == 1:
                        product(i // 2, it)
                    if i % 2 == 0 and i >= 2:
                        product_lo(i // 2 - 1, it)

                walk(dve, g, turn)
                product_lo(FP - 1)
                projected(st)

            def projected(st):
                g = st.lin["out"]
                walk(dve, g, lambda i, it: convert(g.b + i + 2, it), 1, 2)

            def attend(n, heads, scale, kind):
                maps = 2 if kind == "diff" else 1
                full = kind == "xatt"
                width = 512 if full else CW
                tiles = ((0, S), (S, 2 * S)) if full else ((0, P), (P, CW))

                def maxima(h):
                    b = h % 2
                    dve.wait_ge(s["scores"], n["scores"] + h + 1)
                    if h >= 2:
                        dve.wait_ge(s["turned"], n["turned"] + h - 1)
                    if full:
                        link(nc.vector.tensor_reduce(stat[:, b, 0:2], ps[:, 4 + b, :].rearrange("p (t k) -> p t k", t=2), AX, ALU.max))
                    else:
                        for m in range(maps):
                            src = ps[:, 4 + (m if maps == 2 else b), 0:CW]
                            mask = kc("causal") if kind != "dilated" else kc2("dil_add")
                            link(tt(prob[:, b, m * CW:(m + 1) * CW], src, mask, ALU.add))
                        for m in range(maps):
                            for t, (x, y) in enumerate(tiles):
                                i = nc.vector.tensor_reduce(stat[:, b, 2 * m + t:2 * m + t + 1], prob[:, b, m * CW + x:m * CW + y], AX, ALU.max)
                        link(i)
                    ts(stat[:, b, 4:4 + 2 * maps], stat[:, b, 0:2 * maps], -scale, None, ALU.mult).then_inc(s["maxed"], 1)

                def normal(h):
                    b = h % 2
                    dve.wait_ge(s["exped"], n["exped"] + h + 1)
                    if kind == "dilated":
                        for t, (x, y) in enumerate(tiles):
                            i = stt(prob[:, b, x:y], prob[:, b, x:y], 1.0, kc2("dil_times", x, y), ALU.mult, ALU.mult,
                                    accum_out=stat[:, b, 8 + t:9 + t])
                            link(i)
                    link(nc.vector.reciprocal(stat[:, b, 12:12 + 2 * maps], stat[:, b, 8:8 + 2 * maps]))
                    if kind == "diff":
                        link(ts(stat[:, b, 14:16], stat[:, b, 14:16], tiny[:, 0:1], None, ALU.mult))
                    for t, (x, y) in enumerate(tiles):
                        i = ts(prob[:, b, x:y], prob[:, b, x:y], stat[:, b, 12 + t:13 + t], None, ALU.mult)
                    if kind == "diff":
                        link(i)
                        for t, (x, y) in enumerate(tiles):
                            i = stt(prob[:, b, x:y], prob[:, b, CW + x:CW + y], stat[:, b, 14 + t:15 + t], prob[:, b, x:y],
                                    ALU.mult, ALU.add)
                    i.then_inc(s["probs"], 1)

                def output(h):
                    if kind in ("mla", "xatt"):
                        dve.wait_ge(s["mixed_hi"], n["mixed_hi"] + h + 1)
                        if kind == "xatt":
                            r = slice(2 * h, 2 * h + 2)
                            tt(H_lo[:, r, :], ps[:, 7, :].rearrange("p (c n) -> p c n", c=2), H_hi[:, r, :].bitcast(F32), ALU.subtract)\
                                .then_inc(s["mixed_out"], 1)
                        else:
                            tt(H_lo[:, h, :], ps[:, 7, 0:S], H_hi[:, h, :].bitcast(F32), ALU.subtract).then_inc(s["mixed_out"], 1)
                        return
                    dve.wait_ge(s["mixed"], n["mixed"] + h + 1)
                    if kind == "diff":
                        nc.vector.tensor_copy(O1[:, h, :], ps[:, 7, 0:S]).then_inc(s["mixed_out"], 1)
                    else:
                        r = slice(64 * (h % 2), 64 * (h % 2) + 64)
                        nc.vector.tensor_copy(O1[r, h // 2, :], ps[r, 7, 0:S]).then_inc(s["mixed_out"], 1)

                for i in range(heads + 3):
                    if i < heads:
                        maxima(i)
                    if 1 <= i <= heads:
                        normal(i - 1)
                    if i >= 3:
                        output(i - 3)

            def dve_mla(st, n):
                splits(st.lin["latent"])
                idx = st.args[0] // 9
                dve.wait_ge(s["lat_std"], n["lat_std"] + 1)
                link(nc.vector.reciprocal(std[:, :, :], std[:, :, :]))
                for c in range(5):
                    g = vcol(column("mla_q_norm_g", 3 * idx + c)) if c < 3 else vcol(column("mla_kv_norm_g", 2 * idx + c - 3))
                    i = stt(latn[:, c, :], lat[:, c, :], g, std[:, c // 3, :], ALU.mult, ALU.mult)
                    if c in (2, 4):
                        i.then_inc(s["lat_n"], 1)
                for i, (a, b) in enumerate(((0, 3), (3, 5))):
                    dve.wait_ge(s["lat_hi"], n["lat_hi"] + i + 1)
                    tt(A_lo[:, a:b, :], latn[:, a:b, :], A_hi[:, a:b, :].bitcast(F32), ALU.subtract).then_inc(s["lat_lo"], 1)
                dve.wait_ge(s["kr_rot"], n["kr_rot"] + 1)
                tt(rtmp[:, 0, 0, :], lat[:, 5, :], cosm[:, :], ALU.mult)
                link(tt(rtmp[:, 1, 0, :], ps[:, 5, 0:S], sinm[:, :], ALU.mult))
                tt(KRp[:, :], rtmp[:, 0, 0, :], rtmp[:, 1, 0, :], ALU.add).then_inc(s["kr_ready"], 1)
                splits(st.lin["q"])
                splits(st.lin["kv"])
                cos2 = cosm[:, :].unsqueeze(1).to_broadcast([P, 2, S])
                sin2 = sinm[:, :].unsqueeze(1).to_broadcast([P, 2, S])
                dve.wait_ge(s["kr_ready"], n["kr_ready"] + 1)
                for i in range(2):
                    dve.wait_ge(s["qr_rot"], n["qr_rot"] + i + 1)
                    if i:
                        dve.wait_ge(s["qr_ready"], n["qr_ready"] + i)
                    tt(rtmp[:, 0], QRp[:, 2 * i:2 * i + 2, :], cos2, ALU.mult)
                    link(tt(rtmp[:, 1], ps[:, 4 + i, :].rearrange("p (c n) -> p c n", c=2), sin2, ALU.mult))
                    tt(QRp[:, 2 * i:2 * i + 2, :], rtmp[:, 0], rtmp[:, 1], ALU.add).then_inc(s["qr_ready"], 1)
                attend(n, MLA_H, 192.0 ** -0.5, "mla")
                projected(st)

            def splits(g):
                for i in range(g.n):
                    convert(g.b + i + 2)

            def fin_lows(n):
                for i in range(4):
                    dve.wait_ge(s["fin_hi"], n["fin_hi"] + i + 1)
                    r = slice(2 * i, 2 * i + 2)
                    tt(H_lo[:, r, :], O1[:, r, :], H_hi[:, r, :].bitcast(F32), ALU.subtract).then_inc(s["fin_lo"], 1)

            def dve_diff(st, n):
                splits(st.lin["qk"])
                splits(st.lin["v"])
                attend(n, 8, 64.0 ** -0.5, "diff")
                dve.wait_ge(s["mixed_out"], n["mixed_out"] + 8)
                for i in range(4):
                    dve.wait_ge(s["fin_std"], n["fin_std"] + i + 1)
                    r = slice(2 * i, 2 * i + 2)
                    link(nc.vector.reciprocal(z[:, r, :], z[:, r, :]))
                    stt(O1[:, r, :], O1[:, r, :], tiny[:, 1:2], z[:, r, :], ALU.mult, ALU.mult).then_inc(s["fin_n"], 1)
                fin_lows(n)
                projected(st)

            def dve_ssm(st, n):
                splits(st.lin["z"])
                g = st.lin["xbc"]
                for j in range(g.n):
                    convert(g.b + j + 2)
                    p = g.p + j
                    dve.wait_ge(products, g.l + (j + 1) * g.upb)
                    if j >= 2:
                        dve.wait_ge(s["conv_out"], n["conv_out"] + j - 1)
                    for d in range(4):
                        for c in range(2):
                            src, dst = ps[:, bank(p) + c, 0:S - d], conv[:, j % 2, c, d:S]
                            w = vcol(CONVW + 24 * (3 - d) + 2 * j + c)
                            if d == 0:
                                i = ts(dst, src, w, vcol(column("ssm_conv_b", 2 * j + c)), ALU.mult, ALU.add)
                            else:
                                i = stt(dst, src, w, dst, ALU.mult, ALU.add)
                            if d == 3 and c == 1:
                                i.then_inc(banks_free[p % 2], 1)
                            else:
                                step[0] += 1
                                i.then_inc(dve_step, 1)
                                if d or c:
                                    dve.wait_ge(dve_step, step[0] - 1)
                g = st.lin["dt"]
                convert(g.b + 2)
                dve.wait_ge(products, g.l + 1)
                dve.wait_ge(s["conv_out"], n["conv_out"] + 12)
                link(tt(dts[:, 0], ps[:, bank(g.p):bank(g.p) + 2, 0:SSM_H], dtb[:, :].unsqueeze(1).to_broadcast([P, 2, SSM_H]), ALU.add))
                ts(dts[:, 4], dts[:, 0], 0.0, None, ALU.max).then_inc(banks_free[g.p % 2], 1)
                nc.vector.memset(yt[:, 0, 0:1], 0.0).then_inc(s["dt_in"], 1)
                dve.wait_ge(s["dt_ln"], n["dt_ln"] + 1)
                dve.wait_ge(banks_free[g.p % 2], plan.free_val[g.p])
                link(tt(dts[:, 5], dts[:, 4], dts[:, 3], ALU.add))
                stt(dts[:, 6], dts[:, 5], -1.0, alog[:, :].unsqueeze(1).to_broadcast([P, 2, SSM_H]), ALU.mult, ALU.mult).then_inc(s["adt"], 1)
                dve.wait_ge(s["acum"], n["acum"] + 1)
                link(nc.vector.tensor_copy(dts[:, 7], ps[:, 5, 0:64].rearrange("p (t h) -> p t h", t=2)))
                for i in range(SSM_G):
                    dve.wait_ge(s["cb"], n["cb"] + i + 1)
                    tt(CB[:, i, :], ps[:, 6 + i % 2, 0:CW], tri3, ALU.mult).then_inc(s["cb_out"], 1)
                dve.wait_ge(s["cb_out"], n["cb_out"] + SSM_G)

                def decay(h):
                    dve.wait_ge(s["spread"], n["spread"] + h + 1)
                    if h >= 2:
                        dve.wait_ge(s["mixing"], n["mixing"] + h - 1)
                    src = ps[:, 4 + h % 2, 0:S]
                    ts(dec[:, h % 2, 0:S], src, dts[:, 7, 0, h:h + 1], 0.0, ALU.subtract, ALU.min)
                    ts(dec[:, h % 2, S:CW], src[:, P:S], dts[:, 7, 1, h:h + 1], 0.0, ALU.subtract, ALU.min).then_inc(s["dec"], 1)

                def mixing(h):
                    dve.wait_ge(s["dec_exp"], n["dec_exp"] + h + 1)
                    if h >= 2:
                        dve.wait_ge(s["ssd"], n["ssd"] + h - 1)
                    for t, (a, b) in enumerate(((0, S), (S, CW))):
                        i = stt(mixw[:, h % 2, a:b], dec[:, h % 2, a:b], dts[:, 5, t, h:h + 1], CB[:, h // 8, a:b], ALU.mult, ALU.mult)
                    i.then_inc(s["mixing"], 1)

                def output(c):
                    dve.wait_ge(s["ssd"], n["ssd"] + 2 * c + 2)
                    if c >= 2:
                        dve.wait_ge(s["y_out"], n["y_out"] + c - 1)
                    link(stt(yt[:, c % 2, :], XC[:, c, :], dskip[:, c:c + 1], ps[:, 6 + c % 2, 0:S], ALU.mult, ALU.add))
                    tt(Z[:, c, :], yt[:, c % 2, :], Z[:, c, :], ALU.mult).then_inc(s["y_out"], 1)

                for i in range(SSM_H + 3):
                    if i < SSM_H:
                        decay(i)
                    if 1 <= i <= SSM_H:
                        mixing(i - 1)
                    if i >= 3 and (i - 3) % 2:
                        output((i - 3) // 2)
                for i in range(4):
                    dve.wait_ge(s["fin_std"], n["fin_std"] + i + 1)
                    link(nc.vector.reciprocal(std[:, i % 2, :], std[:, i % 2, :]))
                    for c in range(4 * i, 4 * i + 4):
                        k = stt(Z[:, c, :], Z[:, c, :], vcol(column("ssm_norm_g", c)), std[:, i % 2, :], ALU.mult, ALU.mult)
                    k.then_inc(s["fin_n"], 1)
                    dve.wait_ge(s["fin_hi"], n["fin_hi"] + i + 1)
                    r = slice(4 * i, 4 * i + 4)
                    tt(A_lo[:, r, :], Z[:, r, :], A_hi[:, r, :].bitcast(F32), ALU.subtract).then_inc(s["fin_lo"], 1)
                projected(st)

            def dve_hyb(st, n):
                for g in list(st.lin.values())[:-1]:
                    splits(g)
                dve.wait_ge(second_loaded, 32)
                for i in range(8):
                    X = (QN, KN)[i // 2 % 2]
                    r = slice(4 * (i // 4) + 2 * (i % 2), 4 * (i // 4) + 2 * (i % 2) + 2)
                    cos, sin = (("cos_att", "sin_att"), ("cos_ret", "sin_ret"))[i // 4]
                    cos, sin = (kc2(k).unsqueeze(1).to_broadcast([P, 2, S]) for k in (cos, sin))
                    dve.wait_ge(s["rot"], n["rot"] + i + 1)
                    if i:
                        dve.wait_ge(s["rot_out"], n["rot_out"] + i)
                    tt(rtmp[:, 0], X[:, r, :], cos, ALU.mult)
                    link(tt(rtmp[:, 1], ps[:, 4 + i % 2, :].rearrange("p (c n) -> p c n", c=2), sin, ALU.mult))
                    tt(X[:, r, :], rtmp[:, 0], rtmp[:, 1], ALU.add).then_inc(s["rot_out"], 1)
                attend(n, 8, 64.0 ** -0.5, "dilated")
                for h in range(RET_H + 1):
                    if h < RET_H:
                        dve.wait_ge(s["kq"], n["kq"] + h + 1)
                        if h >= 2:
                            dve.wait_ge(s["ret"], n["ret"] + h - 1)
                        tt(prob[:, h % 2, 0:CW], ps[:, 4 + h % 2, 0:CW], kc2(f"decay{h}"), ALU.mult).then_inc(s["kq_out"], 1)
                    if h:
                        dve.wait_ge(s["ret"], n["ret"] + h)
                        nc.vector.tensor_copy(O1[:, 3 + h, :], ps[:, 7, 0:S]).then_inc(s["ret_out"], 1)
                dve.wait_ge(s["ret_out"], n["ret_out"] + RET_H)
                for i in range(2):
                    dve.wait_ge(s["fin_mean"], n["fin_mean"] + i + 1)
                    r = slice(4 + 2 * i, 6 + 2 * i)
                    stt(O1[:, r, :], ps[:, 4 + i, :].rearrange("p (c n) -> p c n", c=2), -1.0 / P, O1[:, r, :], ALU.mult, ALU.add)\
                        .then_inc(s["fin_cent"], 1)
                dve.wait_ge(s["fin_cent"], n["fin_cent"] + 2)
                for i in range(4):
                    dve.wait_ge(s["fin_std"], n["fin_std"] + i + 1)
                    link(nc.vector.reciprocal(z[:, 2 * i:2 * i + 2, :], z[:, 2 * i:2 * i + 2, :]))
                    for c in range(2 * i, 2 * i + 2):
                        gain = vcol(column("attn_gn_g_2", c)) if i < 2 else vcol(column("ret_gn_g_2", c - 4))
                        k = stt(O1[:, c, :], O1[:, c, :], gain, z[:, c, :], ALU.mult, ALU.mult)
                    if i >= 2:
                        link(k)
                        r = slice(2 * i, 2 * i + 2)
                        k = tt(O1[:, r, :], O1[:, r, :], RG[:, 2 * i - 4:2 * i - 2, :], ALU.mult)
                    k.then_inc(s["fin_n"], 1)
                fin_lows(n)
                projected(st)

            def dve_mem(st, n):
                dve.wait_ge(s["h_lo"], n["h_lo"])
                dve.wait_ge(s["mem_std"], n["mem_std"] + 1)
                link(nc.vector.reciprocal(tiny[:, 12:14], tiny[:, 10:12]))
                for t in range(ST):
                    i = ts(mem[:, t, :], mem[:, t, :], tiny[:, 12 + t:13 + t], None, ALU.mult)
                i.then_inc(s["mem_n"], 1)
                dve.wait_ge(s["mem_turned"], n["mem_turned"] + 1)
                for c in range(DC):
                    i = ts(hf[:, c, :], ps[:, 4 + c // 2, c % 2 * S:c % 2 * S + S], vcol(column("mem_norm_g_2", c)), None, ALU.mult)
                i.then_inc(s["mem_f"], 1)
                dve.wait_ge(s["mem_hi"], n["mem_hi"] + 1)
                tt(M_lo[:, :, :], hf[:, :, :], M_hi.bitcast(F32), ALU.subtract).then_inc(s["mem_lo"], 1)

            def dve_xatt(st, n):
                for g in list(st.lin.values())[:-1]:
                    splits(g)
                attend(n, XH, 256.0 ** -0.5, "xatt")
                projected(st)

            def dve_pre(st, n):
                dve.wait_ge(s["std"], n["std"] + 1)
                dve.wait_ge(s["ax_ready"], n["ax_ready"])
                link(nc.vector.reciprocal(std[:, 1, :], std[:, 0, :]))
                for c in range(DC):
                    i = stt(hf[:, c, :], ax[:, c, :], vcol(column(st.args[0], c)), std[:, 1, :], ALU.mult, ALU.mult)
                    if c % 2:
                        i.then_inc(s["hf"], 1)
                for q in range(4):
                    dve.wait_ge(s["h_hi"], n["h_hi"] + q + 1)
                    r = slice(2 * q, 2 * q + 2)
                    tt(H_lo[:, r, :], hf[:, r, :], H_hi[:, r, :].bitcast(F32), ALU.subtract).then_inc(s["h_lo"], 1)

            def dve_post(st, n):
                g = steps[steps.index(st) - 1].lin["out"]
                dve.wait_ge(s["std"], n["std"] + 1)
                link(nc.vector.reciprocal(std[:, 1, :], std[:, 0, :]))
                for c in range(DC):
                    i = stt(z[:, c, :], ybank(g, c), vcol(column(st.args[0], c)), std[:, 1, :], ALU.mult, ALU.mult)
                link(i)
                tt(ax[:, :, :], ax[:, :, :], z[:, :, :], ALU.add).then_inc(s["ax_ready"], 1)

            tri3 = kc("tri")
            for st in steps:
                if st.kind in ("store",):
                    continue
                {"init": dve_init, "ln": dve_ln, "ln_last": dve_ln, "ffn": dve_ffn, "mla": dve_mla, "diff": dve_diff, "ssm": dve_ssm,
                 "pre": dve_pre, "post": dve_post, "hyb": dve_hyb, "mem": dve_mem, "xatt": dve_xatt}[st.kind](st, st.n)

        @block.tensor
        def _(pe):
            def three(out, w, wo, wn, x_hi, x_lo, first, last, swap=False, rest=False):
                a, b = whi[w][:, wo:wo + wn] if isinstance(wn, int) else wn(whi[w]), None
                b = wlo[w][:, wo:wo + wn] if isinstance(wn, int) else wn(wlo[w])
                for i, (l, r) in enumerate(((a, x_hi), (a, x_lo), (b, x_hi))):
                    if swap:
                        l, r = r, l
                    m = pe.matmul(out, l, r, start=first and i == 0, stop=last and i == 2, skip_group_check=rest)
                return m

            def wait_banks(p, it=None):
                if plan.free_need[p] or it is not None:
                    v = plan.free_need[p]
                    pe.wait_ge(banks_free[p % 2], v if it is None else 2 * it + v)

            def wait_split(b, h, it=None):
                v = 2 * b + h + 1
                pe.wait_ge(w_lo, v if it is None else 8 * it + v)

            def columns(g, i, x_hi, x_lo, it=None, tokens=False, wait=None):
                b, p = g.b + i, g.p + i
                wait_banks(p, it)
                for h in range(2):
                    if wait:
                        pe.wait_ge(wait[0], wait[1] + 2 * h + 2)
                    wait_split(b, h, it)
                    for c in range(2):
                        for k in range(4 * h, 4 * h + 4):
                            o = ps[:, bank(p) + c, 0:S]
                            if tokens:
                                t = slice(c * P, c * P + P)
                                m = three(o, b % 2, k * 256, 256, x_hi[:, k, t], x_lo[:, k, t], k == 0, k == 7, swap=True)
                            else:
                                m = three(o, b % 2, k * 256 + c * P, P, x_hi[:, k, :], x_lo[:, k, :], k == 0, k == 7)
                    m.then_inc(products, 1)

            def project(st, x_hi, x_lo, ready, count, per):
                g = st.lin["out"]

                def turn(i, it=None):
                    b = g.b + i
                    if i == 0:
                        wait_banks(g.p)
                        wait_banks(g.p + 1)
                    for h in range(2):
                        k = 2 * i + h
                        if h == 0 or per == 1:
                            v = count + k // per + 1
                            pe.wait_ge(ready, v if it is None else 4 * it + v)
                        wait_split(b, h, it)
                        for c in range(DC):
                            if it is None:
                                xh, xl = x_hi[:, k, :], x_lo[:, k, :]
                            else:
                                xh, xl = (x[:, ds(it * 8 + k, 1), :].rearrange("p a n -> p (a n)") for x in (x_hi, x_lo))
                            last = it is None and k == 2 * g.n - 1
                            m = three(ybank(g, c), b % 2, h * HALF + c * P, P, xh, xl, k == 0 and c % 2 == 0, last, rest=True)
                            if last and c == 3:
                                m.then_inc(products, 1)
                        m.then_inc(products, 1)

                walk(pe, g, turn, 1, 2)

            def mod_sums():
                for half in range(2):
                    for c in range(12):
                        m = pe.matmul(ps[:, 6, 12 * half + c:12 * half + c + 1], mod_acc[:, half, c * P:c * P + P], ones[:, 0:1],
                                      start=True, stop=True)
                m.then_inc(s["mod_sum"], 1)

            def pe_init(st, n):
                pe.wait_ge(init_loaded, n_init)
                for i in range(DEPTH):
                    pe.transpose(ps[:, 0, 72 * i:72 * i + 72], rows[0:72, i, :], ident[0:72, 0:72])
                for i in range(2):
                    pe.transpose(ps[:, 1, 96 * i:96 * i + 96], rows[0:96, 4 + i, :], ident[0:96, 0:96])
                pe.transpose(ps[:, 1, 192:192 + NROWS], rows[0:NROWS, 6, :], ident[0:NROWS, 0:NROWS])
                pe.transpose(ps[:, 2, 0:96], rows[0:96, 7, :], ident[0:96, 0:96]).then_inc(s["vec_turned"], 1)
                for c in range(DC):
                    for t in range(ST):
                        m = pe.transpose(ps[:, 4 + c // 2, c % 2 * S + t * P:c % 2 * S + t * P + P], x_in[:, t, c * P:c * P + P], ident)
                m.then_inc(s["vec_turned"], 1)
                pe.wait_ge(mod_used, 16)
                pe.wait_ge(s["z_in"], 1)
                mod_sums()

            def sums(b, src, ready, count, per=1):
                for c in range(DC):
                    if c % per == 0:
                        pe.wait_ge(ready, count + c // per + 1)
                    m = pe.matmul(ps[:, b, 0:S], ones, src[:, c, :], start=c == 0, stop=c == DC - 1)
                return m

            def pe_ln(st, n):
                sums(4, z, s["z_ready"], n["z_ready"]).then_inc(s["ln_sum"], 1)
                if st.args[0] + 1 < min(plan.mods, SUB * DEPTH):
                    pe.wait_ge(mod_used, 16 * (st.args[0] + 2))
                    mod_sums()
                else:
                    pe.matmul(ps[:, 6, 0:1], ones, ones[:, 0:1], start=True, stop=True).then_inc(s["mod_sum"], 1)
                sums(5, sq, s["squared"], n["squared"], 2).then_inc(s["ln_var"], 1)

            def pe_ffn(st, n):
                g = st.lin["in"]
                walk(pe, g, lambda i, it: columns(g, i, H_hi, H_lo, it, wait=(s["h_lo"], n["h_lo"] - 4) if i == 0 else None))
                project(st, A_hi, A_lo, s["a_lo"], n["a_lo"], 2)

            def attend(n, heads, kind):
                full = kind == "xatt"

                def parts(h):
                    if kind == "mla":
                        r = slice(64 * (h % 2), 64 * (h % 2) + 64)
                        return [(4 + h % 2, [(QN[:, h, :], KN[:, h, :]), (QRp[r, h // 2, :], KRp[r, :])])]
                    if kind == "xatt":
                        return [(4 + h % 2, [(QN[:, 2 * h + c, :], KN[:, 2 * h + c, :]) for c in range(2)])]
                    if kind == "diff":
                        return [(4 + m, [(QN[64 * m:64 * m + 64, h, :], KN[64 * m:64 * m + 64, h, :])]) for m in range(2)]
                    r = slice(64 * (h % 2), 64 * (h % 2) + 64)
                    return [(4 + h % 2, [(QN[r, h // 2, :], KN[r, h // 2, :])])]

                def scores(h):
                    lag = 1 if kind == "diff" else 2
                    if h >= lag:
                        pe.wait_ge(s["exped"] if full else s["maxed"], (n["exped"] if full else n["maxed"]) + h - lag + 1)
                    for b, terms in parts(h):
                        for t in range(ST):
                            keys = S if full or t else P
                            o = S * t if full else P * t
                            for i, (q, k) in enumerate(terms):
                                m = pe.matmul(ps[:, b, o:o + keys], q[:, t * P:t * P + P], k[:, 0:keys],
                                              start=i == 0, stop=i == len(terms) - 1)
                    m.then_inc(s["scores"], 1)

                def turn(h):
                    pe.wait_ge(s["probs"], n["probs"] + h + 1)
                    if h:
                        pe.wait_ge(s["turned_out"], n["turned_out"] + h)
                    moves = ((0, 0), (128, 256), (256, 128), (384, 384)) if full else ((0, 0), (128, 128), (256, 256))
                    for a, b in moves:
                        m = pe.transpose(ps[:, 6, b:b + P], prob[:, h % 2, a:a + P], ident)
                    m.then_inc(s["turned"], 1)

                def mix(h):
                    pe.wait_ge(s["turned_out"], n["turned_out"] + h + 1)
                    if h:
                        pe.wait_ge(s["mixed_out"], n["mixed_out"] + h)
                    pt = probT[:, h % 2, :]
                    if full:
                        for c in range(2):
                            for t in range(ST):
                                m = pe.matmul(ps[:, 7, c * S:c * S + S], VT[:, t, (2 * h + c) * P:(2 * h + c + 1) * P],
                                              pt[:, t * S:t * S + S], start=t == 0, stop=t == 1)
                    else:
                        w, o = (64, 64 * (h % 2)) if kind == "dilated" else (P, 0)
                        for t in range(ST):
                            m = pe.matmul(ps[o:o + w, 7, t * P:S], VT[:, t, h * w:h * w + w], pt[:, t * S:S + t * P],
                                          start=t == 0, stop=t == 1, skip_group_check=True)
                    m.then_inc(s["mixed"], 1)

                for i in range(heads + 2):
                    if i < heads:
                        scores(i)
                    if 1 <= i <= heads:
                        turn(i - 1)
                    if i >= 2:
                        mix(i - 2)

            def pe_mla(st, n):
                g = st.lin["latent"]
                for i in range(3):
                    columns(g, i, H_hi, H_lo, wait=(s["h_lo"], n["h_lo"] - 4) if i == 0 else None)
                pe.wait_ge(s["lat_sq"], n["lat_sq"] + 3)
                for c in range(3):
                    pe.matmul(ps[:, 4, 0:S], ones, sq[:, c, :], start=c == 0, stop=c == 2)
                for c in range(3, 5):
                    m = pe.matmul(ps[:, 4, S:2 * S], ones, sq[:, c, :], start=c == 3, stop=c == 4)
                m.then_inc(s["lat_sum"], 1)
                pe.matmul(ps[:, 5, 0:S], kc("rot_mla"), lat[:, 5, :], start=True, stop=True).then_inc(s["kr_rot"], 1)
                g = st.lin["q"]
                pe.wait_ge(s["lat_lo"], n["lat_lo"] + 1)
                for j in range(g.n):
                    b, p = g.b + j, g.p + j
                    wait_banks(p)
                    wait_split(b, 1)
                    for c in range(3):
                        o = ps[:, bank(p) + c // 2, c % 2 * S:c % 2 * S + S]
                        for k in range(3):
                            m = three(o, b % 2, k * 384 + c * P, P, A_hi[:, k, :], A_lo[:, k, :], k == 0, k == 2)
                    m.then_inc(products, 1)
                g = st.lin["kv"]
                pe.wait_ge(s["lat_lo"], n["lat_lo"] + 2)
                for j in range(g.n):
                    b, p = g.b + j, g.p + 2 * j
                    wait_banks(p)
                    wait_split(b, 1)
                    for c in range(4):
                        o = ps[:, bank(p) + c // 2, c % 2 * S:c % 2 * S + S]
                        for k in range(2):
                            m = three(o, b % 2, k * HALF + c * 256, P, A_hi[:, 3 + k, :], A_lo[:, 3 + k, :], k == 0, k == 1)
                    m.then_inc(products, 1)
                    wait_banks(p + 1)
                    for t in range(ST):
                        for k in range(2):
                            def values(w, k=k):
                                return w[:, k * HALF:(k + 1) * HALF].rearrange("p (h n) -> p h n", h=4)[:, :, P:2 * P]
                            tok = slice(t * P, t * P + P)
                            m = three(ps[:, bank(p + 1) + t, :], b % 2, 0, values, A_hi[:, 3 + k, tok], A_lo[:, 3 + k, tok],
                                      k == 0, k == 1, swap=True)
                    m.then_inc(products, 1)
                for i in range(4):
                    p = st.lin["q"].p + i
                    pe.wait_ge(banks_free[p % 2], plan.free_val[p])
                pe.wait_ge(s["kr_ready"], n["kr_ready"] + 1)
                for i in range(2):
                    pe.matmul(ps[:, 4 + i, :], kc("rot_mla"), QRp[:, 2 * i:2 * i + 2, :], start=True, stop=True)\
                        .then_inc(s["qr_rot"], 1)
                pe.wait_ge(s["qr_ready"], n["qr_ready"] + 2)
                for i in range(4):
                    p = g.p + i
                    pe.wait_ge(banks_free[p % 2], plan.free_val[p])
                attend(n, MLA_H, "mla")
                project(st, H_hi, H_lo, s["mixed_out"], n["mixed_out"], 1)

            def read(g, pairs=1):
                for p in range(g.p, g.p + pairs * g.n)[-2:]:
                    pe.wait_ge(banks_free[p % 2], plan.free_val[p])

            def row(g, x_hi, x_lo, tokens=False, wait=None):
                for i in range(g.n):
                    columns(g, i, x_hi, x_lo, None, tokens, wait if i == 0 else None)

            def fin_sums(n, first=None):
                for i in range(4):
                    pe.wait_ge(s["fin_sq"], n["fin_sq"] + i + 1)
                    pe.matmul(ps[:, 4 + i, :], first if first is not None and i < 2 else ones, sq[:, 2 * i:2 * i + 2, :],
                              start=True, stop=True).then_inc(s["fin_sum"], 1)

            def pe_diff(st, n):
                row(st.lin["qk"], H_hi, H_lo, wait=(s["h_lo"], n["h_lo"] - 4))
                row(st.lin["v"], H_hi, H_lo, tokens=True)
                read(st.lin["v"])
                attend(n, 8, "diff")
                fin_sums(n)
                project(st, H_hi, H_lo, s["fin_lo"], n["fin_lo"], 2)

            def pe_ssm(st, n):
                L = st.lin
                row(L["z"], H_hi, H_lo, wait=(s["h_lo"], n["h_lo"] - 4))
                row(L["xbc"], H_hi, H_lo)
                g = L["dt"]
                wait_banks(g.p)
                wait_split(g.b, 0)
                for t in range(ST):
                    for k in range(DC):
                        tok = slice(t * P, t * P + P)
                        m = three(ps[:, bank(g.p) + t, 0:SSM_H], g.b % 2, k * SSM_H, SSM_H, H_hi[:, k, tok], H_lo[:, k, tok],
                                  k == 0, k == DC - 1, swap=True)
                wait_split(g.b, 1)
                m = pe.matmul(ps[:, 4, 0:1], ones, ones[:, 0:1], start=True, stop=True)
                m.then_inc(products, 1)
                pe.wait_ge(s["conv_out"], n["conv_out"] + 12)
                for q in range(8):
                    if q >= 2:
                        pe.wait_ge(s["x_out"], n["x_out"] + q - 1)
                    for c in range(4):
                        m = pe.transpose(ps[:, 4 + q % 2, c * P:c * P + P], XC[:, q % 4 * 4 + c, q // 4 * P:q // 4 * P + P], ident)
                    m.then_inc(s["x_turned"], 1)
                tri = kc("tri", 0, P)
                pe.wait_ge(s["adt"], n["adt"] + 1)
                pe.wait_ge(s["x_out"], n["x_out"] + 8)
                a0, a1 = dts[:, 6, 0, :], dts[:, 6, 1, :]
                pe.matmul(ps[0:SSM_H, 4, 0:P], a0, tri, start=True, stop=True)
                pe.matmul(ps[0:SSM_H, 4, P:S], a0, ones, start=True, stop=False)
                pe.matmul(ps[0:SSM_H, 4, P:S], a1, tri, start=False, stop=True)
                pe.matmul(ps[:, 5, 0:SSM_H], tri, a0, start=True, stop=True)
                pe.matmul(ps[:, 5, SSM_H:2 * SSM_H], ones, a0, start=True, stop=False)
                pe.matmul(ps[:, 5, SSM_H:2 * SSM_H], tri, a1, start=False, stop=True).then_inc(s["acum"], 1)
                for i in range(SSM_G):
                    if i >= 2:
                        pe.wait_ge(s["cb_out"], n["cb_out"] + i - 1)
                    pe.matmul(ps[:, 6 + i % 2, 0:S], Bm[:, i, 0:P], Cm[:, i, :], start=True, stop=True)
                    pe.matmul(ps[:, 6 + i % 2, S:CW], Bm[:, i, P:S], Cm[:, i, P:S], start=True, stop=True).then_inc(s["cb"], 1)

                def spread(h):
                    if h >= 2:
                        pe.wait_ge(s["dec"], n["dec"] + h - 1)
                    pe.matmul(ps[:, 4 + h % 2, 0:S], ident[0:SSM_H, h:h + 1].to_broadcast([SSM_H, P]), acT[:, :], start=True, stop=True)\
                        .then_inc(s["spread"], 1)

                def mix(h):
                    pe.wait_ge(s["mixing"], n["mixing"] + h + 1)
                    c, o = h // 2, 64 * (h % 2)
                    if c >= 2:
                        pe.wait_ge(s["y_out"], n["y_out"] + c - 1)
                    for t in range(ST):
                        m = pe.matmul(ps[o:o + 64, 6 + c % 2, t * P:S], XT[:, t, h * 64:h * 64 + 64],
                                      mixw[:, h % 2, t * S:t * P + S], start=t == 0, stop=t == 1, skip_group_check=True)
                    m.then_inc(s["ssd"], 1)

                pe.wait_ge(s["acum_t"], n["acum_t"] + 1)
                pe.wait_ge(s["cb_out"], n["cb_out"] + SSM_G)
                for i in range(SSM_H + 2):
                    if i < SSM_H:
                        spread(i)
                    if i >= 2:
                        mix(i - 2)
                for i in range(4):
                    pe.wait_ge(s["fin_sq"], n["fin_sq"] + i + 1)
                    if i >= 2:
                        pe.wait_ge(s["fin_std"], n["fin_std"] + i - 1)
                    for c in range(4):
                        m = pe.matmul(ps[:, 4 + i % 2, 0:S], ones, sqg[:, i % 2, c, :], start=c == 0, stop=c == 3)
                    m.then_inc(s["fin_sum"], 1)
                project(st, A_hi, A_lo, s["fin_lo"], n["fin_lo"], 4)

            def pe_hyb(st, n):
                L = st.lin
                row(L["aqk"], H_hi, H_lo, wait=(s["h_lo"], n["h_lo"] - 4))
                row(L["av"], H_hi, H_lo, tokens=True)
                row(L["rqk"], H_hi, H_lo)
                row(L["rv"], H_hi, H_lo, tokens=True)
                row(L["rg"], H_hi, H_lo)
                read(L["rg"])
                pe.wait_ge(second_loaded, 32)
                for i in range(8):
                    if i >= 2:
                        pe.wait_ge(s["rot_out"], n["rot_out"] + i - 1)
                    X = (QN, KN)[i // 2 % 2]
                    r = slice(4 * (i // 4) + 2 * (i % 2), 4 * (i // 4) + 2 * (i % 2) + 2)
                    pe.matmul(ps[:, 4 + i % 2, :], kc2(("rot_att", "rot_ret")[i // 4]), X[:, r, :], start=True, stop=True)\
                        .then_inc(s["rot"], 1)
                pe.wait_ge(s["rot_out"], n["rot_out"] + 8)
                attend(n, 8, "dilated")
                pe.wait_ge(s["mixed_out"], n["mixed_out"] + 8)
                for i in range(RET_H + 1):
                    if i < RET_H:
                        if i >= 2:
                            pe.wait_ge(s["kq_out"], n["kq_out"] + i - 1)
                        b = ps[:, 4 + i % 2, :]
                        pe.matmul(b[:, 0:S], KN[:, 4 + i, 0:P], QN[:, 4 + i, :], start=True, stop=True)
                        pe.matmul(b[:, S:CW], KN[:, 4 + i, P:S], QN[:, 4 + i, P:S], start=True, stop=True).then_inc(s["kq"], 1)
                    if i:
                        h = i - 1
                        pe.wait_ge(s["kq_out"], n["kq_out"] + h + 1)
                        if h:
                            pe.wait_ge(s["ret_out"], n["ret_out"] + h)
                        for t in range(ST):
                            m = pe.matmul(ps[:, 7, t * P:S], VT[:, t, 512 + h * P:640 + h * P], prob[:, h % 2, t * S:t * P + S],
                                          start=t == 0, stop=t == 1, skip_group_check=True)
                        m.then_inc(s["ret"], 1)
                pe.wait_ge(s["ret_out"], n["ret_out"] + RET_H)
                for i in range(2):
                    pe.matmul(ps[:, 4 + i, :], ones, O1[:, 4 + 2 * i:6 + 2 * i, :], start=True, stop=True).then_inc(s["fin_mean"], 1)
                pe.wait_ge(s["fin_cent"], n["fin_cent"] + 2)
                fin_sums(n, kc("half"))
                project(st, H_hi, H_lo, s["fin_lo"], n["fin_lo"], 2)

            def pe_mem(st, n):
                pe.wait_ge(s["mem_n"], n["mem_n"] + 1)
                for c in range(DC):
                    for t in range(ST):
                        m = pe.transpose(ps[:, 4 + c // 2, c % 2 * S + t * P:c % 2 * S + t * P + P], mem[:, t, c * P:c * P + P], ident)
                m.then_inc(s["mem_turned"], 1)

            def pe_xatt(st, n):
                L = st.lin
                row(L["q"], H_hi, H_lo, wait=(s["h_lo"], n["h_lo"] - 4))
                pe.wait_ge(s["mem_lo"], n["mem_lo"])
                row(L["k"], M_hi, M_lo)
                row(L["v"], M_hi, M_lo, tokens=True)
                read(L["v"])
                attend(n, XH, "xatt")
                project(st, H_hi, H_lo, s["mixed_out"], n["mixed_out"], 2)

            def pe_pre(st, n):
                sums(5, sq, s["squared"], n["squared"], 2).then_inc(s["x_sum"], 1)

            def pe_post(st, n):
                sums(5, sq, s["y_sq"], n["y_sq"], 4).then_inc(s["y_sum"], 1)

            def pe_store(st, n):
                pe.wait_ge(s["ax_ready"], n["ax_ready"])
                for t in range(ST):
                    for c in range(DC):
                        m = pe.transpose(ps[:, 4 + 2 * t + c // 4, c % 4 * P:c % 4 * P + P], ax[:, c, t * P:t * P + P], ident)
                m.then_inc(s["out_turned"], 1)

            for st in steps:
                {"init": pe_init, "ln": pe_ln, "ln_last": pe_ln, "ffn": pe_ffn, "mla": pe_mla, "diff": pe_diff, "ssm": pe_ssm,
                 "pre": pe_pre, "post": pe_post, "hyb": pe_hyb, "mem": pe_mem, "xatt": pe_xatt, "store": pe_store}[st.kind](st, st.n)


_INS = ["x", "c", "positions", "w_mod", "b_mod", "ln_g", "ln_b", "ffn_w_in", "ffn_w_out", "mla_w_in", "mla_q_norm_g",
        "mla_kv_norm_g", "mla_w_q_up", "mla_w_kv_up", "mla_w_out", "diff_w_in", "diff_lambda_q", "diff_lambda_k",
        "diff_subln_g", "diff_w_out", "ssm_w_in", "ssm_conv_w", "ssm_conv_b", "ssm_dt_bias", "ssm_a_log",
        "ssm_d_skip", "ssm_norm_g", "ssm_w_out", "mem_2", "pre_mix_g_2", "post_mix_g_2", "w_in_2", "attn_gn_g_2",
        "ret_gn_g_2", "w_out_2", "pre_mem_g_2", "post_mem_g_2", "mem_norm_g_2", "w_q_mem_2", "w_kv_mem_2",
        "w_o_mem_2", "pre_ffn_g_2", "post_ffn_g_2", "w_gate_up_2", "w_down_2"]


def schedule(A):
    def ffn(s):
        return ("ffn", s, A["ffn_w_in"][s // SUB, s % SUB // 2], A["ffn_w_out"][s // SUB, s % SUB // 2])

    todo = [("init",)]
    for i in range(DEPTH):
        s = SUB * i
        m = i // 3
        todo += [ffn(s), ("ln", s)]
        if i % 3 == 0:
            todo.append(("mla", s + 1, {"in": A["mla_w_in"][m], "q": A["mla_w_q_up"][m], "kv": A["mla_w_kv_up"][m], "out": A["mla_w_out"][m]}))
        else:
            k = ("", "diff", "ssm")[i % 3]
            todo.append((k, s + 1, {"in": A[k + "_w_in"][m], "out": A[k + "_w_out"][m]}))
        todo.append(("ln", s + 1))
        todo += [ffn(s + 2), ("ln" if i < DEPTH - 1 else "ln_last", s + 2)]
    todo += [("pre", "pre_mix_g_2"), ("hyb", {"in": A["w_in_2"][0], "out": A["w_out_2"][0]}), ("post", "post_mix_g_2"),
             ("pre", "pre_mem_g_2"), ("mem",), ("xatt", {"q": A["w_q_mem_2"][0], "kv": A["w_kv_mem_2"][0], "out": A["w_o_mem_2"][0]}),
             ("post", "post_mem_g_2"), ("pre", "pre_ffn_g_2"), ("ffn", SUB * DEPTH, A["w_gate_up_2"][0], A["w_down_2"][0]),
             ("post", "post_ffn_g_2")]
    return todo + [("store",)]


def kernel(**inputs):
    import concourse.bacc as _bacc
    from concourse.bass_utils import run_bass_kernel_spmd as _run

    nc = _bacc.Bacc("TRN2", target_bir_lowering=False, num_devices=1)
    arrays, A = {}, {}
    for name in _INS:
        a = np.ascontiguousarray(inputs[name])
        arrays[f"in_{name}_dram"] = a
        A[name] = nc.dram_tensor(f"in_{name}_dram", a.shape, mybir.dt.from_np(a.dtype), kind="ExternalInput").ap()
    out = nc.dram_tensor("out_0_dram", (1, S, D), F32, kind="ExternalOutput").ap()
    (first, at1), (second, at2) = constants()
    plan = Plan(schedule(A))
    program(nc, plan, A, out, (nc.inline_tensor(first, name="constants_first").ap(), at1, first.shape[1]),
            (nc.inline_tensor(second, name="constants_second").ap(), at2, second.shape[1]))
    r = _run(nc, [arrays], core_ids=[0])
    return r.results[0]["out_0_dram"]
```

```python
import math
from contextlib import ExitStack

import numpy as np

import concourse.bass as bass
from concourse import mybir

F32 = mybir.dt.float32
F32R = mybir.dt.float32r
I32 = mybir.dt.int32
ACT = mybir.ActivationFunctionType
ALU = mybir.AluOpType
AX = mybir.AxisListType.X
ds = bass.ds

P = 128
D = 1024
DC = D // P
S = 256
ST = S // P
DEPTH = 4
SUB = 3
F = 2816
FC = F // P
FP = F // 256
LN_EPS, RMS_EPS = 1e-5, 1e-6
ALPHA = (2.0 * DEPTH) ** 0.25
NEG = -1e30
HALF = 1024
SLOT = 2 * HALF
RAW = 4
CW = P + S
MODU = 3 * D // 2
TWO_PI = 2 * math.pi

MLA_H, MLA_ROPE, QR, KVR = 8, 64, 384, 256
SSM_H, SSM_G, SSM_INNER = 32, 4, 2048
XH = 4
RET_H = 4


def constants():
    i = np.arange(P)
    c = {}
    c["ident"] = np.eye(P)
    c["ones"] = np.ones((P, P))
    c["half"] = (i[:, None] // 64 == i[None, :] // 64).astype(float)
    tri = (i[:, None] <= i[None, :]).astype(float)
    c["tri"] = np.concatenate([tri, np.ones((P, P)), tri], 1)
    low = np.where(i[None, :] <= i[:, None], 0.0, NEG)
    c["causal"] = np.concatenate([low, np.zeros((P, P)), low], 1)

    def rotation(width, half):
        m = np.zeros((P, P))
        for f in range(P):
            g, r = f // width * width, f % width
            if r < half:
                m[g + r + half, f] = -1.0
            elif r < 2 * half:
                m[g + r - half, f] = 1.0
        return m

    c["rot_mla"] = rotation(64, 32)
    inv = np.float32(10000.0) ** (-np.arange(0, MLA_ROPE, 2, dtype=np.float32) / np.float32(MLA_ROPE))
    c["misc"] = np.zeros((P, 8))
    c["misc"][:, 0] = inv[i % 32]
    c["misc"][:, 1] = LN_EPS
    c["misc"][:, 2] = RMS_EPS
    c["misc"][:, 3] = math.pi / 2
    c["misc"][:, 4] = 1.0
    first = list(c)

    c["rot_att"] = rotation(64, 8)
    c["rot_ret"] = rotation(128, 64)
    pos = np.arange(S, dtype=np.float32)

    def tables(width, rot, theta):
        half = rot // 2
        inv = np.float32(theta) ** (-(np.arange(0, rot, 2, dtype=np.float32) / np.float32(rot)))
        cos, sin = np.ones((P, S)), np.zeros((P, S))
        for f in range(P):
            r = f % width
            if r < rot:
                ang = pos * inv[r % half]
                cos[f], sin[f] = np.cos(ang.astype(np.float64)), np.sin(ang.astype(np.float64))
        return cos, sin

    c["cos_att"], c["sin_att"] = tables(64, 16, 500000.0)
    c["cos_ret"], c["sin_ret"] = tables(128, 128, 10000.0)

    def causal_table(fn):
        q, k = i[:, None], i[None, :]
        return np.concatenate([fn(q, k), fn(q + P, k), fn(q + P, k + P)], 1)

    def seen(q, k):
        d = q - k
        return (d >= 0) * ((d <= 128).astype(float) + (d % 4 == 0) + (d % 16 == 0))

    times = causal_table(seen)
    c["dil_add"] = np.where(times > 0, 0.0, NEG)
    c["dil_times"] = times
    for h in range(RET_H):
        g = np.log1p(-(2.0 ** (-5.0 - h)))

        def decay(k, q, g=g):
            return np.where(q >= k, np.exp(g * np.maximum(q - k, 0)), 0.0) * 128.0 ** -0.5
        k, q = i[:, None], np.arange(S)[None, :]
        c[f"decay{h}"] = np.concatenate([decay(k, q), decay(k + P, q[:, P:])], 1)
    second = [k for k in c if k not in first]

    def pack(names):
        at, o = {}, 0
        for k in names:
            at[k] = (o, c[k].shape[1])
            o += c[k].shape[1]
        return np.concatenate([c[k] for k in names], 1).astype(np.float32), at

    return pack(first), pack(second)


ROWS = (("mla_q_norm_g", 6), ("mla_kv_norm_g", 4), ("diff_subln_g", 1), ("ssm_conv_b", 24), ("ssm_norm_g", 16),
        ("attn_gn_g_2", 4), ("ret_gn_g_2", 4), ("pre_mix_g_2", 8), ("post_mix_g_2", 8), ("pre_mem_g_2", 8),
        ("post_mem_g_2", 8), ("mem_norm_g_2", 8), ("pre_ffn_g_2", 8), ("post_ffn_g_2", 8))
NROWS = sum(r for _, r in ROWS)
LNG, LNB, MISC = 288, 384, 480
CONVW = MISC + NROWS
VCOLS = CONVW + 96


def column(name, at=0):
    o = MISC
    for k, r in ROWS:
        if k == name:
            return o + at
        o += r


ATT = ("scores", "maxed", "exped", "probs", "turned", "turned_out", "mixed", "mixed_out")
SIGNALS = {
    "init": dict(c_turned=1, vec_turned=2, vec_ready=3, cond_ready=1, z_in=1, mod_sum=2, angle=1, rope_sin=2, lam_sum=1, lam_exp=1, hf=4, h_hi=4, h_lo=4, ax_ready=1),
    "ffn": dict(a_hi=FP, a_lo=FP),
    "ln": dict(z_ready=8, zsum=7, folded=1, ln_sum=1, centred=4, squared=4, ln_var=1, std=1, mod_sum=2, hf=4, h_hi=4, h_lo=4, ax_ready=1),
    "mla": dict(lat_sq=3, lat_sum=1, kr_rot=1, lat_std=1, lat_n=2, lat_hi=2, lat_lo=2, kr_ready=1, qr_rot=2, qr_ready=2, mixed_hi=MLA_H,
                **{k: MLA_H for k in ATT}),
    "diff": dict(fin_sq=4, fin_sum=4, fin_std=4, fin_n=4, fin_hi=4, fin_lo=4, **{k: 8 for k in ATT}),
    "ssm": dict(conv_out=12, x_turned=8, x_out=8, dt_in=1, dt_ln=1, adt=1, acum=1, acum_t=1, cb=4, cb_out=4, spread=SSM_H,
                dec=SSM_H, dec_exp=SSM_H, mixing=SSM_H, ssd=SSM_H, y_out=SSM_H // 2,
                fin_sq=4, fin_sum=4, fin_std=4, fin_n=4, fin_hi=4, fin_lo=4),
    "ln_last": dict(z_ready=8, zsum=7, folded=1, ln_sum=1, centred=4, squared=4, ln_var=1, std=1, ax_ready=1),
    "pre": dict(folded=1, squared=4, x_sum=1, std=1, hf=4, h_hi=4, h_lo=4),
    "post": dict(folded=1, y_sq=4, y_sum=1, std=1, ax_ready=4),
    "hyb": dict(rot=8, rot_out=8, kq=4, kq_out=4, ret=4, ret_out=4, fin_mean=2, fin_cent=2,
                fin_sq=4, fin_sum=4, fin_std=4, fin_n=4, fin_hi=4, fin_lo=4, **{k: 8 for k in ATT}),
    "mem": dict(mem_std=1, mem_n=1),
    "xatt": dict(mem_turned=1, mem_f=1, mem_hi=1, mem_lo=1, mixed_hi=XH, **{k: XH for k in ATT}),
    "store": dict(out_turned=1, out_ready=1),
}


class Step:
    def __init__(self, kind, args, n):
        self.kind, self.args = kind, args
        self.n = n
        self.lin = {}


class Linear:
    def __init__(self, n, b, l, p, upb):
        self.n, self.b, self.l, self.p, self.upb = n, b, l, p, upb


class Plan:
    def __init__(self, steps):
        self.steps, self.total = [], {}
        self.mods = SUB * DEPTH
        self.blocks = []
        self.used = []
        self.load_at = []
        self.slot = [0] * RAW
        self.lin = 0
        self.free_need, self.free_val = [], []
        self.free = [0, 0]
        for name, *args in steps:
            st = Step(name, args, {k: self.total.get(k, 0) for k in SEMS})
            {"ffn": self.plan_ffn, "mla": self.plan_mla, "diff": self.plan_diff, "ssm": self.plan_ssm, "hyb": self.plan_hyb,
             "xatt": self.plan_xatt}.get(name, self.plan_none)(st, *args)
            for k, v in SIGNALS[name].items():
                self.total[k] = self.total.get(k, 0) + v
            self.steps.append(st)

    def pair(self, explicit=True):
        p = len(self.free_need)
        self.free_need.append(self.free[p % 2])
        self.free[p % 2] += explicit
        self.free_val.append(self.free[p % 2])
        return p

    def block(self, loads, units):
        b = len(self.blocks)
        self.blocks.append(loads)
        self.slot[b % RAW] += 16 * len(loads)
        self.load_at.append(self.slot[b % RAW])
        self.used.append((self.lin + units[0], self.lin + units[1]))
        self.lin += units[-1]
        return b

    def linear(self, st, name, loads, units=(1, 2), pairs=1):
        g = Linear(len(loads), len(self.blocks), self.lin, len(self.free_need), units[-1])
        for x in loads:
            self.block(x, units)
            for _ in range(pairs):
                self.pair()
        st.lin[name] = g
        return g

    def project(self, st, w, k):
        n = k // 2
        g = Linear(n, len(self.blocks), self.lin, len(self.free_need), 2)
        for j in range(n):
            self.block([("out", w, j)], (1, 2) if j < n - 1 else (DC, DC))
        self.pair(False), self.pair(False)
        st.lin["out"] = g

    def plan_none(self, st, *args):
        pass

    def cols(self, st, name, w, lo, hi):
        self.linear(st, name, [[("cols", w, c)] for c in range(lo, hi, 256)])

    def plan_diff(self, st, s, w):
        self.cols(st, "qk", w["in"], 0, 2 * D)
        self.cols(st, "v", w["in"], 2 * D, 3 * D)
        self.project(st, w["out"], DC)

    def plan_ssm(self, st, s, w):
        self.cols(st, "z", w["in"], 0, SSM_INNER)
        self.cols(st, "xbc", w["in"], SSM_INNER, 2 * SSM_INNER + D)
        self.linear(st, "dt", [[("dt", w["in"], 2 * SSM_INNER + D)]], (1, 1))
        self.project(st, w["out"], SSM_INNER // P)

    def plan_hyb(self, st, w):
        for i, k in enumerate(("aqk", "av", "rqk", "rv", "rg")):
            lo, hi = (0, 1024, 1536, 2560, 3072)[i], (1024, 1536, 2560, 3072, 3584)[i]
            self.cols(st, k, w["in"], lo, hi)
        self.project(st, w["out"], DC)

    def plan_xatt(self, st, w):
        self.cols(st, "q", w["q"], 0, D)
        self.cols(st, "k", w["kv"], 0, D)
        self.cols(st, "v", w["kv"], D, 2 * D)
        self.project(st, w["out"], DC)

    def plan_ffn(self, st, s, w_in, w_out):
        self.linear(st, "in", [[("cols", w_in, (j % 2) * F + (j // 2) * 256)] for j in range(2 * FP)])
        self.project(st, w_out, FC)

    def plan_mla(self, st, s, w):
        self.linear(st, "latent", [[("cols", w["in"], 0)], [("cols", w["in"], 256)],
                                   [("part", w["in"], 512, 0, 192), ("part", w["in"], 640, 192, 64)]])
        self.linear(st, "q", [[("q_up", w["q"], h, k) for k in range(3)] + [("q_up_rope", w["q"], h, k) for k in range(3)]
                              for h in range(0, MLA_H, 2)], (1, 1))
        self.linear(st, "kv", [[("rows2", w["kv"], h)] for h in range(0, MLA_H, 4)], (2, 2), pairs=2)
        self.project(st, w["out"], DC)


SEMS = sorted({k for v in SIGNALS.values() for k in v})


def walk(eng, g, turn, first=2, last=0):
    rounds = (g.n - first - last) // 4
    if rounds < 2:
        first, rounds = g.n, 0
    elif not last:
        first = g.n - 4 * rounds
    for i in range(first):
        turn(i, None)
    if rounds:
        with eng.Fori(0, rounds) as it:
            for i in range(first, first + 4):
                turn(i, it)
        for i in range(first + 4 * rounds, g.n):
            turn(i, None)


def program(nc, plan, A, out, first, second):
    steps = plan.steps
    NB = len(plan.blocks)
    ctx = ExitStack()
    with ctx:
        def sem(name):
            return ctx.enter_context(nc.semaphore(name))

        arena = ctx.enter_context(nc.sbuf_tensor("arena", [P, 53200], F32))
        base = 16512
        top = [base]

        def at(name, shape, offset, dt=F32):
            assert base <= offset and offset + 4 * int(np.prod(shape[1:])) <= base + 4 * 53200 - 64
            return nc.alloc_sbuf_tensor_at(name, shape, dt, offset=offset)

        def room(nbytes):
            o = top[0]
            top[0] += (nbytes + 31) // 32 * 32
            return o

        raw = [at(f"raw{i}", [P, SLOT], room(4 * SLOT)) for i in range(RAW)]
        whi = [at(f"whi{i}", [P, SLOT], room(4 * SLOT), F32R) for i in range(2)]
        wlo = [at(f"wlo{i}", [P, SLOT], room(4 * SLOT), F32R) for i in range(2)]
        o_ah, o_al, o_hh, o_hl = room(4 * FC * S), room(4 * FC * S), room(4 * DC * S), room(4 * DC * S)
        A_hi, A_lo = at("A_hi", [P, FC, S], o_ah, F32R), at("A_lo", [P, FC, S], o_al, F32R)
        H_hi, H_lo = at("H_hi", [P, DC, S], o_hh, F32R), at("H_lo", [P, DC, S], o_hl, F32R)
        ax = at("ax", [P, DC, S], room(4 * DC * S))
        o_z = room(4 * DC * S)
        z = at("z", [P, DC, S], o_z)
        o_hf = room(4 * DC * S)
        hf = at("hf", [P, DC, S], o_hf)
        o_s1 = room(4 * 16 * S)
        o_mod = room(4 * 2 * MODU)
        mod_w = at("mod_w", [P, 2, MODU], o_mod)
        crow = at("crow", [DC, P], room(4 * P))
        mod_first = [mod_w[:, 0, :], mod_w[:, 1, :]]
        mod_first += [at(f"mod_first{i}", [P, MODU], o)[:, :] for i, o in enumerate(
            (o_hh, o_hh + 4 * MODU, o_s1, o_s1 + 4 * MODU, o_ah + 4 * ST * D, o_ah + 4 * ST * D + 4 * MODU))]
        mod_acc = at("mod_acc", [P, 2, MODU], room(4 * 2 * MODU))
        K1 = at("K1", [P, first[2]], room(4 * first[2]))
        V = at("V", [P, VCOLS], room(4 * VCOLS))
        cond = at("cond", [P, DC], room(32))
        modc = at("modc", [P, 24], room(96))
        G1, B1, G2, B2, gw = (at(k, [P, DC], room(32)) for k in ("G1", "B1", "G2", "B2", "gw"))
        t8 = at("t8", [P, 2, DC], room(64))
        std = at("std", [P, 2, S], room(8 * S))
        cosm, sinm = at("cosm", [P, S], room(4 * S)), at("sinm", [P, S], room(4 * S))
        tiny = at("tiny", [P, 64], room(256))
        acc = at("acc", [P, 3, S], room(12 * S))
        pool_tick = at("pool_tick", [P, 16], room(64))

        sq = at("sq", [P, DC, S], o_s1 + 4 * DC * S)
        sg = at("sg", [P, 2, 2, S], o_s1)
        am = at("am", [P, 2, 2, S], o_s1 + 16 * S)
        rows = at("rows", [P, 8, P], o_al)
        x_in = at("x_in", [P, ST, D], o_ah)
        x_out = at("x_out", [P, ST, D], o_s1)
        posi = at("posi", [P, S], o_al + 8192, I32)
        ang = at("ang", [P, 3, S], o_al + 12288)
        lat = at("lat", [P, 6, S], o_s1)
        latn = at("latn", [P, 5, S], o_hf)
        QN = at("QN", [P, DC, S], o_ah + 20 * S)
        QRp = at("QRp", [P, 4, S], o_ah + 52 * S)
        KRp = at("KRp", [P, S], o_ah + 68 * S)
        KN = at("KN", [P, DC, S], o_al + 20 * S)
        VT = at("VT", [P, ST, D], o_al + 52 * S)
        rtmp = at("rtmp", [P, 2, 2, S], o_s1 + 4 * 8 * S)
        prob = at("prob", [P, 4, HALF], o_z)
        probT = at("probT", [P, 2, 512], o_s1 + 4 * 12 * S)
        stat = at("stat", [P, 4, 16], room(256))
        sqj = at("sqj", [P, D], o_s1 + 4 * DC * S)
        O1 = at("O1", [P, DC, S], o_s1)
        zr = at("zr", [P, DC, S], o_z, F32R)
        M_hi, M_lo = A_hi[:, 14:22, :], zr
        RG = at("RG", [P, 4, S], o_ah)
        Z = at("Z", [P, 16, S], o_s1)
        XC, XT = at("XC", [P, 16, S], o_ah), at("XT", [P, ST, SSM_INNER], o_al)
        Bm, Cm = at("Bm", [P, 4, S], o_ah + 64 * S), at("Cm", [P, 4, S], o_al + 64 * S)
        CB = at("CB", [P, SSM_G, CW], o_hh)
        dec, mixw = at("dec", [P, 2, CW], o_hl), at("mixw", [P, 2, CW], o_hl + 8 * CW)
        conv = at("conv", [P, 2, 2, S], o_hf)
        yt = at("yt", [P, 2, S], o_hf)
        dts = at("dts", [P, 8, 2, SSM_H], o_hf + 16 * S)
        acT = at("acT", [SSM_H, S], o_hf + 16 * S + 4 * 512)
        sqg = at("sqg", [P, 2, 4, S], o_hf)
        dtb, alog = at("dtb", [P, SSM_H], room(128)), at("alog", [P, SSM_H], room(128))
        skiprow, dskip = at("skiprow", [P, SSM_H], room(128)), at("dskip", [P, 16], room(64))
        lamrow = at("lamrow", [P, 4, 64], o_al + 16384)
        K2 = at("K2", [P, second[2]], o_mod)
        mem = at("mem", [P, ST, D], o_mod + 4 * second[2])
        assert 4 * second[2] + 4 * ST * D <= 8 * 2 * MODU
        assert top[0] <= base + 4 * 53200 - 64, top[0]

        ps = ctx.enter_context(nc.psum_tensor("ps", [P, 8, 512], F32))

        def kc(name, lo=0, hi=None):
            o, w = first[1][name]
            return K1[:, o + lo:o + (w if hi is None else hi)]

        def kc2(name, lo=0, hi=None):
            o, w = second[1][name]
            return K2[:, o + lo:o + (w if hi is None else hi)]

        ident, ones = kc("ident"), kc("ones")

        def bank(p):
            return 2 * (p % 2)

        def ybank(g, c):
            b = bank(g.p + c // 4) + c % 4 // 2
            return ps[:, b, c % 2 * S:(c % 2 + 1) * S]

        def score_bank(h, m=0, maps=1):
            return 4 + h % 2 if maps == 1 else 4 * (1 - h % 2) + m

        def turned_bank(h):
            return (6, 2)[h % 2]

        def mixed_bank(h):
            return (3, 7)[h % 2]

        def vcol(o, n=1):
            return V[:, o:o + n]

        w_loaded = [sem(f"w_loaded{i}") for i in range(RAW)]
        w_hi, w_lo = sem("w_hi"), sem("w_lo")
        products = sem("products")
        banks_free = [sem("banks_free0"), sem("banks_free1")]
        init_loaded, mod_loaded = sem("init_loaded"), [sem("mod_loaded0"), sem("mod_loaded1")]
        c_loaded, first_loaded = sem("c_loaded"), [sem(f"first_loaded{i}") for i in range(len(mod_first))]
        second_loaded = sem("second_loaded")
        mod_used = sem("mod_used")
        dve_step, act_step, pool_step = sem("dve_step"), sem("act_step"), sem("pool_step")
        stored = sem("stored")
        s = {k: sem(k) for k in SEMS}

        def rows_of(name):
            x = A[name]
            while len(x.shape) > 1:
                x = x.rearrange("a b -> (a b)") if len(x.shape) == 2 else x.rearrange("a b c -> a (b c)")
            return x.rearrange("(r p) -> r p", p=P)

        def init_loads():
            yield K1[:, P:], first[0][:, P:]
            o = 0
            for name, r in ROWS[::-1]:
                o += r
                yield rows[NROWS - o:NROWS - o + r, 6, :], rows_of(name)
            yield x_in[:, :, :], A["x"][0].rearrange("(t p) d -> p t d", p=P)
            yield rows[0:96, 4, :], rows_of("ln_g")
            yield rows[0:96, 5, :], rows_of("ln_b")
            for i in range(DEPTH):
                yield rows[0:72, i, :], A["b_mod"][i].rearrange("(r p) -> r p", p=P)
            yield rows[0:96, 7, :], rows_of("ssm_conv_w")
            for i, k in enumerate(("diff_lambda_q", "diff_lambda_k")):
                yield lamrow[:, 2 * i:2 * i + 2, :], A[k][0].partition_broadcast(P)
            yield dtb[:, :], A["ssm_dt_bias"][0].partition_broadcast(P)
            yield alog[:, :], A["ssm_a_log"][0].partition_broadcast(P)
            yield skiprow[:, :], A["ssm_d_skip"][0].partition_broadcast(P)
            yield posi[:, :], A["positions"][0].partition_broadcast(P)
        n_init = 16 * len(list(init_loads()))

        block = ctx.enter_context(nc.Block())

        @block.sync
        def _(sp):
            def view(kind, slot, *a):
                r = raw[slot]
                if kind == "cols":
                    w, c = a
                    return r[:, :].rearrange("p (k n) -> p k n", k=DC), w.rearrange("(k p) n -> p k n", p=P)[:, :, c]
                if kind == "dt":
                    w, c = a
                    return (r[:, 0:DC * SSM_H].rearrange("p (k n) -> p k n", k=DC),
                            w.rearrange("(k p) n -> p k n", p=P)[:, :, c:c + SSM_H])
                if kind == "part":
                    w, c, to, n = a
                    return (r[:, :].rearrange("p (k n) -> p k n", k=DC)[:, :, to:to + n],
                            w.rearrange("(k p) n -> p k n", p=P)[:, :, c:c + n])
                if kind == "out":
                    w, k = a
                    return r[:, :].rearrange("p (k n) -> p k n", k=2), w.rearrange("(k p) n -> p k n", p=P)[:, k, :]
                if kind == "rows2":
                    w, h = a
                    return (r[:, :].rearrange("p (k n) -> p k n", k=2),
                            w.rearrange("(k p) n -> p k n", p=P)[:, :, h * 256:h * 256 + 1024])
                w, h, k = a
                v = w.rearrange("(k p) (h n) -> p k h n", p=P, n=192)
                o = k * 384
                if kind == "q_up":
                    return r[:, o:o + 256].rearrange("p (h n) -> p h n", h=2), v[:, k, h:h + 2, 0:128]
                return r[:, o + 256:o + 384].rearrange("p (h n) -> p h n", h=2), v[:, k, h:h + 2, 128:192]

            def load(b, it=None):
                if b >= RAW:
                    sp.wait_ge(w_lo, 2 * (b - RAW + 1) if it is None else 2 * (b - RAW + 1) + 8 * it)
                for kind, *a in plan.blocks[b]:
                    if kind == "cols":
                        w, c = a
                        a = [w, ds(c if it is None else it * 512 + c, 256)]
                    elif kind == "out":
                        w, j = a
                        a = [w, ds(2 * j if it is None else it * 8 + 2 * j, 2)]
                    sp.dma_start(*view(kind, b % RAW, *a)).then_inc(w_loaded[b % RAW], 16)

            def load_mod(sub, k, half, it=None):
                u = 16 * sub + 2 * k + half
                if u >= 2:
                    sp.wait_ge(mod_used, u - 1 if it is None else u - 1 + 2 * it)
                w = A["w_mod"][sub // SUB][:, sub % SUB * 3 * D + half * MODU:][:, 0:MODU]
                row = k * P if it is None else it * P + k * P
                sp.dma_start(mod_w[:, half, :], w[ds(row, P), :]).then_inc(mod_loaded[half], 16)

            for st in steps:
                if st.kind == "init":
                    sp.dma_start(K1[:, 0:P], first[0][:, 0:P]).then_inc(c_loaded, 16)
                    sp.dma_start(crow[:, :], A["c"][0].rearrange("(r p) -> r p", p=P)).then_inc(c_loaded, 16)
                    ring = len(mod_first)
                    for u in range(2 * DC):
                        if u == ring:
                            for dst, src in init_loads():
                                sp.dma_start(dst, src).then_inc(init_loaded, 16)
                        if u == 2 * DC - 2:
                            load(0)
                            load(1)
                        if u >= ring:
                            sp.wait_ge(mod_used, u - ring + 1)
                        w = A["w_mod"][0][u // 2 * P:u // 2 * P + P, u % 2 * MODU:u % 2 * MODU + MODU]
                        sp.dma_start(mod_first[u % ring], w).then_inc(first_loaded[u % ring], 16)
                if st.kind == "ffn":
                    nxt = st.args[0] + 1
                    mods = nxt < min(SUB * DEPTH, plan.mods)
                    def turn_in(i, it):
                        if g.b + i >= 2:
                            load(g.b + i, it)
                        if mods and i >= 2 and i % 2:
                            load_mod(nxt, (i - 2) // 4, (i - 2) // 2 % 2, it)

                    g = st.lin["in"]
                    peeled = 6 if g.b < RAW else 2
                    walk(sp, g, turn_in, peeled)

                    def turn_out(i, it):
                        load(g.b + i, it)
                        if mods and i in (1, 3):
                            load_mod(nxt, 6, i // 2, it)

                    for half in range(2 * mods):
                        load_mod(nxt, 5, half)
                    g = st.lin["out"]
                    walk(sp, g, turn_out, 1, 2)
                    if st.args[0] == SUB * DEPTH - 1:
                        sp.wait_ge(s["mod_sum"], st.n["mod_sum"])
                        sp.dma_start(K2[:, :], second[0]).then_inc(second_loaded, 16)
                        sp.dma_start(mem[:, :, :], A["mem_2"][0].rearrange("(t p) d -> p t d", p=P)).then_inc(second_loaded, 16)
                if st.kind in ("mla", "diff", "ssm", "hyb", "xatt"):
                    nxt = st.args[0] + 1 if st.kind not in ("hyb", "xatt") else 10 ** 6
                    todo = [(nxt, k, half) for k in range(DC) for half in range(2)] if nxt < plan.mods else []
                    for g in st.lin.values():
                        for b in range(g.b, g.b + g.n):
                            load(b)
                            late = g is st.lin["out"] and b == g.b + 1
                            while todo and (late or b < st.lin["out"].b):
                                load_mod(*todo.pop(0))
                                if not late:
                                    break
                if st.kind == "store":
                    sp.wait_ge(s["out_ready"], st.n["out_ready"] + 1)
                    sp.dma_start(out[0].rearrange("(t p) d -> p t d", p=P), x_out[:, :, :]).then_inc(stored, 16)
                    sp.wait_ge(stored, 16)

        @block.gpsimd
        def _(pool):
            n = min(plan.mods, SUB * DEPTH)
            if n > 1:
                pool.wait_ge(s["cond_ready"], 1)
                with pool.Fori(1, n) as sub:
                    pool.wait_ge(s["mod_sum"], sub * 2)
                    for k in range(DC):
                        for half in range(2):
                            pool.wait_ge(mod_loaded[half], sub * 128 + 16 * (k + 1) - 128)
                            nc.gpsimd.tensor_tensor(pool_tick[:, 2 * k + half:2 * k + half + 1], cond[:, 0:1], cond[:, 0:1], ALU.add)
                            w = mod_w[:, half, :]
                            if k == 0:
                                nc.gpsimd.tensor_scalar(mod_acc[:, half, :], w, cond[:, 0:1], 1.0, ALU.mult, ALU.mult)\
                                    .then_inc(mod_used, 1)
                                continue
                            nc.gpsimd.tensor_scalar(w, w, cond[:, k:k + 1], 1.0, ALU.mult, ALU.mult).then_inc(pool_step, 1)
                            pool.wait_ge(pool_step, sub * 14 - 14 + 2 * (k - 1) + half + 1)
                            pool.wait_ge(mod_used, sub * 16 + 2 * k + half - 1)
                            nc.gpsimd.tensor_tensor(mod_acc[:, half, :], mod_acc[:, half, :], w, ALU.add)\
                                .then_inc(mod_used, 1)

        @block.scalar
        def _(act):
            step = [0]

            def link(ins):
                step[0] += 1
                ins.then_inc(act_step, 1)
                act.wait_ge(act_step, step[0])

            def copy(dst, src):
                return nc.scalar.activation(dst, src, ACT.Copy)

            def convert(b, it=None, upb=0):
                if b >= NB:
                    return
                act.wait_ge(w_loaded[b % RAW], plan.load_at[b] if it is None else plan.load_at[b] + 16 * it)
                for h in range(2):
                    if b >= 2:
                        u = plan.used[b - 2][h]
                        act.wait_ge(products, u if it is None else 4 * upb * it + u)
                    copy(whi[b % 2][:, h * HALF:(h + 1) * HALF], raw[b % RAW][:, h * HALF:(h + 1) * HALF]).then_inc(w_hi, 1)

            def ready_table(func):
                nc.scalar.activation(tiny[:, 20:21], kc("misc", 4, 5), func)

            def split_h(n):
                for q in range(4):
                    act.wait_ge(s["hf"], n["hf"] + q + 1)
                    copy(H_hi[:, 2 * q:2 * q + 2, :], hf[:, 2 * q:2 * q + 2, :]).then_inc(s["h_hi"], 1)

            def evacuate(g, j, dst, b=None):
                p = g.p + j
                act.wait_ge(products, g.l + (j + 1) * g.upb)
                copy(dst, ps[:, bank(p):bank(p) + 2, 0:S]).then_inc(banks_free[p % 2], 1)

            def attend(n, heads, scale, kind):
                maps = 2 if kind == "diff" else 1
                full = kind == "xatt"
                width = 512 if full else CW
                tiles = ((0, S), (S, 2 * S)) if full else ((0, P), (P, CW))

                def exps(h):
                    act.wait_ge(s["maxed"], n["maxed"] + h + 1)
                    for m in range(maps):
                        for t, (a, b) in enumerate(tiles):
                            src = ps[:, 4 + h % 2, a:b] if full else prob[:, h % 4, m * width + a:m * width + b]
                            i = nc.scalar.activation(prob[:, h % 4, m * width + a:m * width + b], src, ACT.Exp,
                                                     bias=stat[:, h % 4, 4 + 2 * m + t:5 + 2 * m + t], scale=scale,
                                                     accum_out=None if kind == "dilated" else stat[:, h % 4, 8 + 2 * m + t:9 + 2 * m + t])
                    i.then_inc(s["exped"], 1)

                def turned(h):
                    act.wait_ge(s["turned"], n["turned"] + h + 1)
                    if h >= 2:
                        act.wait_ge(s["mixed"], n["mixed"] + h - 1)
                    copy(probT[:, h % 2, 0:width], ps[:, turned_bank(h), 0:width]).then_inc(s["turned_out"], 1)

                def rounded(h):
                    act.wait_ge(s["mixed"], n["mixed"] + h + 1)
                    if kind == "xatt":
                        copy(H_hi[:, 2 * h:2 * h + 2, :], ps[:, mixed_bank(h), :].rearrange("p (c n) -> p c n", c=2)).then_inc(s["mixed_hi"], 1)
                    else:
                        copy(H_hi[:, h, :], ps[:, mixed_bank(h), 0:S]).then_inc(s["mixed_hi"], 1)

                for i in range(heads + 4):
                    if i < heads:
                        exps(i)
                    if 2 <= i < heads + 2:
                        turned(i - 2)
                    if i >= 4 and kind in ("mla", "xatt"):
                        rounded(i - 4)

            def act_init(st, n):
                act.wait_ge(s["c_turned"], 1)
                nc.scalar.activation(cond[:, :], ps[:, 3, 0:DC], ACT.Silu).then_inc(s["cond_ready"], 1)
                act.wait_ge(s["vec_turned"], 1)
                copy(V[:, 0:288], ps[:, 0, 0:288]).then_inc(s["vec_ready"], 1)
                copy(V[:, 288:CONVW], ps[:, 1, 0:CONVW - 288]).then_inc(s["vec_ready"], 1)
                copy(V[:, CONVW:CONVW + 96], ps[:, 2, 0:96]).then_inc(s["vec_ready"], 1)
                act.wait_ge(s["vec_ready"], 3)
                act.wait_ge(s["lam_sum"], 1)
                nc.scalar.activation(tiny[:, 6:8], tiny[:, 4:6], ACT.Exp).then_inc(s["lam_exp"], 1)
                act.wait_ge(s["vec_turned"], 2)
                copy(z[:, :, :], ps[:, 4:8, :].rearrange("p b (c n) -> p (b c) n", c=2)).then_inc(s["z_in"], 1)
                act.wait_ge(s["angle"], 1)
                nc.scalar.activation(sinm[:, :], ang[:, 0, :], ACT.Sin).then_inc(s["rope_sin"], 1)
                link(nc.scalar.activation(ang[:, 1, :], ang[:, 0, :], ACT.Abs))
                nc.scalar.activation(cosm[:, :], ang[:, 1, :], ACT.Sin, bias=kc("misc", 3, 4), scale=-1.0).then_inc(s["rope_sin"], 1)
                convert(0)
                convert(1)
                split_h(n)

            def act_ln(st, n):
                finish(steps[steps.index(st) - 1].lin["out"])
                for q in range(4):
                    act.wait_ge(s["centred"], n["centred"] + q + 1)
                    nc.scalar.activation(sq[:, 2 * q:2 * q + 2, :], z[:, 2 * q:2 * q + 2, :], ACT.Square).then_inc(s["squared"], 1)
                ready_table(ACT.Sqrt)
                act.wait_ge(s["ln_var"], n["ln_var"] + 1)
                nc.scalar.activation(std[:, 0, :], ps[:, 5, 0:S], ACT.Sqrt, bias=kc("misc", 1, 2), scale=1.0 / D).then_inc(s["std"], 1)
                if st.kind == "ln":
                    for c in range(DC):
                        if c % 2 == 0:
                            act.wait_ge(s["hf"], n["hf"] + c // 2 + 1)
                        i = nc.scalar.activation(H_hi[:, c, :], hf[:, c, :], ACT.Identity, bias=B1[:, c:c + 1])
                        if c % 2:
                            i.then_inc(s["h_hi"], 1)

            def act_ffn(st, n):
                g = st.lin["in"]

                def gate(i, it=None):
                    p = g.p + i
                    u = g.l + 2 * (i + 1)
                    act.wait_ge(products, u if it is None else 8 * it + u)
                    nc.scalar.activation(sg[:, i // 2 % 2], ps[:, bank(p):bank(p) + 2, 0:S], ACT.Silu)\
                        .then_inc(banks_free[p % 2], 1)

                def product_hi(j, it=None):
                    p = g.p + 2 * j + 1
                    v = plan.free_val[p]
                    act.wait_ge(banks_free[p % 2], v if it is None else 2 * it + v)
                    to = A_hi[:, 2 * j:2 * j + 2, :] if it is None else A_hi[:, ds(it * 4 + 2 * j, 2), :]
                    copy(to, am[:, j % 2]).then_inc(s["a_hi"], 1)

                def turn(i, it=None):
                    convert(g.b + i + 2, it, 2)
                    if i % 2 == 0:
                        gate(i, it)
                    if i % 2 == 0 and i >= 2:
                        product_hi(i // 2 - 1, it)

                walk(act, g, turn)
                product_hi(FP - 1)
                projected(st)

            def projected(st):
                g = st.lin["out"]
                walk(act, g, lambda i, it: None if it is None and i == g.n - 1 else convert(g.b + i + 2, it, 2), 1, 2)

            def finish(g):
                convert(g.b + g.n + 1)

            def act_mla(st, n):
                g = st.lin["latent"]
                for j in range(3):
                    convert(g.b + j + 2)
                    evacuate(g, j, lat[:, 2 * j:2 * j + 2, :])
                    act.wait_ge(banks_free[(g.p + j) % 2], plan.free_val[g.p + j])
                    m = 2 if j < 2 else 1
                    nc.scalar.activation(sq[:, 2 * j:2 * j + m, :], lat[:, 2 * j:2 * j + m, :], ACT.Square).then_inc(s["lat_sq"], 1)
                act.wait_ge(s["lat_sum"], n["lat_sum"] + 1)
                nc.scalar.activation(std[:, 0, :], ps[:, 4, 0:S], ACT.Sqrt, bias=kc("misc", 2, 3), scale=1.0 / QR)
                nc.scalar.activation(std[:, 1, :], ps[:, 4, S:2 * S], ACT.Sqrt, bias=kc("misc", 2, 3), scale=1.0 / KVR)\
                    .then_inc(s["lat_std"], 1)
                for i, (a, b) in enumerate(((0, 3), (3, 5))):
                    act.wait_ge(s["lat_n"], n["lat_n"] + i + 1)
                    copy(A_hi[:, a:b, :], latn[:, a:b, :]).then_inc(s["lat_hi"], 1)
                g = st.lin["q"]
                for j in range(g.n):
                    p = g.p + j
                    convert(g.b + j + 2)
                    act.wait_ge(products, g.l + j + 1)
                    copy(QN[:, 2 * j:2 * j + 2, :], ps[:, bank(p), :].rearrange("p (c n) -> p c n", c=2))
                    copy(QRp[:, j, :], ps[:, bank(p) + 1, 0:S]).then_inc(banks_free[p % 2], 1)
                g = st.lin["kv"]
                for j in range(g.n):
                    p = g.p + 2 * j
                    convert(g.b + j + 2)
                    act.wait_ge(products, g.l + 2 * j + 1)
                    copy(KN[:, 4 * j:4 * j + 4, :], ps[:, bank(p):bank(p) + 2, :].rearrange("p b (c n) -> p (b c) n", c=2))\
                        .then_inc(banks_free[p % 2], 1)
                    act.wait_ge(products, g.l + 2 * j + 2)
                    copy(VT[:, :, 512 * j:512 * j + 512], ps[:, bank(p + 1):bank(p + 1) + 2, :]).then_inc(banks_free[(p + 1) % 2], 1)
                attend(n, MLA_H, 192.0 ** -0.5, "mla")
                projected(st)

            def linear_evac(g, dst, func=ACT.Copy, start=0, count=None):
                for j in range(start, count or g.n):
                    p = g.p + j
                    convert(g.b + j + 2)
                    act.wait_ge(products, g.l + (j + 1) * g.upb)
                    nc.scalar.activation(dst(j), ps[:, bank(p):bank(p) + 2, 0:S], func).then_inc(banks_free[p % 2], 1)

            def fin_stats(n, i, scale, eps):
                act.wait_ge(s["fin_sum"], n["fin_sum"] + i + 1)
                nc.scalar.activation(z[:, 2 * i:2 * i + 2, :], ps[:, 4 + i, :].rearrange("p (c n) -> p c n", c=2), ACT.Sqrt,
                                     bias=kc("misc", eps, eps + 1), scale=scale).then_inc(s["fin_std"], 1)

            def fin_round(n):
                for i in range(4):
                    act.wait_ge(s["fin_n"], n["fin_n"] + i + 1)
                    copy(H_hi[:, 2 * i:2 * i + 2, :], O1[:, 2 * i:2 * i + 2, :]).then_inc(s["fin_hi"], 1)

            def act_diff(st, n):
                linear_evac(st.lin["qk"], lambda j: (QN if j < 4 else KN)[:, 2 * (j % 4):2 * (j % 4) + 2, :])
                linear_evac(st.lin["v"], lambda j: VT[:, :, 256 * j:256 * j + 256])
                attend(n, 8, 64.0 ** -0.5, "diff")
                for i in range(4):
                    act.wait_ge(s["mixed_out"], n["mixed_out"] + 8)
                    nc.scalar.activation(sq[:, 2 * i:2 * i + 2, :], O1[:, 2 * i:2 * i + 2, :], ACT.Square).then_inc(s["fin_sq"], 1)
                ready_table(ACT.Sqrt)
                for i in range(4):
                    fin_stats(n, i, 1.0 / P, 2)
                fin_round(n)
                projected(st)

            def act_ssm(st, n):
                linear_evac(st.lin["z"], lambda j: Z[:, 2 * j:2 * j + 2, :], ACT.Silu)
                g = st.lin["xbc"]
                for j in range(g.n):
                    p = g.p + j
                    convert(g.b + j + 2)
                    act.wait_ge(banks_free[p % 2], plan.free_val[p])
                    dst = XC[:, 2 * j:2 * j + 2, :] if j < 8 else (Bm if j < 10 else Cm)[:, 2 * (j % 2):2 * (j % 2) + 2, :]
                    nc.scalar.activation(dst, conv[:, j % 2], ACT.Silu).then_inc(s["conv_out"], 1)
                g = st.lin["dt"]
                convert(g.b + 2)
                link(nc.scalar.activation(alog[:, :], alog[:, :], ACT.Exp))
                act.wait_ge(s["dt_in"], n["dt_in"] + 1)
                link(nc.scalar.activation(dts[:, 1], dts[:, 0], ACT.Abs))
                link(nc.scalar.activation(dts[:, 2], dts[:, 1], ACT.Exp, scale=-1.0))
                nc.scalar.activation(dts[:, 3], dts[:, 2], ACT.Ln, bias=kc("misc", 4, 5)).then_inc(s["dt_ln"], 1)
                for q in range(8):
                    act.wait_ge(s["x_turned"], n["x_turned"] + q + 1)
                    copy(XT[:, q // 4, q % 4 * 512:q % 4 * 512 + 512], ps[:, 4 + q % 2, :]).then_inc(s["x_out"], 1)
                act.wait_ge(s["acum"], n["acum"] + 1)
                copy(acT[:, :], ps[0:SSM_H, 4, 0:S]).then_inc(s["acum_t"], 1)
                for h in range(SSM_H):
                    act.wait_ge(s["dec"], n["dec"] + h + 1)
                    nc.scalar.activation(dec[:, h % 2, :], dec[:, h % 2, :], ACT.Exp).then_inc(s["dec_exp"], 1)
                act.wait_ge(s["y_out"], n["y_out"] + 16)

                def squares(i):
                    nc.scalar.activation(sqg[:, i % 2], Z[:, 4 * i:4 * i + 4, :], ACT.Square).then_inc(s["fin_sq"], 1)

                squares(0)
                for i in range(4):
                    if i < 3:
                        squares(i + 1)
                    act.wait_ge(s["fin_sum"], n["fin_sum"] + i + 1)
                    nc.scalar.activation(std[:, i % 2, :], ps[:, 4 + i % 2, 0:S], ACT.Sqrt, bias=kc("misc", 2, 3), scale=1.0 / 512)\
                        .then_inc(s["fin_std"], 1)
                    act.wait_ge(s["fin_n"], n["fin_n"] + i + 1)
                    copy(A_hi[:, 4 * i:4 * i + 4, :], Z[:, 4 * i:4 * i + 4, :]).then_inc(s["fin_hi"], 1)
                projected(st)

            def act_hyb(st, n):
                L = st.lin
                linear_evac(L["aqk"], lambda j: (QN if j < 2 else KN)[:, 2 * (j % 2):2 * (j % 2) + 2, :])
                linear_evac(L["av"], lambda j: VT[:, :, 256 * j:256 * j + 256])
                linear_evac(L["rqk"], lambda j: (QN if j < 2 else KN)[:, 4 + 2 * (j % 2):6 + 2 * (j % 2), :])
                linear_evac(L["rv"], lambda j: VT[:, :, 512 + 256 * j:768 + 256 * j])
                linear_evac(L["rg"], lambda j: RG[:, 2 * j:2 * j + 2, :], ACT.Silu)
                attend(n, 8, 64.0 ** -0.5, "dilated")
                for i in range(4):
                    if i < 2:
                        act.wait_ge(s["mixed_out"], n["mixed_out"] + 8)
                    else:
                        act.wait_ge(s["fin_cent"], n["fin_cent"] + i - 1)
                    nc.scalar.activation(sq[:, 2 * i:2 * i + 2, :], O1[:, 2 * i:2 * i + 2, :], ACT.Square).then_inc(s["fin_sq"], 1)
                for i in range(4):
                    fin_stats(n, i, 1.0 / 64 if i < 2 else 1.0 / P, 2 if i < 2 else 1)
                fin_round(n)
                projected(st)

            def act_mem(st, n):
                act.wait_ge(second_loaded, 32)
                act.wait_ge(s["h_hi"], n["h_hi"])
                for t in range(ST):
                    link(nc.scalar.activation(sqj[:, :], mem[:, t, :], ACT.Square, accum_out=tiny[:, 8 + t:9 + t]))
                nc.scalar.activation(tiny[:, 10:12], tiny[:, 8:10], ACT.Sqrt, bias=kc("misc", 2, 3), scale=1.0 / D).then_inc(s["mem_std"], 1)

            def act_xatt(st, n):
                L = st.lin
                linear_evac(L["q"], lambda j: QN[:, 2 * j:2 * j + 2, :], count=2)
                act.wait_ge(s["mem_f"], n["mem_f"] + 1)
                copy(M_hi, hf[:, :, :]).then_inc(s["mem_hi"], 1)
                linear_evac(L["q"], lambda j: QN[:, 2 * j:2 * j + 2, :], start=2)
                linear_evac(L["k"], lambda j: KN[:, 2 * j:2 * j + 2, :])
                linear_evac(L["v"], lambda j: VT[:, :, 256 * j:256 * j + 256])
                attend(n, XH, 256.0 ** -0.5, "xatt")
                projected(st)

            def act_pre(st, n):
                parts = steps[steps.index(st) - 1].kind == "post"
                for q in range(4):
                    act.wait_ge(s["ax_ready"], n["ax_ready"] - (3 - q) * parts)
                    nc.scalar.activation(sq[:, 2 * q:2 * q + 2, :], ax[:, 2 * q:2 * q + 2, :], ACT.Square).then_inc(s["squared"], 1)
                ready_table(ACT.Sqrt)
                act.wait_ge(s["x_sum"], n["x_sum"] + 1)
                nc.scalar.activation(std[:, 0, :], ps[:, 5, 0:S], ACT.Sqrt, bias=kc("misc", 2, 3), scale=1.0 / D).then_inc(s["std"], 1)
                split_h(n)

            def act_post(st, n):
                g = steps[steps.index(st) - 1].lin["out"]
                for q in range(4):
                    act.wait_ge(products, g.l + 2 * (g.n - 1) + 2 + 2 * q)
                    b = bank(g.p + q // 2) + q % 2
                    nc.scalar.activation(sq[:, 2 * q:2 * q + 2, :], ps[:, b, :].rearrange("p (c n) -> p c n", c=2), ACT.Square)\
                        .then_inc(s["y_sq"], 1)
                finish(g)
                ready_table(ACT.Sqrt)
                act.wait_ge(s["y_sum"], n["y_sum"] + 1)
                nc.scalar.activation(std[:, 0, :], ps[:, 5, 0:S], ACT.Sqrt, bias=kc("misc", 2, 3), scale=1.0 / D).then_inc(s["std"], 1)

            def act_store(st, n):
                act.wait_ge(s["out_turned"], n["out_turned"] + 1)
                copy(x_out[:, :, :], ps[:, 4:8, :].rearrange("p (t b) n -> p t (b n)", t=ST)).then_inc(s["out_ready"], 1)

            for st in steps:
                {"init": act_init, "ln": act_ln, "ln_last": act_ln, "ffn": act_ffn, "mla": act_mla, "diff": act_diff, "ssm": act_ssm,
                 "pre": act_pre, "post": act_post, "hyb": act_hyb, "mem": act_mem, "xatt": act_xatt,
                 "store": act_store}[st.kind](st, st.n)

        @block.vector
        def _(dve):
            step = [0]

            def link(ins):
                step[0] += 1
                ins.then_inc(dve_step, 1)
                dve.wait_ge(dve_step, step[0])

            tt, ts, stt = nc.vector.tensor_tensor, nc.vector.tensor_scalar, nc.vector.scalar_tensor_tensor

            def convert(b, it=None):
                if b >= NB:
                    return
                for h in range(2):
                    v = 2 * b + h + 1
                    dve.wait_ge(w_hi, v if it is None else 8 * it + v)
                    r = slice(h * HALF, (h + 1) * HALF)
                    tt(wlo[b % 2][:, r], raw[b % RAW][:, r], whi[b % 2][:, r].bitcast(F32), ALU.subtract).then_inc(w_lo, 1)

            def coefficients(sub, n):
                if sub < SUB * DEPTH:
                    dve.wait_ge(s["mod_sum"], n["mod_sum"] + 1)
                    i, j = divmod(sub, SUB)
                    link(tt(modc[:, 0:16], ps[:, 6, 0:16], vcol(72 * i + 24 * j, 16), ALU.add))
                    link(ts(t8[:, 0, :], modc[:, 8:16], 1.0, None, ALU.add))
                    if sub:
                        g, b = vcol(LNG + 8 * (sub - 1), 8), vcol(LNB + 8 * (sub - 1), 8)
                        tt(G1[:, :], t8[:, 0, :], g, ALU.mult)
                        link(tt(t8[:, 1, :], t8[:, 0, :], b, ALU.mult))
                        tt(B1[:, :], t8[:, 1, :], modc[:, 0:8], ALU.add)
                        ts(G2[:, :], g, ALPHA, None, ALU.mult)
                        link(ts(B2[:, :], b, ALPHA, None, ALU.mult))
                    else:
                        nc.vector.tensor_copy(G1[:, :], t8[:, 0, :])
                        nc.vector.tensor_copy(B1[:, :], modc[:, 0:8])
                        nc.vector.memset(G2[:, :], ALPHA)
                        link(nc.vector.memset(B2[:, :], 0.0))
                else:
                    nc.vector.tensor_copy(G2[:, :], vcol(LNG + 8 * (sub - 1), 8))
                    link(nc.vector.tensor_copy(B2[:, :], vcol(LNB + 8 * (sub - 1), 8)))

            def fold(n, ready):
                f = acc[:, 1:3, :]
                for q in range(1, 4):
                    dve.wait_ge(s[ready], n[ready] + q + 1)
                    link(tt(f, f if q > 1 else sq[:, 0:2, :], sq[:, 2 * q:2 * q + 2, :], ALU.add))
                tt(acc[:, 1, :], acc[:, 1, :], acc[:, 2, :], ALU.add).then_inc(s["folded"], 1)

            def gates(sub, n):
                dve.wait_ge(s["mod_sum"], n["mod_sum"] + 2)
                i, j = divmod(sub, SUB)
                link(tt(modc[:, 16:24], ps[:, 7, 0:8], vcol(72 * i + 24 * j + 16, 8), ALU.add))
                ts(gw[:, :], modc[:, 16:24], 1.0 if j == 1 else 0.5, None, ALU.mult)

            def residual():
                for c in range(DC):
                    i = ts(ax[:, c, :], z[:, c, :], G2[:, c:c + 1], B2[:, c:c + 1], ALU.mult, ALU.add)
                i.then_inc(s["ax_ready"], 1)

            def spread(n):
                for c in range(DC):
                    i = ts(hf[:, c, :], z[:, c, :], G1[:, c:c + 1], B1[:, c:c + 1], ALU.mult, ALU.add)
                    if c % 2:
                        i.then_inc(s["hf"], 1)
                for q in range(4):
                    dve.wait_ge(s["h_hi"], n["h_hi"] + q + 1)
                    r = slice(2 * q, 2 * q + 2)
                    tt(H_lo[:, r, :], hf[:, r, :], H_hi[:, r, :].bitcast(F32), ALU.subtract).then_inc(s["h_lo"], 1)
                residual()

            def dve_init(st, n):
                def modulation(u):
                    k, half = u // 2, u % 2
                    ring = len(mod_first)
                    dve.wait_ge(first_loaded[u % ring], 16 * (u // ring + 1))
                    w = mod_first[u % ring]
                    if k == 0:
                        ts(mod_acc[:, half, :], w, cond[:, 0:1], None, ALU.mult).then_inc(mod_used, 1)
                        return
                    dve.wait_ge(mod_used, u - 1)
                    stt(mod_acc[:, half, :], w, cond[:, k:k + 1], mod_acc[:, half, :], ALU.mult, ALU.add).then_inc(mod_used, 1)

                dve.wait_ge(s["cond_ready"], 1)
                for u in range(8):
                    modulation(u)
                dve.wait_ge(init_loaded, n_init)
                link(nc.vector.tensor_copy(ang[:, 2, :], posi[:, :]))
                link(ts(ang[:, 0, :], ang[:, 2, :], kc("misc", 0, 1), None, ALU.mult))
                magic = 1.5 * 2.0 ** 23
                link(ts(ang[:, 1, :], ang[:, 0, :], 1.0 / TWO_PI, magic, ALU.mult, ALU.add))
                link(ts(ang[:, 1, :], ang[:, 1, :], magic, None, ALU.subtract))
                c1, c2 = 6.28125, 0.0019350051879882812
                for c in (c1, c2, TWO_PI - c1 - c2):
                    link(stt(ang[:, 0, :], ang[:, 1, :], -c, ang[:, 0, :], ALU.mult, ALU.add))
                ts(ang[:, 0, :], ang[:, 0, :], 3.1415925, -3.1415925, ALU.min, ALU.max).then_inc(s["angle"], 1)
                for i in range(2):
                    r = slice(64 * i, 64 * i + 64)
                    nc.vector.tensor_copy(dskip[r, :], skiprow[r, :].rearrange("p (c i) -> p c i", i=2)[:, :, i])
                lam_init = 0.8 - 0.6 * math.exp(-0.3 * 1)
                link(tt(lamrow[:, 0:2, :], lamrow[:, 0:2, :], lamrow[:, 2:4, :], ALU.mult))
                nc.vector.tensor_reduce(tiny[:, 4:6], lamrow[:, 0:2, :], AX, ALU.add).then_inc(s["lam_sum"], 1)
                dve.wait_ge(s["lam_exp"], 1)
                link(tt(tiny[:, 2:3], tiny[:, 7:8], tiny[:, 6:7], ALU.subtract))
                ts(tiny[:, 0:1], tiny[:, 2:3], lam_init, None, ALU.subtract)
                dve.wait_ge(s["vec_ready"], 3)
                ts(tiny[:, 1:2], vcol(column("diff_subln_g")), 1.0 - lam_init, None, ALU.mult)
                for u in range(8, 2 * DC - 2):
                    modulation(u)
                convert(0)
                convert(1)
                modulation(2 * DC - 2)
                modulation(2 * DC - 1)
                coefficients(0, n)
                dve.wait_ge(s["z_in"], 1)
                spread(n)
                gates(0, n)

            def dve_ln(st, n):
                sub = st.args[0]

                def running(c):
                    dve.wait_ge(s["z_ready"], n["z_ready"] + c + 1)
                    if c > 1:
                        dve.wait_ge(s["zsum"], n["zsum"] + c - 1)
                    tt(acc[:, 0, :], acc[:, 0, :] if c > 1 else z[:, 0, :], z[:, c, :], ALU.add).then_inc(s["zsum"], 1)

                g = steps[steps.index(st) - 1].lin["out"]
                for c in range(DC):
                    if c == 0:
                        dve.wait_ge(s["ax_ready"], n["ax_ready"])
                    dve.wait_ge(products, g.l + 2 * (g.n - 1) + 1 + (c | 1))
                    stt(z[:, c, :], ybank(g, c), gw[:, c:c + 1], ax[:, c, :], ALU.mult, ALU.add).then_inc(s["z_ready"], 1)
                    if c > 1:
                        running(c - 1)
                running(DC - 1)
                dve.wait_ge(s["ln_sum"], n["ln_sum"] + 1)
                dve.wait_ge(s["z_ready"], n["z_ready"] + DC)
                mean = ps[:, 4, 0:S].unsqueeze(1).to_broadcast([P, 2, S])
                for q in range(4):
                    r = slice(2 * q, 2 * q + 2)
                    stt(z[:, r, :], mean, -1.0 / D, z[:, r, :], ALU.mult, ALU.add).then_inc(s["centred"], 1)
                fold(n, "squared")
                if st.kind == "ln":
                    convert(g.b + g.n)
                coefficients(sub + 1, n)
                dve.wait_ge(s["std"], n["std"] + 1)
                link(nc.vector.reciprocal(std[:, 1, :], std[:, 0, :]))
                rstd = std[:, 1, :].unsqueeze(1).to_broadcast([P, 4, S])
                dve.wait_ge(s["centred"], n["centred"] + 4)
                if st.kind == "ln":
                    for q, lo in ((0, False), (1, False), (0, True), (2, False), (1, True), (3, False), (2, True), (3, True)):
                        if not lo:
                            for c in (2 * q, 2 * q + 1):
                                i = stt(hf[:, c, :], z[:, c, :], G1[:, c:c + 1], std[:, 1, :], ALU.mult, ALU.mult)
                            i.then_inc(s["hf"], 1)
                        else:
                            dve.wait_ge(s["h_hi"], n["h_hi"] + q + 1)
                            for c in (2 * q, 2 * q + 1):
                                i = stt(H_lo[:, c, :], hf[:, c, :], B1[:, c:c + 1], H_hi[:, c, :].bitcast(F32), ALU.add, ALU.subtract)
                            i.then_inc(s["h_lo"], 1)
                    convert(g.b + g.n + 1)
                for h in range(2):
                    r = slice(4 * h, 4 * h + 4)
                    i = tt(z[:, r, :], z[:, r, :], rstd, ALU.mult)
                link(i)
                if st.kind == "ln":
                    gates(sub + 1, n)
                residual()

            def dve_ffn(st, n):
                g = st.lin["in"]

                def product(j, it=None):
                    p = g.p + 2 * j + 1
                    v = plan.free_val[p - 1]
                    dve.wait_ge(banks_free[(p - 1) % 2], v if it is None else 2 * it + v)
                    u = g.l + 4 * (j + 1)
                    dve.wait_ge(products, u if it is None else 8 * it + u)
                    tt(am[:, j % 2], sg[:, j % 2], ps[:, bank(p):bank(p) + 2, 0:S], ALU.mult).then_inc(banks_free[p % 2], 1)

                def product_lo(j, it=None):
                    v = n["a_hi"] + j + 1
                    dve.wait_ge(s["a_hi"], v if it is None else 2 * it + v)
                    r = slice(2 * j, 2 * j + 2) if it is None else ds(it * 4 + 2 * j, 2)
                    tt(A_lo[:, r, :], am[:, j % 2], A_hi[:, r, :].bitcast(F32), ALU.subtract).then_inc(s["a_lo"], 1)

                def turn(i, it=None):
                    convert(g.b + i + 2, it)
                    if i % 2 == 1:
                        product(i // 2, it)
                    if i % 2 == 0 and i >= 2:
                        product_lo(i // 2 - 1, it)

                walk(dve, g, turn)
                product_lo(FP - 1)
                projected(st)

            def projected(st):
                g = st.lin["out"]
                walk(dve, g, lambda i, it: None if it is None and i >= g.n - 2 else convert(g.b + i + 2, it), 1, 2)


            def attend(n, heads, scale, kind):
                maps = 2 if kind == "diff" else 1
                full = kind == "xatt"
                width = 512 if full else CW
                tiles = ((0, S), (S, 2 * S)) if full else ((0, P), (P, CW))

                dve.wait_ge(s["ax_ready"], n["ax_ready"])

                def maxima(h):
                    b = h % 4
                    dve.wait_ge(s["scores"], n["scores"] + h + 1)
                    if h >= 4:
                        dve.wait_ge(s["turned"], n["turned"] + h - 3)
                    if full:
                        link(nc.vector.tensor_reduce(stat[:, b, 0:2], ps[:, 4 + h % 2, :].rearrange("p (t k) -> p t k", t=2), AX, ALU.max))
                    else:
                        for m in range(maps):
                            src = ps[:, score_bank(h, m, maps), 0:CW]
                            mask = kc("causal") if kind != "dilated" else kc2("dil_add")
                            link(tt(prob[:, b, m * CW:(m + 1) * CW], src, mask, ALU.add))
                        for m in range(maps):
                            for t, (x, y) in enumerate(tiles):
                                i = nc.vector.tensor_reduce(stat[:, b, 2 * m + t:2 * m + t + 1], prob[:, b, m * CW + x:m * CW + y], AX, ALU.max)
                        link(i)
                    ts(stat[:, b, 4:4 + 2 * maps], stat[:, b, 0:2 * maps], -scale, None, ALU.mult).then_inc(s["maxed"], 1)

                def normal(h):
                    b = h % 4
                    dve.wait_ge(s["exped"], n["exped"] + h + 1)
                    if kind == "dilated":
                        for t, (x, y) in enumerate(tiles):
                            i = stt(prob[:, b, x:y], prob[:, b, x:y], 1.0, kc2("dil_times", x, y), ALU.mult, ALU.mult,
                                    accum_out=stat[:, b, 8 + t:9 + t])
                            link(i)
                    link(nc.vector.reciprocal(stat[:, b, 12:12 + 2 * maps], stat[:, b, 8:8 + 2 * maps]))
                    if kind == "diff":
                        link(ts(stat[:, b, 14:16], stat[:, b, 14:16], tiny[:, 0:1], None, ALU.mult))
                    for t, (x, y) in enumerate(tiles):
                        i = ts(prob[:, b, x:y], prob[:, b, x:y], stat[:, b, 12 + t:13 + t], None, ALU.mult)
                    if kind == "diff":
                        link(i)
                        for t, (x, y) in enumerate(tiles):
                            i = stt(prob[:, b, x:y], prob[:, b, CW + x:CW + y], stat[:, b, 14 + t:15 + t], prob[:, b, x:y],
                                    ALU.mult, ALU.add)
                    i.then_inc(s["probs"], 1)

                def output(h):
                    if kind in ("mla", "xatt"):
                        dve.wait_ge(s["mixed_hi"], n["mixed_hi"] + h + 1)
                        if kind == "xatt":
                            r = slice(2 * h, 2 * h + 2)
                            tt(H_lo[:, r, :], ps[:, mixed_bank(h), :].rearrange("p (c n) -> p c n", c=2), H_hi[:, r, :].bitcast(F32), ALU.subtract)\
                                .then_inc(s["mixed_out"], 1)
                        else:
                            tt(H_lo[:, h, :], ps[:, mixed_bank(h), 0:S], H_hi[:, h, :].bitcast(F32), ALU.subtract).then_inc(s["mixed_out"], 1)
                        return
                    dve.wait_ge(s["mixed"], n["mixed"] + h + 1)
                    if kind == "diff":
                        nc.vector.tensor_copy(O1[:, h, :], ps[:, mixed_bank(h), 0:S]).then_inc(s["mixed_out"], 1)
                    else:
                        r = slice(64 * (h % 2), 64 * (h % 2) + 64)
                        nc.vector.tensor_copy(O1[r, h // 2, :], ps[r, mixed_bank(h), 0:S]).then_inc(s["mixed_out"], 1)

                for i in range(heads + 4):
                    if i < heads:
                        maxima(i)
                    if 1 <= i <= heads:
                        normal(i - 1)
                    if i >= 4:
                        output(i - 4)

            def dve_mla(st, n):
                splits(st.lin["latent"])
                idx = st.args[0] // 9
                dve.wait_ge(s["lat_std"], n["lat_std"] + 1)
                link(nc.vector.reciprocal(std[:, :, :], std[:, :, :]))
                for c in range(5):
                    g = vcol(column("mla_q_norm_g", 3 * idx + c)) if c < 3 else vcol(column("mla_kv_norm_g", 2 * idx + c - 3))
                    i = stt(latn[:, c, :], lat[:, c, :], g, std[:, c // 3, :], ALU.mult, ALU.mult)
                    if c in (2, 4):
                        i.then_inc(s["lat_n"], 1)
                for i, (a, b) in enumerate(((0, 3), (3, 5))):
                    dve.wait_ge(s["lat_hi"], n["lat_hi"] + i + 1)
                    tt(A_lo[:, a:b, :], latn[:, a:b, :], A_hi[:, a:b, :].bitcast(F32), ALU.subtract).then_inc(s["lat_lo"], 1)
                dve.wait_ge(s["kr_rot"], n["kr_rot"] + 1)
                tt(rtmp[:, 0, 0, :], lat[:, 5, :], cosm[:, :], ALU.mult)
                link(tt(rtmp[:, 1, 0, :], ps[:, 5, 0:S], sinm[:, :], ALU.mult))
                tt(KRp[:, :], rtmp[:, 0, 0, :], rtmp[:, 1, 0, :], ALU.add).then_inc(s["kr_ready"], 1)
                splits(st.lin["q"])
                splits(st.lin["kv"])
                cos2 = cosm[:, :].unsqueeze(1).to_broadcast([P, 2, S])
                sin2 = sinm[:, :].unsqueeze(1).to_broadcast([P, 2, S])
                dve.wait_ge(s["kr_ready"], n["kr_ready"] + 1)
                for i in range(2):
                    dve.wait_ge(s["qr_rot"], n["qr_rot"] + i + 1)
                    if i:
                        dve.wait_ge(s["qr_ready"], n["qr_ready"] + i)
                    tt(rtmp[:, 0], QRp[:, 2 * i:2 * i + 2, :], cos2, ALU.mult)
                    link(tt(rtmp[:, 1], ps[:, 4 + i, :].rearrange("p (c n) -> p c n", c=2), sin2, ALU.mult))
                    tt(QRp[:, 2 * i:2 * i + 2, :], rtmp[:, 0], rtmp[:, 1], ALU.add).then_inc(s["qr_ready"], 1)
                attend(n, MLA_H, 192.0 ** -0.5, "mla")
                projected(st)

            def splits(g):
                for i in range(g.n):
                    convert(g.b + i + 2)

            def fin_low(n, i):
                dve.wait_ge(s["fin_hi"], n["fin_hi"] + i + 1)
                r = slice(2 * i, 2 * i + 2)
                tt(H_lo[:, r, :], O1[:, r, :], H_hi[:, r, :].bitcast(F32), ALU.subtract).then_inc(s["fin_lo"], 1)

            def dve_diff(st, n):
                splits(st.lin["qk"])
                splits(st.lin["v"])
                attend(n, 8, 64.0 ** -0.5, "diff")
                dve.wait_ge(s["mixed_out"], n["mixed_out"] + 8)
                for i in range(4):
                    dve.wait_ge(s["fin_std"], n["fin_std"] + i + 1)
                    r = slice(2 * i, 2 * i + 2)
                    link(nc.vector.reciprocal(z[:, r, :], z[:, r, :]))
                    stt(O1[:, r, :], O1[:, r, :], tiny[:, 1:2], z[:, r, :], ALU.mult, ALU.mult).then_inc(s["fin_n"], 1)
                    if i:
                        fin_low(n, i - 1)
                fin_low(n, 3)
                projected(st)

            def dve_ssm(st, n):
                splits(st.lin["z"])
                g = st.lin["xbc"]
                for j in range(g.n):
                    convert(g.b + j + 2)
                    p = g.p + j
                    dve.wait_ge(products, g.l + (j + 1) * g.upb)
                    if j >= 2:
                        dve.wait_ge(s["conv_out"], n["conv_out"] + j - 1)
                    for d in range(4):
                        for c in range(2):
                            src, dst = ps[:, bank(p) + c, 0:S - d], conv[:, j % 2, c, d:S]
                            w = vcol(CONVW + 24 * (3 - d) + 2 * j + c)
                            if d == 0:
                                i = ts(dst, src, w, vcol(column("ssm_conv_b", 2 * j + c)), ALU.mult, ALU.add)
                            else:
                                i = stt(dst, src, w, dst, ALU.mult, ALU.add)
                            if d == 3 and c == 1:
                                i.then_inc(banks_free[p % 2], 1)
                            else:
                                step[0] += 1
                                i.then_inc(dve_step, 1)
                                if d or c:
                                    dve.wait_ge(dve_step, step[0] - 1)
                g = st.lin["dt"]
                convert(g.b + 2)
                dve.wait_ge(products, g.l + 1)
                dve.wait_ge(s["conv_out"], n["conv_out"] + 12)
                link(tt(dts[:, 0], ps[:, bank(g.p):bank(g.p) + 2, 0:SSM_H], dtb[:, :].unsqueeze(1).to_broadcast([P, 2, SSM_H]), ALU.add))
                ts(dts[:, 4], dts[:, 0], 0.0, None, ALU.max).then_inc(banks_free[g.p % 2], 1)
                nc.vector.memset(yt[:, 0, 0:1], 0.0).then_inc(s["dt_in"], 1)
                dve.wait_ge(s["dt_ln"], n["dt_ln"] + 1)
                dve.wait_ge(banks_free[g.p % 2], plan.free_val[g.p])
                link(tt(dts[:, 5], dts[:, 4], dts[:, 3], ALU.add))
                stt(dts[:, 6], dts[:, 5], -1.0, alog[:, :].unsqueeze(1).to_broadcast([P, 2, SSM_H]), ALU.mult, ALU.mult).then_inc(s["adt"], 1)
                dve.wait_ge(s["acum"], n["acum"] + 1)
                link(nc.vector.tensor_copy(dts[:, 7], ps[:, 5, 0:64].rearrange("p (t h) -> p t h", t=2)))
                for i in range(SSM_G):
                    dve.wait_ge(s["cb"], n["cb"] + i + 1)
                    tt(CB[:, i, :], ps[:, 6 + i % 2, 0:CW], tri3, ALU.mult).then_inc(s["cb_out"], 1)
                dve.wait_ge(s["cb_out"], n["cb_out"] + SSM_G)

                def decay(h):
                    dve.wait_ge(s["spread"], n["spread"] + h + 1)
                    if h >= 2:
                        dve.wait_ge(s["mixing"], n["mixing"] + h - 1)
                    src = ps[:, 4 + h % 2, 0:S]
                    ts(dec[:, h % 2, 0:S], src, dts[:, 7, 0, h:h + 1], 0.0, ALU.subtract, ALU.min)
                    ts(dec[:, h % 2, S:CW], src[:, P:S], dts[:, 7, 1, h:h + 1], 0.0, ALU.subtract, ALU.min).then_inc(s["dec"], 1)

                def mixing(h):
                    dve.wait_ge(s["dec_exp"], n["dec_exp"] + h + 1)
                    if h >= 2:
                        dve.wait_ge(s["ssd"], n["ssd"] + h - 1)
                    for t, (a, b) in enumerate(((0, S), (S, CW))):
                        i = stt(mixw[:, h % 2, a:b], dec[:, h % 2, a:b], dts[:, 5, t, h:h + 1], CB[:, h // 8, a:b], ALU.mult, ALU.mult)
                    i.then_inc(s["mixing"], 1)

                def output(c):
                    dve.wait_ge(s["ssd"], n["ssd"] + 2 * c + 2)
                    if c >= 2:
                        dve.wait_ge(s["y_out"], n["y_out"] + c - 1)
                    link(stt(yt[:, c % 2, :], XC[:, c, :], dskip[:, c:c + 1], ps[:, 6 + c % 2, 0:S], ALU.mult, ALU.add))
                    tt(Z[:, c, :], yt[:, c % 2, :], Z[:, c, :], ALU.mult).then_inc(s["y_out"], 1)

                for i in range(SSM_H + 3):
                    if i < SSM_H:
                        decay(i)
                    if 1 <= i <= SSM_H:
                        mixing(i - 1)
                    if i >= 3 and (i - 3) % 2:
                        output((i - 3) // 2)
                for i in range(4):
                    dve.wait_ge(s["fin_std"], n["fin_std"] + i + 1)
                    link(nc.vector.reciprocal(std[:, i % 2, :], std[:, i % 2, :]))
                    for c in range(4 * i, 4 * i + 4):
                        k = stt(Z[:, c, :], Z[:, c, :], vcol(column("ssm_norm_g", c)), std[:, i % 2, :], ALU.mult, ALU.mult)
                    k.then_inc(s["fin_n"], 1)
                    dve.wait_ge(s["fin_hi"], n["fin_hi"] + i + 1)
                    r = slice(4 * i, 4 * i + 4)
                    tt(A_lo[:, r, :], Z[:, r, :], A_hi[:, r, :].bitcast(F32), ALU.subtract).then_inc(s["fin_lo"], 1)
                projected(st)

            def dve_hyb(st, n):
                for g in list(st.lin.values())[:-1]:
                    splits(g)
                dve.wait_ge(second_loaded, 32)
                for i in range(8):
                    X = (QN, KN)[i // 2 % 2]
                    r = slice(4 * (i // 4) + 2 * (i % 2), 4 * (i // 4) + 2 * (i % 2) + 2)
                    cos, sin = (("cos_att", "sin_att"), ("cos_ret", "sin_ret"))[i // 4]
                    cos, sin = (kc2(k).unsqueeze(1).to_broadcast([P, 2, S]) for k in (cos, sin))
                    dve.wait_ge(s["rot"], n["rot"] + i + 1)
                    if i:
                        dve.wait_ge(s["rot_out"], n["rot_out"] + i)
                    tt(rtmp[:, 0], X[:, r, :], cos, ALU.mult)
                    link(tt(rtmp[:, 1], ps[:, 4 + i % 2, :].rearrange("p (c n) -> p c n", c=2), sin, ALU.mult))
                    tt(X[:, r, :], rtmp[:, 0], rtmp[:, 1], ALU.add).then_inc(s["rot_out"], 1)
                attend(n, 8, 64.0 ** -0.5, "dilated")
                for h in range(RET_H + 1):
                    if h < RET_H:
                        dve.wait_ge(s["kq"], n["kq"] + h + 1)
                        if h >= 2:
                            dve.wait_ge(s["ret"], n["ret"] + h - 1)
                        tt(prob[:, h % 2, 0:CW], ps[:, 4 + h % 2, 0:CW], kc2(f"decay{h}"), ALU.mult).then_inc(s["kq_out"], 1)
                    if h:
                        dve.wait_ge(s["ret"], n["ret"] + h)
                        nc.vector.tensor_copy(O1[:, 3 + h, :], ps[:, 7, 0:S]).then_inc(s["ret_out"], 1)
                dve.wait_ge(s["ret_out"], n["ret_out"] + RET_H)
                for i in range(2):
                    dve.wait_ge(s["fin_mean"], n["fin_mean"] + i + 1)
                    r = slice(4 + 2 * i, 6 + 2 * i)
                    stt(O1[:, r, :], ps[:, 4 + i, :].rearrange("p (c n) -> p c n", c=2), -1.0 / P, O1[:, r, :], ALU.mult, ALU.add)\
                        .then_inc(s["fin_cent"], 1)
                dve.wait_ge(s["fin_cent"], n["fin_cent"] + 2)
                for i in range(4):
                    dve.wait_ge(s["fin_std"], n["fin_std"] + i + 1)
                    link(nc.vector.reciprocal(z[:, 2 * i:2 * i + 2, :], z[:, 2 * i:2 * i + 2, :]))
                    for c in range(2 * i, 2 * i + 2):
                        gain = vcol(column("attn_gn_g_2", c)) if i < 2 else vcol(column("ret_gn_g_2", c - 4))
                        k = stt(O1[:, c, :], O1[:, c, :], gain, z[:, c, :], ALU.mult, ALU.mult)
                    if i >= 2:
                        link(k)
                        r = slice(2 * i, 2 * i + 2)
                        k = tt(O1[:, r, :], O1[:, r, :], RG[:, 2 * i - 4:2 * i - 2, :], ALU.mult)
                    k.then_inc(s["fin_n"], 1)
                    if i:
                        fin_low(n, i - 1)
                fin_low(n, 3)
                projected(st)

            def dve_mem(st, n):
                dve.wait_ge(s["h_lo"], n["h_lo"])
                dve.wait_ge(s["mem_std"], n["mem_std"] + 1)
                link(nc.vector.reciprocal(tiny[:, 12:14], tiny[:, 10:12]))
                for t in range(ST):
                    i = ts(mem[:, t, :], mem[:, t, :], tiny[:, 12 + t:13 + t], None, ALU.mult)
                i.then_inc(s["mem_n"], 1)

            def dve_xatt(st, n):
                for i in range(st.lin["q"].n):
                    convert(st.lin["q"].b + i + 2)
                    if i == 1:
                        dve.wait_ge(s["mem_turned"], n["mem_turned"] + 1)
                        for c in range(DC):
                            i = ts(hf[:, c, :], ps[:, 4 + c // 2, c % 2 * S:c % 2 * S + S], vcol(column("mem_norm_g_2", c)), None, ALU.mult)
                        i.then_inc(s["mem_f"], 1)
                        dve.wait_ge(s["mem_hi"], n["mem_hi"] + 1)
                        tt(M_lo[:, :, :], hf[:, :, :], M_hi.bitcast(F32), ALU.subtract).then_inc(s["mem_lo"], 1)
                splits(st.lin["k"])
                splits(st.lin["v"])
                attend(n, XH, 256.0 ** -0.5, "xatt")
                projected(st)

            def dve_pre(st, n):
                g = steps[steps.index(st) - 2].lin["out"]
                fold(n, "squared")
                convert(g.b + g.n)
                dve.wait_ge(s["std"], n["std"] + 1)
                dve.wait_ge(s["ax_ready"], n["ax_ready"])
                link(nc.vector.reciprocal(std[:, 1, :], std[:, 0, :]))
                for c in range(DC):
                    i = stt(hf[:, c, :], ax[:, c, :], vcol(column(st.args[0], c)), std[:, 1, :], ALU.mult, ALU.mult)
                    if c % 2:
                        i.then_inc(s["hf"], 1)
                for q in range(4):
                    dve.wait_ge(s["h_hi"], n["h_hi"] + q + 1)
                    r = slice(2 * q, 2 * q + 2)
                    tt(H_lo[:, r, :], hf[:, r, :], H_hi[:, r, :].bitcast(F32), ALU.subtract).then_inc(s["h_lo"], 1)
                convert(g.b + g.n + 1)

            def dve_post(st, n):
                g = steps[steps.index(st) - 1].lin["out"]
                fold(n, "y_sq")
                dve.wait_ge(s["std"], n["std"] + 1)
                link(nc.vector.reciprocal(std[:, 1, :], std[:, 0, :]))
                for q in range(4):
                    r = slice(2 * q, 2 * q + 2)
                    for c in range(2 * q, 2 * q + 2):
                        i = stt(z[:, c, :], ybank(g, c), vcol(column(st.args[0], c)), std[:, 1, :], ALU.mult, ALU.mult)
                    link(i)
                    tt(ax[:, r, :], ax[:, r, :], z[:, r, :], ALU.add).then_inc(s["ax_ready"], 1)

            tri3 = kc("tri")
            for st in steps:
                if st.kind in ("store",):
                    continue
                {"init": dve_init, "ln": dve_ln, "ln_last": dve_ln, "ffn": dve_ffn, "mla": dve_mla, "diff": dve_diff, "ssm": dve_ssm,
                 "pre": dve_pre, "post": dve_post, "hyb": dve_hyb, "mem": dve_mem, "xatt": dve_xatt}[st.kind](st, st.n)

        @block.tensor
        def _(pe):
            def three(out, w, wo, wn, x_hi, x_lo, first, last, swap=False, rest=False):
                a, b = whi[w][:, wo:wo + wn] if isinstance(wn, int) else wn(whi[w]), None
                b = wlo[w][:, wo:wo + wn] if isinstance(wn, int) else wn(wlo[w])
                for i, (l, r) in enumerate(((a, x_hi), (a, x_lo), (b, x_hi))):
                    if swap:
                        l, r = r, l
                    m = pe.matmul(out, l, r, start=first and i == 0, stop=last and i == 2, skip_group_check=rest)
                return m

            def wait_banks(p, it=None):
                if plan.free_need[p] or it is not None:
                    v = plan.free_need[p]
                    pe.wait_ge(banks_free[p % 2], v if it is None else 2 * it + v)

            def wait_split(b, h, it=None):
                v = 2 * b + h + 1
                pe.wait_ge(w_lo, v if it is None else 8 * it + v)

            def columns(g, i, x_hi, x_lo, it=None, tokens=False, wait=None):
                b, p = g.b + i, g.p + i
                wait_banks(p, it)
                for h in range(2):
                    wait_split(b, h, it)
                    order = [(c, k) for c in range(2) for k in range(4 * h, 4 * h + 4)]
                    for c, k in sorted(order, key=lambda x: x[1] // 2) if wait else order:
                        if wait and c == 0 and k % 2 == 0:
                            pe.wait_ge(wait[0], wait[1] + k // 2 + 1)
                        o = ps[:, bank(p) + c, 0:S]
                        if tokens:
                            t = slice(c * P, c * P + P)
                            m = three(o, b % 2, k * 256, 256, x_hi[:, k, t], x_lo[:, k, t], k == 0, k == 7, swap=True)
                        else:
                            m = three(o, b % 2, k * 256 + c * P, P, x_hi[:, k, :], x_lo[:, k, :], k == 0, k == 7)
                    m.then_inc(products, 1)

            def project(st, x_hi, x_lo, ready, count, per):
                g = st.lin["out"]

                def turn(i, it=None):
                    b = g.b + i
                    last = it is None and i == g.n - 1
                    if i == 0:
                        order = [(h, 4 * q + c) for q in range(2) for h in range(2) for c in range(4)]
                        wait_banks(g.p)
                    elif last:
                        order = [(h, c) for c in range(DC) for h in range(2)]
                    else:
                        order = [(h, c) for h in range(2) for c in range(DC)]
                    for h, c in order:
                        k = 2 * i + h
                        if c == 0:
                            if h == 0 or per == 1:
                                v = count + k // per + 1
                                pe.wait_ge(ready, v if it is None else 4 * it + v)
                            wait_split(b, h, it)
                        if i == 0 and h == 0 and c == 4:
                            wait_banks(g.p + 1)
                        if it is None:
                            xh, xl = x_hi[:, k, :], x_lo[:, k, :]
                        else:
                            xh, xl = (x[:, ds(it * 8 + k, 1), :].rearrange("p a n -> p (a n)") for x in (x_hi, x_lo))
                        m = three(ybank(g, c), b % 2, h * HALF + c * P, P, xh, xl, k == 0 and c % 2 == 0, last and h == 1, rest=True)
                        if last and h == 1 or not last and c == DC - 1:
                            m.then_inc(products, 1)

                walk(pe, g, turn, 1, 2)

            def mod_sums(lo, hi, signal=True):
                for c in range(lo, hi):
                    b, o = (6, c) if c < 16 else (7, c - 16)
                    m = pe.matmul(ps[:, b, o:o + 1], mod_acc[:, c // 12, c % 12 * P:c % 12 * P + P], ones[:, 0:1], start=True, stop=True)
                if signal:
                    m.then_inc(s["mod_sum"], 1)

            def pe_init(st, n):
                pe.wait_ge(c_loaded, 32)
                pe.transpose(ps[:, 3, 0:DC], crow[:, :], ident[0:DC, 0:DC]).then_inc(s["c_turned"], 1)
                pe.wait_ge(init_loaded, n_init)
                for i in range(DEPTH):
                    pe.transpose(ps[:, 0, 72 * i:72 * i + 72], rows[0:72, i, :], ident[0:72, 0:72])
                for i in range(2):
                    pe.transpose(ps[:, 1, 96 * i:96 * i + 96], rows[0:96, 4 + i, :], ident[0:96, 0:96])
                pe.transpose(ps[:, 1, 192:192 + NROWS], rows[0:NROWS, 6, :], ident[0:NROWS, 0:NROWS])
                pe.transpose(ps[:, 2, 0:96], rows[0:96, 7, :], ident[0:96, 0:96]).then_inc(s["vec_turned"], 1)
                for c in range(DC):
                    for t in range(ST):
                        m = pe.transpose(ps[:, 4 + c // 2, c % 2 * S + t * P:c % 2 * S + t * P + P], x_in[:, t, c * P:c * P + P], ident)
                m.then_inc(s["vec_turned"], 1)
                pe.wait_ge(mod_used, 16)
                pe.wait_ge(s["z_in"], 1)
                mod_sums(0, 16)
                mod_sums(16, 24)

            def folded(n, signal):
                pe.wait_ge(s["folded"], n["folded"] + 1)
                pe.matmul(ps[:, 5, 0:S], ones, acc[:, 1, :], start=True, stop=True).then_inc(s[signal], 1)

            def pe_ln(st, n):
                more = st.args[0] + 1 < min(plan.mods, SUB * DEPTH)
                if more:
                    pe.wait_ge(mod_used, 16 * (st.args[0] + 2))
                    mod_sums(0, 5, False)
                pe.wait_ge(s["zsum"], n["zsum"] + 7)
                pe.matmul(ps[:, 4, 0:S], ones, acc[:, 0, :], start=True, stop=True).then_inc(s["ln_sum"], 1)
                if more:
                    mod_sums(5, 16)
                folded(n, "ln_var")
                if more:
                    mod_sums(16, 24)

            def pe_ffn(st, n):
                g = st.lin["in"]
                walk(pe, g, lambda i, it: columns(g, i, H_hi, H_lo, it, wait=(s["h_lo"], n["h_lo"] - 4) if i == 0 else None))
                project(st, A_hi, A_lo, s["a_lo"], n["a_lo"], 2)

            def attend(n, heads, kind):
                full = kind == "xatt"

                def parts(h):
                    if kind == "mla":
                        r = slice(64 * (h % 2), 64 * (h % 2) + 64)
                        return [(score_bank(h), [(QN[:, h, :], KN[:, h, :]), (QRp[r, h // 2, :], KRp[r, :])])]
                    if kind == "xatt":
                        return [(score_bank(h), [(QN[:, 2 * h + c, :], KN[:, 2 * h + c, :]) for c in range(2)])]
                    if kind == "diff":
                        return [(score_bank(h, m, 2), [(QN[64 * m:64 * m + 64, h, :], KN[64 * m:64 * m + 64, h, :])]) for m in range(2)]
                    r = slice(64 * (h % 2), 64 * (h % 2) + 64)
                    return [(score_bank(h), [(QN[r, h // 2, :], KN[r, h // 2, :])])]

                def scores(h):
                    if h >= 2:
                        pe.wait_ge(s["exped"] if full else s["maxed"], (n["exped"] if full else n["maxed"]) + h - 1)
                    for b, terms in parts(h):
                        for t in range(ST):
                            keys = S if full or t else P
                            o = S * t if full else P * t
                            for i, (q, k) in enumerate(terms):
                                m = pe.matmul(ps[:, b, o:o + keys], q[:, t * P:t * P + P], k[:, 0:keys],
                                              start=i == 0, stop=i == len(terms) - 1)
                    m.then_inc(s["scores"], 1)

                def turn(h):
                    pe.wait_ge(s["probs"], n["probs"] + h + 1)
                    if h >= 2:
                        pe.wait_ge(s["turned_out"], n["turned_out"] + h - 1)
                    moves = ((0, 0), (128, 256), (256, 128), (384, 384)) if full else ((0, 0), (128, 128), (256, 256))
                    for a, b in moves:
                        m = pe.transpose(ps[:, turned_bank(h), b:b + P], prob[:, h % 4, a:a + P], ident)
                    m.then_inc(s["turned"], 1)

                def mix(h):
                    pe.wait_ge(s["turned_out"], n["turned_out"] + h + 1)
                    if h >= 2:
                        pe.wait_ge(s["mixed_out"], n["mixed_out"] + h - 1)
                    pt = probT[:, h % 2, :]
                    if full:
                        for c in range(2):
                            for t in range(ST):
                                m = pe.matmul(ps[:, mixed_bank(h), c * S:c * S + S], VT[:, t, (2 * h + c) * P:(2 * h + c + 1) * P],
                                              pt[:, t * S:t * S + S], start=t == 0, stop=t == 1)
                    else:
                        w, o = (64, 64 * (h % 2)) if kind == "dilated" else (P, 0)
                        for t in range(ST):
                            m = pe.matmul(ps[o:o + w, mixed_bank(h), t * P:S], VT[:, t, h * w:h * w + w], pt[:, t * S:S + t * P],
                                          start=t == 0, stop=t == 1, skip_group_check=True)
                    m.then_inc(s["mixed"], 1)

                for i in range(heads + 3):
                    if i < heads:
                        scores(i)
                    if 2 <= i < heads + 2:
                        turn(i - 2)
                    if i >= 3:
                        mix(i - 3)
                pe.wait_ge(s["mixed_out"], n["mixed_out"] + heads - 1)

            def pe_mla(st, n):
                g = st.lin["latent"]
                for i in range(3):
                    columns(g, i, H_hi, H_lo, wait=(s["h_lo"], n["h_lo"] - 4) if i == 0 else None)
                pe.wait_ge(s["lat_sq"], n["lat_sq"] + 3)
                for c in range(3):
                    pe.matmul(ps[:, 4, 0:S], ones, sq[:, c, :], start=c == 0, stop=c == 2)
                for c in range(3, 5):
                    m = pe.matmul(ps[:, 4, S:2 * S], ones, sq[:, c, :], start=c == 3, stop=c == 4)
                m.then_inc(s["lat_sum"], 1)
                pe.matmul(ps[:, 5, 0:S], kc("rot_mla"), lat[:, 5, :], start=True, stop=True).then_inc(s["kr_rot"], 1)
                g = st.lin["q"]
                pe.wait_ge(s["lat_lo"], n["lat_lo"] + 1)
                for j in range(g.n):
                    b, p = g.b + j, g.p + j
                    wait_banks(p)
                    wait_split(b, 1)
                    for c in range(3):
                        o = ps[:, bank(p) + c // 2, c % 2 * S:c % 2 * S + S]
                        for k in range(3):
                            m = three(o, b % 2, k * 384 + c * P, P, A_hi[:, k, :], A_lo[:, k, :], k == 0, k == 2)
                    m.then_inc(products, 1)
                g = st.lin["kv"]
                pe.wait_ge(s["lat_lo"], n["lat_lo"] + 2)
                for j in range(g.n):
                    b, p = g.b + j, g.p + 2 * j
                    wait_banks(p)
                    wait_split(b, 1)
                    for c in range(4):
                        o = ps[:, bank(p) + c // 2, c % 2 * S:c % 2 * S + S]
                        for k in range(2):
                            m = three(o, b % 2, k * HALF + c * 256, P, A_hi[:, 3 + k, :], A_lo[:, 3 + k, :], k == 0, k == 1)
                    m.then_inc(products, 1)
                    wait_banks(p + 1)
                    for t in range(ST):
                        for k in range(2):
                            def values(w, k=k):
                                return w[:, k * HALF:(k + 1) * HALF].rearrange("p (h n) -> p h n", h=4)[:, :, P:2 * P]
                            tok = slice(t * P, t * P + P)
                            m = three(ps[:, bank(p + 1) + t, :], b % 2, 0, values, A_hi[:, 3 + k, tok], A_lo[:, 3 + k, tok],
                                      k == 0, k == 1, swap=True)
                    m.then_inc(products, 1)
                for i in range(4):
                    p = st.lin["q"].p + i
                    pe.wait_ge(banks_free[p % 2], plan.free_val[p])
                pe.wait_ge(s["kr_ready"], n["kr_ready"] + 1)
                for i in range(2):
                    pe.matmul(ps[:, 4 + i, :], kc("rot_mla"), QRp[:, 2 * i:2 * i + 2, :], start=True, stop=True)\
                        .then_inc(s["qr_rot"], 1)
                pe.wait_ge(s["qr_ready"], n["qr_ready"] + 2)
                for i in range(4):
                    p = g.p + i
                    pe.wait_ge(banks_free[p % 2], plan.free_val[p])
                attend(n, MLA_H, "mla")
                project(st, H_hi, H_lo, s["mixed_out"], n["mixed_out"], 1)

            def read(g, pairs=1):
                for p in range(g.p, g.p + pairs * g.n)[-2:]:
                    pe.wait_ge(banks_free[p % 2], plan.free_val[p])

            def row(g, x_hi, x_lo, tokens=False, wait=None):
                for i in range(g.n):
                    columns(g, i, x_hi, x_lo, None, tokens, wait if i == 0 else None)

            def fin_sums(n, first=None):
                for i in range(4):
                    pe.wait_ge(s["fin_sq"], n["fin_sq"] + i + 1)
                    pe.matmul(ps[:, 4 + i, :], first if first is not None and i < 2 else ones, sq[:, 2 * i:2 * i + 2, :],
                              start=True, stop=True).then_inc(s["fin_sum"], 1)

            def pe_diff(st, n):
                row(st.lin["qk"], H_hi, H_lo, wait=(s["h_lo"], n["h_lo"] - 4))
                row(st.lin["v"], H_hi, H_lo, tokens=True)
                read(st.lin["v"])
                attend(n, 8, "diff")
                fin_sums(n)
                project(st, H_hi, H_lo, s["fin_lo"], n["fin_lo"], 2)

            def pe_ssm(st, n):
                L = st.lin
                row(L["z"], H_hi, H_lo, wait=(s["h_lo"], n["h_lo"] - 4))
                row(L["xbc"], H_hi, H_lo)
                g = L["dt"]
                wait_banks(g.p)
                wait_split(g.b, 0)
                for t in range(ST):
                    for k in range(DC):
                        tok = slice(t * P, t * P + P)
                        m = three(ps[:, bank(g.p) + t, 0:SSM_H], g.b % 2, k * SSM_H, SSM_H, H_hi[:, k, tok], H_lo[:, k, tok],
                                  k == 0, k == DC - 1, swap=True)
                wait_split(g.b, 1)
                m = pe.matmul(ps[:, 4, 0:1], ones, ones[:, 0:1], start=True, stop=True)
                m.then_inc(products, 1)
                pe.wait_ge(s["conv_out"], n["conv_out"] + 12)
                for q in range(8):
                    if q >= 2:
                        pe.wait_ge(s["x_out"], n["x_out"] + q - 1)
                    for c in range(4):
                        m = pe.transpose(ps[:, 4 + q % 2, c * P:c * P + P], XC[:, q % 4 * 4 + c, q // 4 * P:q // 4 * P + P], ident)
                    m.then_inc(s["x_turned"], 1)
                tri = kc("tri", 0, P)
                pe.wait_ge(s["adt"], n["adt"] + 1)
                pe.wait_ge(s["x_out"], n["x_out"] + 8)
                a0, a1 = dts[:, 6, 0, :], dts[:, 6, 1, :]
                pe.matmul(ps[0:SSM_H, 4, 0:P], a0, tri, start=True, stop=True)
                pe.matmul(ps[0:SSM_H, 4, P:S], a0, ones, start=True, stop=False)
                pe.matmul(ps[0:SSM_H, 4, P:S], a1, tri, start=False, stop=True)
                pe.matmul(ps[:, 5, 0:SSM_H], tri, a0, start=True, stop=True)
                pe.matmul(ps[:, 5, SSM_H:2 * SSM_H], ones, a0, start=True, stop=False)
                pe.matmul(ps[:, 5, SSM_H:2 * SSM_H], tri, a1, start=False, stop=True).then_inc(s["acum"], 1)
                for i in range(SSM_G):
                    if i >= 2:
                        pe.wait_ge(s["cb_out"], n["cb_out"] + i - 1)
                    pe.matmul(ps[:, 6 + i % 2, 0:S], Bm[:, i, 0:P], Cm[:, i, :], start=True, stop=True)
                    pe.matmul(ps[:, 6 + i % 2, S:CW], Bm[:, i, P:S], Cm[:, i, P:S], start=True, stop=True).then_inc(s["cb"], 1)

                def spread(h):
                    if h >= 2:
                        pe.wait_ge(s["dec"], n["dec"] + h - 1)
                    pe.matmul(ps[:, 4 + h % 2, 0:S], ident[0:SSM_H, h:h + 1].to_broadcast([SSM_H, P]), acT[:, :], start=True, stop=True)\
                        .then_inc(s["spread"], 1)

                def mix(h):
                    pe.wait_ge(s["mixing"], n["mixing"] + h + 1)
                    c, o = h // 2, 64 * (h % 2)
                    if c >= 2:
                        pe.wait_ge(s["y_out"], n["y_out"] + c - 1)
                    for t in range(ST):
                        m = pe.matmul(ps[o:o + 64, 6 + c % 2, t * P:S], XT[:, t, h * 64:h * 64 + 64],
                                      mixw[:, h % 2, t * S:t * P + S], start=t == 0, stop=t == 1, skip_group_check=True)
                    m.then_inc(s["ssd"], 1)

                pe.wait_ge(s["acum_t"], n["acum_t"] + 1)
                pe.wait_ge(s["cb_out"], n["cb_out"] + SSM_G)
                for i in range(SSM_H + 2):
                    if i < SSM_H:
                        spread(i)
                    if i >= 2:
                        mix(i - 2)
                for i in range(4):
                    pe.wait_ge(s["fin_sq"], n["fin_sq"] + i + 1)
                    if i >= 2:
                        pe.wait_ge(s["fin_std"], n["fin_std"] + i - 1)
                    for c in range(4):
                        m = pe.matmul(ps[:, 4 + i % 2, 0:S], ones, sqg[:, i % 2, c, :], start=c == 0, stop=c == 3)
                    m.then_inc(s["fin_sum"], 1)
                project(st, A_hi, A_lo, s["fin_lo"], n["fin_lo"], 4)

            def pe_hyb(st, n):
                L = st.lin
                row(L["aqk"], H_hi, H_lo, wait=(s["h_lo"], n["h_lo"] - 4))
                row(L["av"], H_hi, H_lo, tokens=True)
                row(L["rqk"], H_hi, H_lo)
                row(L["rv"], H_hi, H_lo, tokens=True)
                row(L["rg"], H_hi, H_lo)
                read(L["rg"])
                pe.wait_ge(second_loaded, 32)
                for i in range(8):
                    if i >= 2:
                        pe.wait_ge(s["rot_out"], n["rot_out"] + i - 1)
                    X = (QN, KN)[i // 2 % 2]
                    r = slice(4 * (i // 4) + 2 * (i % 2), 4 * (i // 4) + 2 * (i % 2) + 2)
                    pe.matmul(ps[:, 4 + i % 2, :], kc2(("rot_att", "rot_ret")[i // 4]), X[:, r, :], start=True, stop=True)\
                        .then_inc(s["rot"], 1)
                pe.wait_ge(s["rot_out"], n["rot_out"] + 8)
                attend(n, 8, "dilated")
                pe.wait_ge(s["mixed_out"], n["mixed_out"] + 8)
                for i in range(RET_H + 1):
                    if i < RET_H:
                        if i >= 2:
                            pe.wait_ge(s["kq_out"], n["kq_out"] + i - 1)
                        b = ps[:, 4 + i % 2, :]
                        pe.matmul(b[:, 0:S], KN[:, 4 + i, 0:P], QN[:, 4 + i, :], start=True, stop=True)
                        pe.matmul(b[:, S:CW], KN[:, 4 + i, P:S], QN[:, 4 + i, P:S], start=True, stop=True).then_inc(s["kq"], 1)
                    if i:
                        h = i - 1
                        pe.wait_ge(s["kq_out"], n["kq_out"] + h + 1)
                        if h:
                            pe.wait_ge(s["ret_out"], n["ret_out"] + h)
                        for t in range(ST):
                            m = pe.matmul(ps[:, 7, t * P:S], VT[:, t, 512 + h * P:640 + h * P], prob[:, h % 2, t * S:t * P + S],
                                          start=t == 0, stop=t == 1, skip_group_check=True)
                        m.then_inc(s["ret"], 1)
                pe.wait_ge(s["ret_out"], n["ret_out"] + RET_H)
                for i in range(2):
                    pe.matmul(ps[:, 4 + i, :], ones, O1[:, 4 + 2 * i:6 + 2 * i, :], start=True, stop=True).then_inc(s["fin_mean"], 1)
                pe.wait_ge(s["fin_cent"], n["fin_cent"] + 2)
                fin_sums(n, kc("half"))
                project(st, H_hi, H_lo, s["fin_lo"], n["fin_lo"], 2)

            def pe_mem(st, n):
                pass

            def pe_xatt(st, n):
                L = st.lin
                for i in range(L["q"].n):
                    columns(L["q"], i, H_hi, H_lo, wait=(s["h_lo"], n["h_lo"] - 4) if i == 0 else None)
                    if i == 1:
                        pe.wait_ge(s["mem_n"], n["mem_n"])
                        for c in range(DC):
                            for t in range(ST):
                                m = pe.transpose(ps[:, 4 + c // 2, c % 2 * S + t * P:c % 2 * S + t * P + P], mem[:, t, c * P:c * P + P], ident)
                        m.then_inc(s["mem_turned"], 1)
                pe.wait_ge(s["mem_lo"], n["mem_lo"] + 1)
                row(L["k"], M_hi, M_lo)
                row(L["v"], M_hi, M_lo, tokens=True)
                read(L["v"])
                attend(n, XH, "xatt")
                project(st, H_hi, H_lo, s["mixed_out"], n["mixed_out"], 2)

            def pe_pre(st, n):
                folded(n, "x_sum")

            def pe_post(st, n):
                folded(n, "y_sum")

            def pe_store(st, n):
                pe.wait_ge(s["ax_ready"], n["ax_ready"])
                for t in range(ST):
                    for c in range(DC):
                        m = pe.transpose(ps[:, 4 + 2 * t + c // 4, c % 4 * P:c % 4 * P + P], ax[:, c, t * P:t * P + P], ident)
                m.then_inc(s["out_turned"], 1)

            for st in steps:
                {"init": pe_init, "ln": pe_ln, "ln_last": pe_ln, "ffn": pe_ffn, "mla": pe_mla, "diff": pe_diff, "ssm": pe_ssm,
                 "pre": pe_pre, "post": pe_post, "hyb": pe_hyb, "mem": pe_mem, "xatt": pe_xatt, "store": pe_store}[st.kind](st, st.n)


_INS = ["x", "c", "positions", "w_mod", "b_mod", "ln_g", "ln_b", "ffn_w_in", "ffn_w_out", "mla_w_in", "mla_q_norm_g",
        "mla_kv_norm_g", "mla_w_q_up", "mla_w_kv_up", "mla_w_out", "diff_w_in", "diff_lambda_q", "diff_lambda_k",
        "diff_subln_g", "diff_w_out", "ssm_w_in", "ssm_conv_w", "ssm_conv_b", "ssm_dt_bias", "ssm_a_log",
        "ssm_d_skip", "ssm_norm_g", "ssm_w_out", "mem_2", "pre_mix_g_2", "post_mix_g_2", "w_in_2", "attn_gn_g_2",
        "ret_gn_g_2", "w_out_2", "pre_mem_g_2", "post_mem_g_2", "mem_norm_g_2", "w_q_mem_2", "w_kv_mem_2",
        "w_o_mem_2", "pre_ffn_g_2", "post_ffn_g_2", "w_gate_up_2", "w_down_2"]


def schedule(A):
    def ffn(s):
        return ("ffn", s, A["ffn_w_in"][s // SUB, s % SUB // 2], A["ffn_w_out"][s // SUB, s % SUB // 2])

    todo = [("init",)]
    for i in range(DEPTH):
        s = SUB * i
        m = i // 3
        todo += [ffn(s), ("ln", s)]
        if i % 3 == 0:
            todo.append(("mla", s + 1, {"in": A["mla_w_in"][m], "q": A["mla_w_q_up"][m], "kv": A["mla_w_kv_up"][m], "out": A["mla_w_out"][m]}))
        else:
            k = ("", "diff", "ssm")[i % 3]
            todo.append((k, s + 1, {"in": A[k + "_w_in"][m], "out": A[k + "_w_out"][m]}))
        todo.append(("ln", s + 1))
        todo += [ffn(s + 2), ("ln" if i < DEPTH - 1 else "ln_last", s + 2)]
    todo += [("pre", "pre_mix_g_2"), ("hyb", {"in": A["w_in_2"][0], "out": A["w_out_2"][0]}), ("post", "post_mix_g_2"),
             ("pre", "pre_mem_g_2"), ("mem",), ("xatt", {"q": A["w_q_mem_2"][0], "kv": A["w_kv_mem_2"][0], "out": A["w_o_mem_2"][0]}),
             ("post", "post_mem_g_2"), ("pre", "pre_ffn_g_2"), ("ffn", SUB * DEPTH, A["w_gate_up_2"][0], A["w_down_2"][0]),
             ("post", "post_ffn_g_2")]
    return todo + [("store",)]


def kernel(**inputs):
    import concourse.bacc as _bacc
    from concourse.bass_utils import run_bass_kernel_spmd as _run

    nc = _bacc.Bacc("TRN2", target_bir_lowering=False, num_devices=1)
    arrays, A = {}, {}
    for name in _INS:
        a = np.ascontiguousarray(inputs[name])
        arrays[f"in_{name}_dram"] = a
        A[name] = nc.dram_tensor(f"in_{name}_dram", a.shape, mybir.dt.from_np(a.dtype), kind="ExternalInput").ap()
    out = nc.dram_tensor("out_0_dram", (1, S, D), F32, kind="ExternalOutput").ap()
    (first, at1), (second, at2) = constants()
    plan = Plan(schedule(A))
    program(nc, plan, A, out, (nc.inline_tensor(first, name="constants_first").ap(), at1, first.shape[1]),
            (nc.inline_tensor(second, name="constants_second").ap(), at2, second.shape[1]))
    r = _run(nc, [arrays], core_ids=[0])
    return r.results[0]["out_0_dram"]
```
